# Optimizing a Trainium2 kernel written in Bass

```python
import math
import jax, jax.numpy as jnp
from jax import lax
import numpy as np

D_MODEL = 1024
BATCH = 1
SEQ = 512
DEPTH = 2
DEC_BATCH = 8
DEC_SEQ = 1
PAST_LEN = 4096
PAGE_SIZE = 128

N_MIXERS = 2
N_RET_LAYERS = (DEPTH + N_MIXERS - 1) // N_MIXERS
N_GDN_LAYERS = DEPTH // N_MIXERS

RET_HEADS = 4
RET_DK = D_MODEL // RET_HEADS
RET_DV = 2 * RET_DK
RET_IN = 2 * RET_HEADS * RET_DK + 2 * RET_HEADS * RET_DV
RET_CHUNK = 64
ROPE_BASE = 10000.0

GDN_HEADS = 8
GDN_DK = 128
GDN_DV = 128
GDN_QKV = GDN_HEADS * (2 * GDN_DK + GDN_DV)
GDN_IN = GDN_QKV + GDN_HEADS * GDN_DV + 2 * GDN_HEADS
CONV_W = 4
GDN_CHUNK = 64

D_FF = 2816
EPS = 1e-6

kernel_name = 'retention_gdn_macaron_decode_step'

def _rmsnorm(x, g):
    xf = x.astype(jnp.float32)
    y = xf * lax.rsqrt(jnp.mean(xf * xf, axis=-1, keepdims=True) + EPS)
    return (y * g.astype(jnp.float32)).astype(x.dtype)

def _swiglu(x, w_gu, w_down):
    a, b = jnp.split(x @ w_gu, 2, axis=-1)
    return (jax.nn.silu(a) * b) @ w_down

def _l2norm(x):
    return x * lax.rsqrt(jnp.sum(x * x, axis=-1, keepdims=True) + EPS)

def _rotate(x, pos):
    theta = 1.0 / (ROPE_BASE ** jnp.linspace(0.0, 1.0, x.shape[-1] // 2, dtype=jnp.float32))
    ang = pos[:, None] * theta[None, :]
    cos = jnp.cos(ang)[None, :, None, :]
    sin = jnp.sin(ang)[None, :, None, :]
    x1 = x[..., 0::2]
    x2 = x[..., 1::2]
    return jnp.stack([x1 * cos - x2 * sin, x2 * cos + x1 * sin], axis=-1).reshape(x.shape)

def _to_chunks(x, c):
    B, T = x.shape[:2]
    n = -(-T // c)
    x = jnp.pad(x, [(0, 0), (0, n * c - T)] + [(0, 0)] * (x.ndim - 2))
    x = x.reshape((B, n, c) + x.shape[2:])
    return jnp.swapaxes(x, 2, 3)

def _from_chunks(o, T):
    B, n, H, c, e = o.shape
    return jnp.swapaxes(o, 2, 3).reshape(B, n * c, H, e)[:, :T]

def _retention(h, pos0, S0, w_in, w_out):
    f32 = jnp.float32
    B, T, _ = h.shape
    qd = RET_HEADS * RET_DK
    vd = RET_HEADS * RET_DV
    q, k, v, gate = jnp.split(h @ w_in, [qd, 2 * qd, 2 * qd + vd], axis=-1)
    pos = jnp.arange(T, dtype=f32) + pos0
    q = _rotate(q.reshape(B, T, RET_HEADS, RET_DK).astype(f32), pos)
    k = _rotate(k.reshape(B, T, RET_HEADS, RET_DK).astype(f32), pos) * (RET_DK ** -0.5)
    v = v.reshape(B, T, RET_HEADS, RET_DV).astype(f32)
    log_gamma = jnp.log(1.0 - 2.0 ** (-5.0 - jnp.arange(RET_HEADS, dtype=f32)))
    a = jnp.broadcast_to(log_gamma, (B, T, RET_HEADS))
    c = min(RET_CHUNK, T)
    qc, kc, vc, ac = _to_chunks(q, c), _to_chunks(k, c), _to_chunks(v, c), _to_chunks(a, c)
    b = jnp.cumsum(ac, axis=-1)
    causal = jnp.tril(jnp.ones((c, c), dtype=bool))
    decay = jnp.exp(jnp.where(causal, b[..., :, None] - b[..., None, :], -jnp.inf))
    P = jnp.einsum('bnhid,bnhjd->bnhij', qc, kc) * decay
    intra = jnp.einsum('bnhij,bnhje->bnhie', P, vc)
    b_last = b[..., -1:]
    q_dec = qc * jnp.exp(b)[..., None]
    k_dec = kc * jnp.exp(b_last - b)[..., None]
    c_dec = jnp.exp(b_last[..., 0])

    def step(S, xs):
        qd_, kd_, v_, cd_ = xs
        inter = jnp.einsum('bhcd,bhde->bhce', qd_, S)
        S = cd_[..., None, None] * S + jnp.einsum('bhcd,bhce->bhde', kd_, v_)
        return S, inter

    xs = (jnp.moveaxis(q_dec, 1, 0), jnp.moveaxis(k_dec, 1, 0), jnp.moveaxis(vc, 1, 0), jnp.moveaxis(c_dec, 1, 0))
    S, inter = lax.scan(step, S0.astype(f32), xs)
    o = _from_chunks(intra + jnp.moveaxis(inter, 0, 1), T)
    o = o * lax.rsqrt(jnp.mean(o * o, axis=-1, keepdims=True) + EPS)
    o = o.reshape(B, T, vd) * jax.nn.silu(gate.astype(f32))
    return o.astype(h.dtype) @ w_out, S

def _gated_delta(h, conv_buf, S0, w_in, conv_w, a_log, dt_bias, norm_w, w_out):
    f32 = jnp.float32
    B, T, _ = h.shape
    H, DK, DV = GDN_HEADS, GDN_DK, GDN_DV
    qkv, z, beta_raw, a_raw = jnp.split(h @ w_in, [GDN_QKV, GDN_QKV + H * DV, GDN_QKV + H * DV + H], axis=-1)
    xp = jnp.concatenate([conv_buf.astype(qkv.dtype), qkv], axis=1)
    new_buf = xp[:, T:]
    conv = xp[:, 0:T].astype(f32) * conv_w[0].astype(f32)
    for j in range(1, CONV_W):
        conv = conv + xp[:, j:j + T].astype(f32) * conv_w[j].astype(f32)
    qkv = jax.nn.silu(conv)
    q, k, v = jnp.split(qkv, [H * DK, 2 * H * DK], axis=-1)
    q = _l2norm(q.reshape(B, T, H, DK)) * (DK ** -0.5)
    k = _l2norm(k.reshape(B, T, H, DK))
    v = v.reshape(B, T, H, DV)
    beta = jax.nn.sigmoid(beta_raw.astype(f32))
    a = -jnp.exp(a_log.astype(f32)) * jax.nn.softplus(a_raw.astype(f32) + dt_bias.astype(f32))
    c = min(GDN_CHUNK, T)
    qc, kc, vc = _to_chunks(q, c), _to_chunks(k, c), _to_chunks(v, c)
    bc, ac = _to_chunks(beta, c), _to_chunks(a, c)
    b = jnp.cumsum(ac, axis=-1)
    diff = b[..., :, None] - b[..., None, :]
    strict = jnp.tril(jnp.ones((c, c), dtype=bool), -1)
    causal = jnp.tril(jnp.ones((c, c), dtype=bool))
    L = jnp.einsum('bnhid,bnhjd->bnhij', kc, kc) * jnp.exp(jnp.where(strict, diff, -jnp.inf)) * bc[..., :, None]
    rhs = jnp.concatenate([vc * bc[..., None], kc * (bc * jnp.exp(b))[..., None]], axis=-1)
    sol = lax.linalg.triangular_solve(L + jnp.eye(c, dtype=f32), rhs, left_side=True, lower=True, unit_diagonal=True)
    U, Wk = sol[..., :DV], sol[..., DV:]
    P = jnp.einsum('bnhid,bnhjd->bnhij', qc, kc) * jnp.exp(jnp.where(causal, diff, -jnp.inf))
    b_last = b[..., -1:]
    q_dec = qc * jnp.exp(b)[..., None]
    k_dec = kc * jnp.exp(b_last - b)[..., None]
    c_dec = jnp.exp(b_last[..., 0])

    def step(S, xs):
        qd_, kd_, u_, wk_, p_, cd_ = xs
        W = u_ - jnp.einsum('bhcd,bhde->bhce', wk_, S)
        o = jnp.einsum('bhcd,bhde->bhce', qd_, S) + jnp.einsum('bhij,bhje->bhie', p_, W)
        S = cd_[..., None, None] * S + jnp.einsum('bhcd,bhce->bhde', kd_, W)
        return S, o

    xs = tuple(jnp.moveaxis(t, 1, 0) for t in (q_dec, k_dec, U, Wk, P, c_dec))
    S, o = lax.scan(step, S0.astype(f32), xs)
    o = _from_chunks(jnp.moveaxis(o, 0, 1), T)
    o = o * lax.rsqrt(jnp.mean(o * o, axis=-1, keepdims=True) + EPS) * norm_w.astype(f32)
    o = o * jax.nn.silu(z.astype(f32).reshape(B, T, H, DV))
    return o.reshape(B, T, H * DV).astype(h.dtype) @ w_out, S, new_buf

def _trunk(x, pos0, s_ret, s_gdn, s_conv, norm_g, ffn_gu, ffn_down, ret_w_in, ret_w_out,
           gdn_w_in, gdn_conv_w, gdn_a_log, gdn_dt_bias, gdn_norm_w, gdn_w_out, final_g):
    new_ret, new_gdn, new_conv = [], [], []
    for i in range(DEPTH):
        x = x + 0.5 * _swiglu(_rmsnorm(x, norm_g[i, 0]), ffn_gu[i, 0], ffn_down[i, 0])
        hn = _rmsnorm(x, norm_g[i, 1])
        j = i // N_MIXERS
        if i % N_MIXERS == 0:
            m, s = _retention(hn, pos0, s_ret[j], ret_w_in[j], ret_w_out[j])
            new_ret.append(s.astype(s_ret.dtype))
        else:
            m, s, buf = _gated_delta(hn, s_conv[j], s_gdn[j], gdn_w_in[j], gdn_conv_w[j], gdn_a_log[j],
                                     gdn_dt_bias[j], gdn_norm_w[j], gdn_w_out[j])
            new_gdn.append(s.astype(s_gdn.dtype))
            new_conv.append(buf.astype(s_conv.dtype))
        x = x + m
        x = x + 0.5 * _swiglu(_rmsnorm(x, norm_g[i, 2]), ffn_gu[i, 1], ffn_down[i, 1])
    return _rmsnorm(x, final_g), jnp.stack(new_ret), jnp.stack(new_gdn), jnp.stack(new_conv)

def setup_inputs(seed: int = 0) -> dict:
    key = jax.random.key(seed)
    ks = jax.random.split(key, 17)
    f32 = jnp.float32

    def nrm(k, shape, scale):
        return jax.random.normal(k, shape, f32) * scale

    x_prompt = nrm(ks[0], (BATCH, SEQ, D_MODEL), 1.0)
    x_sample = nrm(ks[1], (DEC_BATCH, DEC_SEQ, D_MODEL), 1.0)
    state_ret = nrm(ks[2], (N_RET_LAYERS, DEC_BATCH, RET_HEADS, RET_DK, RET_DV), 1.0)
    state_gdn = nrm(ks[3], (N_GDN_LAYERS, DEC_BATCH, GDN_HEADS, GDN_DK, GDN_DV), 0.5)
    state_gdn_conv = nrm(ks[4], (N_GDN_LAYERS, DEC_BATCH, CONV_W - 1, GDN_QKV), 1.0)
    norm_g = 1.0 + nrm(ks[5], (DEPTH, 3, D_MODEL), 0.05)
    ffn_gu = nrm(ks[6], (DEPTH, 2, D_MODEL, 2 * D_FF), D_MODEL ** -0.5)
    ffn_down = nrm(ks[7], (DEPTH, 2, D_FF, D_MODEL), D_FF ** -0.5)
    ret_w_in = nrm(ks[8], (N_RET_LAYERS, D_MODEL, RET_IN), D_MODEL ** -0.5)
    ret_w_out = nrm(ks[9], (N_RET_LAYERS, RET_HEADS * RET_DV, D_MODEL), (RET_HEADS * RET_DV) ** -0.5)
    gdn_w_in = nrm(ks[10], (N_GDN_LAYERS, D_MODEL, GDN_IN), D_MODEL ** -0.5)
    gdn_conv_w = nrm(ks[11], (N_GDN_LAYERS, CONV_W, GDN_QKV), CONV_W ** -0.5)
    gdn_a_log = jnp.log(jax.random.uniform(ks[12], (N_GDN_LAYERS, GDN_HEADS), f32, 1.0, 16.0))
    dt = jnp.exp(jax.random.uniform(ks[13], (N_GDN_LAYERS, GDN_HEADS), f32, math.log(1e-3), math.log(1e-1)))
    gdn_dt_bias = dt + jnp.log(-jnp.expm1(-dt))
    gdn_norm_w = 1.0 + nrm(ks[14], (N_GDN_LAYERS, GDN_DV), 0.05)
    gdn_w_out = nrm(ks[15], (N_GDN_LAYERS, GDN_HEADS * GDN_DV, D_MODEL), (GDN_HEADS * GDN_DV) ** -0.5)
    final_g = 1.0 + nrm(ks[16], (D_MODEL,), 0.05)
    return {'x_prompt': x_prompt, 'x_sample': x_sample, 'state_ret': state_ret, 'state_gdn': state_gdn,
            'state_gdn_conv': state_gdn_conv, 'norm_g': norm_g, 'ffn_gu': ffn_gu, 'ffn_down': ffn_down,
            'ret_w_in': ret_w_in, 'ret_w_out': ret_w_out, 'gdn_w_in': gdn_w_in, 'gdn_conv_w': gdn_conv_w,
            'gdn_a_log': gdn_a_log, 'gdn_dt_bias': gdn_dt_bias, 'gdn_norm_w': gdn_norm_w,
            'gdn_w_out': gdn_w_out, 'final_g': final_g}

def reference(x_prompt, x_sample, state_ret, state_gdn, state_gdn_conv, norm_g, ffn_gu, ffn_down,
              ret_w_in, ret_w_out, gdn_w_in, gdn_conv_w, gdn_a_log, gdn_dt_bias, gdn_norm_w,
              gdn_w_out, final_g):
    bp = x_prompt.shape[0]
    zero_ret = jnp.zeros((N_RET_LAYERS, bp, RET_HEADS, RET_DK, RET_DV), state_ret.dtype)
    zero_gdn = jnp.zeros((N_GDN_LAYERS, bp, GDN_HEADS, GDN_DK, GDN_DV), state_gdn.dtype)
    zero_conv = jnp.zeros((N_GDN_LAYERS, bp, CONV_W - 1, GDN_QKV), state_gdn_conv.dtype)
    y_prompt, ret_p, gdn_p, conv_p = _trunk(
        x_prompt, 0.0, zero_ret, zero_gdn, zero_conv, norm_g, ffn_gu, ffn_down, ret_w_in, ret_w_out,
        gdn_w_in, gdn_conv_w, gdn_a_log, gdn_dt_bias, gdn_norm_w, gdn_w_out, final_g)
    y_sample, ret_s, gdn_s, conv_s = _trunk(
        x_sample, float(PAST_LEN), state_ret, state_gdn, state_gdn_conv, norm_g, ffn_gu, ffn_down,
        ret_w_in, ret_w_out, gdn_w_in, gdn_conv_w, gdn_a_log, gdn_dt_bias, gdn_norm_w, gdn_w_out, final_g)
    return (y_prompt, y_sample, ret_p, gdn_p, conv_p, ret_s, gdn_s, conv_s)


_drawn_inputs = setup_inputs


def setup_inputs(seed=0):
    import zlib

    import numpy as np

    out = dict(_drawn_inputs(seed))
    spreads = {}
    factors = {'gdn_norm_w': 2.707}
    for name, (base, spread) in spreads.items():
        noise = np.random.default_rng([zlib.crc32(name.encode()), seed]).standard_normal(out[name].shape)
        drawn = base * np.exp(spread * noise) if base else spread * noise
        out[name] = __import__('jax').numpy.asarray(drawn.astype(out[name].dtype))
    for name, factor in factors.items():
        out[name] = (out[name] * factor).astype(out[name].dtype)
    return out
```

```python
from contextlib import ExitStack

import concourse.bass as bass
from concourse import mybir

F32 = mybir.dt.float32
F32R = mybir.dt.float32r
ALU = mybir.AluOpType
ACT = mybir.ActivationFunctionType

P = 128
D, SEQ, DEC = 1024, 512, 8
KT = D // P
NTOK = SEQ + DEC
HALF = NTOK // 2
FF = 2816
FT = FF // P
EPS = 1e-6
SLOT = 16 * P


RH, RK, RV = 4, 256, 512
RET_SCALE = RK ** -0.5
RING = 4


class Steps:

    def __init__(self, names):
        self.names, self.seen = names.split(), 0

    def __call__(self, name, turn):
        return turn * len(self.names) + self.names.index(name) + 1

    def did(self, name):
        assert self.names[self.seen % len(self.names)] == name, (name, self.names[self.seen % len(self.names)])
        self.seen += 1
        return 1


RET_T = Steps("p0 p1 p23 k01 v0 v1 v2 k23 v3 vs o0 o1 o2 o3 s0 s1 n "
              "b0 b1 q0 q1 b2 b3 q2 q3 b4 b5 q4 q5 b6 b7 q6 q7 ns")
RET_V = Steps("q k pt0 pt1 pt23 k01 k23 ro u0 u1 on0 y0 lo0 u2 u3 on1 y1 lo1 u4 u5 on2 y2 lo2 u6 u7 on3 y3 lo3 "
              "os ossq rs osn ys yh yl")
RET_A = Steps("v0 v1 v2 v3 vs o0 sq0 o1 sq1 o2 sq2 o3 sq3 s0 s1 root "
              "g0 g1 silu0 hi0 g2 g3 silu1 hi1 g4 g5 silu2 hi2 g6 g7 silu3 hi3 rs")
RET_P = Steps("sum0 sum1 sum2 sum3")
RET_UNITS, RET_SLOTS = 20, 8
RET_SLOT_DONE = [0, 2, 4, 6, 8, 10, 12, 16, 20]


GH, GG, GC, LV = 8, 4, 4, 6
GDN_SLOTS, GDN_UNITS = 10, 24
GDN_SLOT_DONE = [0, 2, 4, 6, 8, 10, 12, 14, 16, 20, 24]
CONV, TAPS = 3 * D, 4
U_LEN = TAPS - 1 + SEQ + TAPS * DEC
C_LEN = U_LEN - (TAPS - 1)
TAIL = U_LEN - SEQ


def pairs(before, early, level, late, turn):
    out = []
    for p in range(2):
        both = (2 * p, 2 * p + 1)
        for group in before:
            out += [f"{n}.{c}" for c in both for n in group.split()]
        for l in range(1, LV + 1):
            for group in level:
                out += [f"{n}{l}.{c}" for c in both for n in group.split() if not (l == LV and n == "b")]
        for group in late:
            out += [f"{n}.{c}" for c in both for n in group.split()]
    return " ".join(out)


def each(n, *names):
    return " ".join(f"{m}{i}" for i in range(n) for m in names)


PRE_T = Steps("cw ba rc bcol blast smp")
PRE_V = Steps("wl cw rc ba y m d di z w p0 p1 p2 p3 p4 p5 p6 l r sp a bcol cdl kd beb sma smb eab")
PRE_A = Steps("wh e na beta ebc cd kd ea")
GDN_T = Steps(" ".join([
    "ct", each(12, "cs"), each(8, "ln"),
    pairs(["br kt vt kk", "qk mt"], None, ["t", "a b"], ["u wk", "w o s"], None),
    "r0", " ".join(f"wr{b}" for b in range(4)), " ".join(f"os{b}" for b in range(4)),
    "r1", " ".join(f"wr{b}" for b in range(4, 8)), " ".join(f"os{b}" for b in range(4, 8)),
    each(4, "nn")]))
GDN_V = Steps(" ".join([
    "uz s0", each(12, "ux", "ca", "cb", "cc", "cd"), each(8, "ri", "dq"),
    pairs(["aut", "dd", "kb kd vb", "L", "m0 pt qd"], None, ["a b"], ["W S"], None),
    "wa0 wb0 wc0", each(4, "dg"), each(4, "kw", "sn"),
    "wa1 wb1 wc1", " ".join(f"dg{b}" for b in range(4, 8)), " ".join(f"kw{b} sn{b}" for b in range(4, 8)),
    "oz", each(4, "rn", "y", "yz"), each(4, "lo")]))
GDN_A = Steps(" ".join([
    each(4, "si"), "si4 cse0 si5 si6 si7 si8 cse1 si9 si10 si11 cse2", each(8, "sq", "rt"),
    pairs(["eb", "d2 d1", "mt"], None, ["t"], ["u wk", "oc"], None),
    "sz", each(4, "nsq", "nrt"), each(4, "hi")]))
GDN_P = Steps(" ".join([
    pairs(["n2 n1", "d1b", "l0"], None, ["l"], ["s2"], None),
    each(8, "se")]))


class Phase:

    def __init__(self, kind, slots, units, cols, norm, index):
        self.per_slot, self.per_unit = max(slots, units) // slots, max(slots, units) // units
        self.kind, self.slots, self.units, self.cols, self.norm, self.index = kind, slots, units, cols, norm, index


    def slot_done(self, k):
        return self.part0 + self.per_slot * (k - self.slot0 + 1)

    def unit_done(self, u):
        return self.part0 + self.per_unit * (u - self.unit0 + 1)


def plan():
    phases = [
        Phase("gate_up", FT, 2 * FT, 16 * P, 0, 0),
        Phase("down", 2 * KT, KT, 11 * P, 1, 0),
        Phase("ret", RET_SLOTS * RH, RET_UNITS * RH, 16 * P, 2, 0),
        Phase("gate_up", FT, 2 * FT, 16 * P, 2, 1),
        Phase("down", 2 * KT, KT, 11 * P, 3, 1),
        Phase("gate_up", FT, 2 * FT, 16 * P, 3, 2),
        Phase("down", 2 * KT, KT, 11 * P, 4, 2),
        Phase("gdn", GDN_SLOTS * 2, GDN_UNITS * 2, 16 * P, 5, 0),
        Phase("gate_up", FT, 2 * FT, 16 * P, 5, 3),
        Phase("down", 2 * KT, KT, 11 * P, 6, 3),
    ]
    slot, unit, part = 0, KT, KT
    for n, ph in enumerate(phases):
        ph.slot0, ph.unit0, ph.part0 = slot, unit, part
        slot, unit = slot + ph.slots, unit + ph.units
        part += max(ph.slots, ph.units)
        ph.next_cols = phases[n + 1].cols if n + 1 < len(phases) else 0
    return phases


def rolled(eng, n, body, peel_first=False):
    start = 0
    if peel_first:
        body(0, n == 1)
        start = 1
    if n - 1 > start:
        with eng.Fori(start, n - 1) as i:
            body(i, False)
    if n - 1 >= start:
        body(n - 1, True)


def build(nc, a, outs):
    with ExitStack() as ctx:
        def sb(name, shape, dt=F32, stack=ctx):
            return stack.enter_context(nc.sbuf_tensor(name, shape, dt))

        def sem(name):
            return ctx.enter_context(nc.semaphore(name))

        x = sb("x", [P, KT, NTOK])
        xh = sb("xh", [P, KT, NTOK], F32R)
        xl = sb("xl", [P, KT, NTOK], F32R)
        raw = sb("raw", [P, 2, SLOT])
        wh = sb("wh", [P, 2, SLOT], F32R)
        wl = sb("wl", [P, 2, SLOT], F32R)
        ident = sb("ident", [P, P])
        ones = sb("ones", [P, P])
        gains = sb("gains", [P, 56])
        gain_rows = sb("gain_rows", [56, P])
        eps = sb("eps", [P, 1])
        ssq = sb("ssq", [P, NTOK])
        sq = sb("sq", [P, 2, NTOK])
        rinv = sb("rinv", [P, NTOK])
        ps = ctx.enter_context(nc.psum_tensor("ps", [P, 8, 512], F32))

        def pair(u):
            return ps[:, 2 * (u % 2):2 * (u % 2) + 2, 0:HALF]

        def halves(ap):
            return ap.rearrange("p (h t) -> p h t", h=2)

        w_landed = [sem("w_landed0"), sem("w_landed1")]
        w_high = sem("w_high")
        w_low = sem("w_low")
        parts_done = sem("parts_done")
        acc_free = sem("acc_free")
        x_high = sem("x_high")
        x_sq = sem("x_sq")
        x_low = sem("x_low")
        x_ssq = sem("x_ssq")
        ssq_sum = sem("ssq_sum")
        ssq_root = sem("ssq_root")
        ssq_inv = sem("ssq_inv")
        consts = sem("consts")
        ones_set = sem("ones_set")
        x_landed = sem("x_landed")
        gains_turned = sem("gains_turned")
        gains_ready = sem("gains_ready")
        gate_ready = sem("gate_ready")
        h_ready = sem("h_ready")
        h_high = sem("h_high")
        h_low = sem("h_low")
        stored = sem("stored")
        act_held, pool_held = sem("act_held"), sem("pool_held")
        ret_consts = sem("ret_consts")
        ret_tables = sem("ret_tables")
        ret_t, ret_v, ret_a, ret_p = sem("ret_t"), sem("ret_v"), sem("ret_a"), sem("ret_p")
        head_landed = sem("head_landed")
        s_landed = [sem(f"s_landed{n}") for n in range(RING)]
        s_stored = [sem(f"s_stored{n}") for n in range(RING)]
        s_out_stored = sem("s_out_stored")
        pre_landed = sem("pre_landed")
        pre_t, pre_v, pre_a = sem("pre_t"), sem("pre_v"), sem("pre_a")
        gdn_t, gdn_v, gdn_a, gdn_p = sem("gdn_t"), sem("gdn_v"), sem("gdn_a"), sem("gdn_p")
        c_landed = sem("c_landed")
        c_stored = sem("c_stored")
        g_landed = [sem(f"g_landed{n}") for n in range(RING)]
        g_stored = [sem(f"g_stored{n}") for n in range(RING)]
        gs_stored = sem("gs_stored")
        eps_set = sem("eps_set")
        softplus_ready = sem("softplus_ready")
        y_ready, y_turned, y_out = sem("y_ready"), sem("y_turned"), sem("y_out")
        y_stored = [sem("y_stored0"), sem("y_stored1")]

        phases = plan()

        def heads(ap):
            return ap.rearrange("p (h o) -> p h o", o=1).broadcast_to([P, ap.shape[1], P])

        def every(ap):
            return ap.rearrange("p (o n) -> p o n", o=1).broadcast_to([P, GG, P])

        def by_head(bank, n=P):
            return ps[:, bank, 0:GG * n].rearrange("p (h n) -> p h n", h=GG)

        with ExitStack() as st:
            xin = sb("xin", [P, 4, D], stack=st)
            xin_s = sb("xin_s", [DEC, D], stack=st)
        with ExitStack() as st:
            rq = sb("rq", [P, 2, NTOK], stack=st)
            rk = sb("rk", [P, 2, NTOK], stack=st)
            rv = sb("rv", [P, 4, NTOK], stack=st)
            rg = sb("rg", [P, 4, NTOK], stack=st)
            ro = sb("ro", [P, 4, SEQ], stack=st)
            vtok = sb("vtok", [P, 4, RV], stack=st)
            vtok_s = sb("vtok_s", [DEC, RV], stack=st)
            head_c = sb("head_c", [P, SEQ + 5], stack=st)
            cosr = sb("cosr", [P, NTOK], stack=st)
            sinr = sb("sinr", [P, NTOK], stack=st)
            rot = sb("rot", [P, 2, NTOK], stack=st)
            osq = rot[:, :, 0:SEQ]
            osum = sb("osum", [P, SEQ], stack=st)
            rinv_o = sb("rinv_o", [P, SEQ], stack=st)
            s_out = sb("s_out", [P, 2, RV], stack=st)
            s_ring = sb("s_ring", [P, RING, 2, RV], stack=st)
            sel = sb("sel", [DEC, DEC, P], stack=st)
            o_s = sb("o_s", [P, 4, DEC], stack=st)
            osq_s = sb("osq_s", [P, 4, DEC], stack=st)
            rinv_s = sb("rinv_s", [P, DEC], stack=st)
            yh = sb("yh", [P, 4, NTOK], F32R, stack=st)
            with ExitStack() as scores:
                ktok = sb("ktok", [P, 4, RK], stack=scores)
                pt = sb("pt", [P, 1280], stack=scores)
            yl = sb("yl", [P, 4, NTOK], F32R, stack=st)
        with ExitStack() as st:
            gq = sb("gq", [P, GG, NTOK], stack=st)
            gk = sb("gk", [P, GG, NTOK], stack=st)
            gv = sb("gv", [P, GG, NTOK], stack=st)
            gz = sb("gz", [P, GG, NTOK], stack=st)
            gs = sb("gs", [P, GG, P], stack=st)
            gs2 = sb("gs2", [P, GG, P], stack=st)
            g_ring = sb("g_ring", [P, RING, GG, P], stack=st)
            gcon = sb("gcon", [P, 3 * P + 7 * P + DEC], stack=st)
            a_log = sb("a_log", [P, GH], stack=st)
            dt_b = sb("dt_b", [P, GH], stack=st)
            norm_w = sb("norm_w", [P, 1], stack=st)
            conv_w = sb("conv_w", [P, TAPS, 3 * GH], stack=st)
            eps_q = sb("eps_q", [P, 1], stack=st)
            small = sb("small", [P, 7, 5, GH], stack=st)
            ba = sb("ba", [P, 5, 2 * GH], stack=st)
            r_col = sb("r_col", [P, 5], stack=st)
            bcol = sb("bcol", [P, 4, GH], stack=st)
            ebcol = sb("ebcol", [P, 4, GH], stack=st)
            kdcol = sb("kdcol", [P, 4, GH], stack=st)
            cdrep = sb("cdrep", [P, 4, GH], stack=st)
            bebcol = sb("bebcol", [P, 4, GH], stack=st)
            sm = sb("sm", [P, 2, GH, DEC], stack=st)
            eab = sb("eab", [P, 2, GH, DEC], stack=st)
            with ExitStack() as sc:
                wba = sb("wba", [P, KT, 16], stack=sc)
                wbah = sb("wbah", [P, KT, 16], F32R, stack=sc)
                wbal = sb("wbal", [P, KT, 16], F32R, stack=sc)
                conv_rows = sb("conv_rows", [TAPS * 3 * GH, P], stack=sc)
            with ExitStack() as sc:
                gpad = sb("gpad", [P, 1024], stack=sc)
                uu = sb("uu", [P, 2, U_LEN], stack=sc)
                cv = sb("cv", [P, 2, C_LEN], stack=sc)
                c_in = sb("c_in", [DEC * 3, 3, GG * P], stack=sc)
                c_out = sb("c_out", [TAIL, 3, GG * P], stack=sc)
            with ExitStack() as sc:
                names = "d1 d2 eb kb kd vb m mt t1 la lb u".split()
                chain = [{n: sb(f"{n}_{x_}", [P, GG, P], stack=sc) for n in names} for x_ in range(2)]
                for ch in chain:
                    ch["dd"], ch["wk"] = ch["u"], ch["lb"]
            with ExitStack() as sc:
                gyh = sb("gyh", [P, GG, NTOK], F32R, stack=sc)
                gyl = sb("gyl", [P, GG, NTOK], F32R, stack=sc)
                gsq = sb("gsq", [P, 2, NTOK], stack=sc)
                grt = sb("grt", [P, 2, NTOK], stack=sc)
                wt = sb("wt", [P, GG, DEC], stack=sc)
                dg = sb("dg", [P, 4, GG, P], stack=sc)
        ut, negup, biglo = (gcon[:, n * P:(n + 1) * P] for n in range(3))
        levels = [gcon[:, (3 + n) * P:(4 + n) * P] for n in range(7)]
        smask = gcon[:, 10 * P:10 * P + DEC]
        with ExitStack() as st:
            yy = sb("yy", [P, KT, NTOK], stack=st)
            y_tok = sb("y_tok", [P, 2, D], stack=st)
        with ExitStack() as st:
            gate = sb("gate", [P, NTOK], stack=st)
            up = sb("up", [P, NTOK], stack=st)
            hh = sb("hh", [P, FT, NTOK], F32R, stack=st)
            hl = sb("hl", [P, FT, NTOK], F32R, stack=st)

        block = ctx.enter_context(nc.Block())

        @block.sync
        def _(sp):
            sp.dma_start(ident[:], a["c_ident"]).then_inc(consts, 16)
            sp.dma_start(gain_rows[0:48, :], a["norm_g"].rearrange("l n (t p) -> (l n t) p", p=P)).then_inc(consts, 16)
            sp.dma_start(gain_rows[48:56, :], a["final_g"].rearrange("(t p) -> t p", p=P)).then_inc(consts, 16)
            sp.dma_start(xin[:], a["x_prompt"].rearrange("b (c p) d -> p (b c) d", p=P)).then_inc(x_landed, 16)
            sp.dma_start(xin_s[:], a["x_sample"].rearrange("b s d -> (b s) d")).then_inc(x_landed, 16)

            def tiles(s, t0, n, cols=P):
                return raw[:, s, t0 * P:t0 * P + n * cols].rearrange("p (t c) -> p t c", c=cols)

            def ret_body(ph, h):
                wi = a["ret_w_in"][0].rearrange("(t p) n -> p t n", p=P)
                wo = a["ret_w_out"][0].rearrange("(h t p) n -> h p t n", p=P, t=4)
                starts = [h * RK, RH * RK + h * RK, 2 * RH * RK + h * RV, 2 * RH * RK + h * RV + 2 * P,
                          2 * RH * RK + RH * RV + h * RV, 2 * RH * RK + RH * RV + h * RV + 2 * P]
                for j in range(RET_SLOTS):
                    s, k = j % 2, ph.slot0 + RET_SLOTS * h + j
                    sp.wait_ge(w_low, k - 1)
                    if j < 6:
                        for t in (0, 4):
                            sp.dma_start(tiles(s, 2 * t, 4, 2 * P), wi[:, t:t + 4, bass.ds(starts[j], 2 * P)]).then_inc(w_landed[s], 16)
                    else:
                        for t in (0, 2):
                            src = wo[bass.ds(h, 1), :, t:t + 2, (j - 6) * 4 * P:(j - 5) * 4 * P]
                            sp.dma_start(tiles(s, 4 * t, 2, 4 * P), src.rearrange("h p t n -> p (h t) n")).then_inc(w_landed[s], 16)

            def gdn_body(ph, g):
                wi = a["gdn_w_in"][0].rearrange("(t p) n -> p t n", p=P)
                wo = a["gdn_w_out"][0].rearrange("(g t p) n -> g p t n", p=P, t=GG)
                for j in range(GDN_SLOTS):
                    s, k = j % 2, ph.slot0 + GDN_SLOTS * g + j
                    sp.wait_ge(w_low, k - 1)
                    if j < 8:
                        c = (j // 2) * D + g * GG * P + (j % 2) * 2 * P
                        for t in (0, 4):
                            sp.dma_start(tiles(s, 2 * t, 4, 2 * P), wi[:, t:t + 4, c:c + 2 * P]).then_inc(w_landed[s], 16)
                    else:
                        for t in (0, 2):
                            sp.dma_start(tiles(s, 4 * t, 2, 4 * P), wo[g, :, t:t + 2, (j - 8) * 4 * P:(j - 7) * 4 * P])\
                                .then_inc(w_landed[s], 16)

            for ph in phases:
                if ph.kind == "gdn":
                    for g in range(2):
                        gdn_body(ph, g)
                    continue
                if ph.kind == "ret":
                    with sp.Fori(0, RH) as h:
                        ret_body(ph, h)
                    continue

                def body(i, last):
                    for s in range(2):
                        k = ph.slot0 + 2 * i + s
                        if not isinstance(k, int) or k >= 2:
                            sp.wait_ge(w_low, k - 1)
                        if ph.kind == "gate_up":
                            w = a["ffn_gu"][ph.index // 2, ph.index % 2].rearrange("(t p) n -> p t n", p=P)
                            c = (2 * i + s) * P
                            sp.dma_start(tiles(s, 0, KT), w[:, :, bass.ds(c, P)]).then_inc(w_landed[s], 16)
                            sp.dma_start(tiles(s, KT, KT), w[:, :, bass.ds(c + FF, P)]).then_inc(w_landed[s], 16)
                        if ph.kind == "down":
                            w = a["ffn_down"][ph.index // 2, ph.index % 2].rearrange("(s t p) n -> p s t n", s=2, p=P)
                            sp.dma_start(tiles(s, 0, 6), w[:, s, 0:6, bass.ds(i * P, P)]).then_inc(w_landed[s], 16)
                            sp.dma_start(tiles(s, 6, 5), w[:, s, 6:11, bass.ds(i * P, P)]).then_inc(w_landed[s], 16)
                rolled(sp, ph.slots // 2, body, ph.slot0 == 0)

            for c in range(5):
                rows = P if c < 4 else DEC
                sp.wait_ge(y_out, c + 1)
                dst = outs[0][0, c * P:(c + 1) * P, :] if c < 4 else outs[1].rearrange("b s d -> (b s) d")
                sp.dma_start(dst, y_tok[0:rows, c % 2, :]).then_inc(y_stored[c % 2], 16)
            sp.wait_ge(y_stored[0], 48)
            sp.wait_ge(y_stored[1], 32)

        @block.gpsimd
        def _(pool):
            nc.gpsimd.memset(ones[:], 1.0).then_inc(ones_set, 1)
            nc.gpsimd.memset(eps[:], EPS).then_inc(ones_set, 1)

            def sum_squares(m):
                if m:
                    pool.wait_ge(ssq_sum, m)
                for t in range(KT):
                    pool.wait_ge(x_sq, KT * m + t + 1)
                    if t == 0:
                        nc.gpsimd.tensor_copy(ssq[:], sq[:, t % 2, :]).then_inc(x_ssq, 1)
                    else:
                        pool.wait_ge(x_ssq, KT * m + t)
                        nc.gpsimd.tensor_tensor(ssq[:], ssq[:], sq[:, t % 2, :], ALU.add).then_inc(x_ssq, 1)

            ret_in = a["state_ret"][0].rearrange("b h (p t) e -> b h p t e", t=2)
            ret_new = outs[5][0].rearrange("b h (p t) e -> b h p t e", t=2)
            ret_last = outs[2][0, 0].rearrange("h (p t) e -> h p t e", t=2)

            def ret_body(ph, h):
                def state(dram, b):
                    return dram[b, bass.ds(h, 1)].rearrange("h p t e -> p (h t) e")

                first = isinstance(h, int) and h == 0
                if not first:
                    pool.wait_ge(ret_v, RET_V("k23", h - 1))
                    pool.wait_ge(ret_a, RET_A("g7", h - 1))
                pool.sem_inc(pool_held, 1)
                pool.dma_start(head_c[:], a["c_head"][bass.ds(h, 1)].rearrange("h p n -> (h p) n")).then_inc(head_landed, 16)
                for b in range(RING):
                    if not first:
                        pool.wait_ge(s_stored[b], 32 * h)
                        pool.wait_ge(ret_t, RET_T(f"q{b + RING}", h - 1))
                    pool.sem_inc(pool_held, 1)
                    pool.dma_start(s_ring[:, b], state(ret_in, b)).then_inc(s_landed[b], 16)
                for e in range(4):
                    pool.wait_ge(ret_a, RET_A(f"sq{e}", h))
                    if e == 0:
                        if not first:
                            pool.wait_ge(ret_t, RET_T("n", h - 1))
                        pool.sem_inc(pool_held, 1)
                        nc.gpsimd.tensor_copy(osum[:], osq[:, 0, :]).then_inc(ret_p, RET_P.did("sum0"))
                    else:
                        pool.wait_ge(ret_p, RET_P(f"sum{e - 1}", h))
                        nc.gpsimd.tensor_tensor(osum[:], osum[:], osq[:, e % 2, :], ALU.add).then_inc(ret_p, RET_P.did(f"sum{e}"))
                pool.wait_ge(ret_a, RET_A("s1", h))
                pool.sem_inc(pool_held, 1)
                pool.dma_start(ret_last[bass.ds(h, 1)].rearrange("h p t e -> p (h t) e"), s_out[:]).then_inc(s_out_stored, 16)
                for b in range(DEC):
                    pool.wait_ge(ret_v, RET_V(f"u{b}", h))
                    pool.sem_inc(pool_held, 1)
                    pool.dma_start(state(ret_new, b), s_ring[:, b % RING]).then_inc(s_stored[b % RING], 16)
                    c = b - 1
                    if c >= 0 and c + RING < DEC:
                        pool.wait_ge(s_stored[c], 32 * h + 16)
                        pool.wait_ge(ret_t, RET_T(f"q{c}", h))
                        pool.sem_inc(pool_held, 1)
                        pool.dma_start(s_ring[:, c], state(ret_in, c + RING)).then_inc(s_landed[c], 16)

            def gdn_consts():
                pool.wait_ge(parts_done, gdn.part0)
                def row(src, n):
                    return src.rearrange("(o n) -> o n", o=1).broadcast_to([P, n])
                for dst, src in ((gcon[:], a["c_gdn"]), (wba[:], a["gdn_w_in"][0].rearrange("(t p) n -> p t n", p=P)[:, :, 4 * D:4 * D + 16]),
                                 (conv_rows[:], a["gdn_conv_w"][0].rearrange("j (t p) -> (j t) p", p=P)),
                                 (a_log[:], row(a["gdn_a_log"][0], GH)), (dt_b[:], row(a["gdn_dt_bias"][0], GH)),
                                 (norm_w[:], a["gdn_norm_w"].rearrange("o (p n) -> (o p) n", n=1))):
                    pool.dma_start(dst, src).then_inc(pre_landed, 16)
                nc.gpsimd.memset(eps_q[:], EPS * P).then_inc(eps_set, 1)

            def gdn_body(ph, g):
                T, V, A, Q = GDN_T, GDN_V, GDN_A, GDN_P
                h0 = g * GG

                def state(dram, b):
                    return dram[0, b, h0:h0 + GG].rearrange("h p e -> p h e")

                if g == 0:
                    pool.wait_ge(pre_v, PRE_V("wl", 0))
                    pool.wait_ge(pre_t, PRE_T("ba", 0))
                else:
                    pool.wait_ge(parts_done, ph.part0 + GDN_UNITS * g)
                c_src = a["state_gdn_conv"][0].rearrange("b j (y n) -> (b j) y n", y=3)[:, :, h0 * P:(h0 + GG) * P]
                pool.dma_start(c_in[:], c_src).then_inc(c_landed, 16)
                for b in range(RING):
                    if g:
                        pool.wait_ge(g_stored[b], 32 * g)
                    pool.dma_start(g_ring[:, b], state(a["state_gdn"], b)).then_inc(g_landed[b], 16)
                pool.wait_ge(gdn_a, A("cse2", g))
                cols = lambda o: o.rearrange("j (y n) -> j y n", y=3)[:, :, h0 * P:(h0 + GG) * P]
                pool.dma_start(cols(outs[4][0, 0]), c_out[0:3]).then_inc(c_stored, 16)
                for b in range(DEC):
                    pool.dma_start(cols(outs[7][0, b]), c_out[4 + 4 * b:7 + 4 * b]).then_inc(c_stored, 16)
                add = lambda o, i0, i1, op: nc.gpsimd.tensor_tensor(o, i0, i1, op)
                for p in range(2):
                    both = [(2 * p + x_, chain[x_]) for x_ in range(2)]
                    for c, ch in both:
                        pool.wait_ge(gdn_v, V(f"dd.{c}", g))
                        if p == 0:
                            pool.wait_ge(c_stored, 144 * (g + 1))
                        add(ch["d2"][:], ch["dd"][:], every(negup), ALU.add).then_inc(gdn_p, Q.did(f"n2.{c}"))
                        add(ch["d1"][:], ch["dd"][:], every(biglo), ALU.add).then_inc(gdn_p, Q.did(f"n1.{c}"))
                    for c, ch in both:
                        pool.wait_ge(gdn_a, A(f"d1.{c}", g))
                        add(ch["d1"][:], ch["d1"][:], heads(small[:, 6, c, h0:h0 + GG]), ALU.mult).then_inc(gdn_p, Q.did(f"d1b.{c}"))
                    for c, ch in both:
                        pool.wait_ge(gdn_v, V(f"L.{c}", g))
                        add(ch["la"][:], ch["d1"][:], every(levels[0]), ALU.mult).then_inc(gdn_p, Q.did(f"l0.{c}"))
                    for l in range(1, LV + 1):
                        for c, ch in both:
                            if l == 2:
                                pool.wait_ge(gdn_v, V(f"m0.{c}", g))
                            if l > 2:
                                pool.wait_ge(gdn_t, T(f"t{l - 2}.{c}", g))
                            add(ch["lb" if l % 2 else "la"][:], ch["d1"][:], every(levels[l]), ALU.mult).then_inc(gdn_p, Q.did(f"l{l}.{c}"))
                    for c, ch in both:
                        pool.wait_ge(gdn_v, V("s0" if c == 0 else f"S.{c - 1}", g))
                        add(gs2[:], gs[:], heads(cdrep[:, c, h0:h0 + GG]), ALU.mult).then_inc(gdn_p, Q.did(f"s2.{c}"))
                pool.wait_ge(gdn_v, V("S.3", g))
                pool.dma_start(outs[3][0, 0, h0:h0 + GG].rearrange("h p e -> p h e"), gs[:]).then_inc(gs_stored, 16)
                for b in range(DEC):
                    r_, hf = b % RING, b // RING
                    pool.wait_ge(g_landed[r_], 32 * g + 16 * hf + 16)
                    pool.wait_ge(gdn_t, T(f"r{hf}", g))
                    add(g_ring[:, r_], g_ring[:, r_], heads(eab[:, 0, h0:h0 + GG, b]), ALU.mult).then_inc(gdn_p, Q.did(f"se{b}"))
                    if b % RING == RING - 1:
                        for q in range(b - RING + 1, b + 1):
                            pool.wait_ge(gdn_v, V(f"sn{q}", g))
                            pool.dma_start(state(outs[6], q), g_ring[:, q % RING]).then_inc(g_stored[q % RING], 16)
                        for q in range(b - RING + 1, b + 1):
                            if hf == 0:
                                pool.wait_ge(g_stored[q], 32 * g + 16)
                                pool.wait_ge(gdn_t, T(f"os{q}", g))
                                pool.dma_start(g_ring[:, q], state(a["state_gdn"], q + RING)).then_inc(g_landed[q], 16)

            gdn = [ph for ph in phases if ph.kind == "gdn"][0]
            sum_squares(0)
            for ph in phases:
                if ph.kind == "gdn":
                    gdn_consts()
                    for g in range(2):
                        gdn_body(ph, g)
                    sum_squares(ph.norm)
                    for b in range(RING):
                        pool.wait_ge(g_stored[b], 64)
                    pool.wait_ge(gs_stored, 32)
                if ph.kind == "down":
                    sum_squares(ph.norm)
                if ph.kind == "ret":
                    pool.dma_start(sel[:], a["c_sel"]).then_inc(ret_consts, 16)
                    pool.dma_start(cosr[:], a["c_cos"]).then_inc(ret_consts, 16)
                    pool.dma_start(sinr[:], a["c_sin"]).then_inc(ret_consts, 16)
                    ret_body(ph, 0)
                    with pool.Fori(1, RH) as h:
                        ret_body(ph, h)
                    sum_squares(ph.norm)
                    for b in range(RING):
                        pool.wait_ge(s_stored[b], 32 * RH)
                    pool.wait_ge(s_out_stored, 16 * RH)

        @block.tensor
        def _(pe):
            pe.wait_ge(consts, 48)
            nc.tensor.transpose(ps[:, 7, 0:56], gain_rows[:, :], ident[0:56, 0:56]).then_inc(gains_turned, 1)
            pe.wait_ge(x_landed, 32)
            for t in range(KT):
                if t >= 2:
                    pe.wait_ge(acc_free, t - 1)
                b = 2 * (t % 2)
                for c in range(4):
                    nc.tensor.transpose(ps[:, b, c * P:(c + 1) * P], xin[:, c, t * P:(t + 1) * P], ident[:])
                nc.tensor.transpose(ps[:, b + 1, 0:DEC], xin_s[:, t * P:(t + 1) * P],
                                    ident[0:DEC, 0:DEC]).then_inc(parts_done, 1)

            def products(q, s, n_tiles, col0, step, high, low, kt0, first, last_):
                for t in range(n_tiles):
                    c = col0 + t * step
                    hi_w, lo_w = wh[:, s, c:c + P], wl[:, s, c:c + P]
                    begin, end = first and t == 0, last_ and t == n_tiles - 1
                    for w_, v, b_, e_ in ((hi_w, high, begin, False), (hi_w, low, False, False), (lo_w, high, False, end)):
                        for h in range(2):
                            m_ = nc.tensor.matmul(ps[:, 2 * q + h, 0:HALF], w_, v[:, kt0 + t, h * HALF:(h + 1) * HALF],
                                                  start=b_, stop=e_)
                return m_

            def norm_sum(m):
                pe.wait_ge(x_ssq, KT * (m + 1))
                if m == 0:
                    pe.wait_ge(ones_set, 2)
                    pe.wait_ge(gains_ready, 1)
                for h in range(2):
                    m_ = nc.tensor.matmul(ps[:, 6 + h, 0:HALF], ones[:], ssq[:, h * HALF:(h + 1) * HALF],
                                          start=True, stop=True)
                m_.then_inc(ssq_sum, 1)

            def ret_body(ph, h):
                def slot(j):
                    pe.wait_ge(w_low, ph.slot0 + RET_SLOTS * h + j + 1)

                first = isinstance(h, int) and h == 0
                for j in range(4):
                    slot(j)
                    for g in range(2):
                        pe.wait_ge(acc_free, ph.unit0 + RET_UNITS * h + 2 * j + g - 1)
                        m_ = in_products(g, j % 2, j < 2, g)
                        m_.then_inc(parts_done, 1)
                        if first and j == 0 and g == 0:
                            norm_sum(ph.norm - 1)
                pe.wait_ge(ret_v, RET_V("k", h))
                if first:
                    pe.wait_ge(ssq_root, ph.norm)
                    pe.wait_ge(ret_consts, 48)
                off = [0, 512, 896, 1152]
                for jb in range(4):
                    w = SEQ - P * jb
                    o = ps[:, 4 + min(jb, 2), 0:w] if jb < 3 else ps[:, 6, 256:384]
                    for t in range(2):
                        m_ = nc.tensor.matmul(o, rk[:, t, jb * P:(jb + 1) * P], rq[:, t, jb * P:SEQ], start=t == 0, stop=t == 1)
                    if jb != 2:
                        m_.then_inc(ret_t, RET_T.did(["p0", "p1", "", "p23"][jb]))

                def turn_k(c, name):
                    for n in range(2):
                        for t in range(2):
                            m_ = nc.tensor.transpose(ps[:, 7, (2 * n + t) * P:(2 * n + t + 1) * P],
                                                     rk[:, t, (c + n) * P:(c + n + 1) * P], ident[:])
                    m_.then_inc(ret_t, RET_T.did(name))

                def turn_v(c):
                    for e in range(4):
                        m_ = nc.tensor.transpose(ps[:, 4 + c, e * P:(e + 1) * P], rv[:, e, c * P:(c + 1) * P], ident[:])
                    m_.then_inc(ret_t, RET_T.did(f"v{c}"))

                turn_k(0, "k01")
                for c in range(3):
                    pe.wait_ge(ret_v, RET_V(["pt0", "pt1", "pt23"][c], h))
                    if c == 0:
                        pe.wait_ge(acc_free, ph.unit0 + RET_UNITS * h + 8)
                    turn_v(c)
                pe.wait_ge(ret_v, RET_V("k01", h))
                turn_k(2, "k23")
                pe.wait_ge(ret_v, RET_V("k23", h))
                turn_v(3)
                pe.wait_ge(ret_a, RET_A("v3", h))
                for e in range(4):
                    m_ = nc.tensor.transpose(ps[0:DEC, 7, e * P:(e + 1) * P], rv[:, e, SEQ:NTOK], ident[:])
                m_.then_inc(ret_t, RET_T.did("vs"))
                pe.wait_ge(ret_a, RET_A("vs", h))
                for e in range(4):
                    for jb in range(4):
                        m_ = nc.tensor.matmul(ps[:, 4 + e, jb * P:SEQ], vtok[:, jb, e * P:(e + 1) * P],
                                              pt[:, off[jb]:off[jb] + SEQ - P * jb], start=jb == 0, stop=jb == 3)
                    m_.then_inc(ret_t, RET_T.did(f"o{e}"))
                for t in range(2):
                    pe.wait_ge(ret_a, RET_A(f"sq{t}", h))
                    for jb in range(4):
                        m_ = nc.tensor.matmul(ps[:, 4 + t, :], ktok[:, jb, t * P:(t + 1) * P], vtok[:, jb, :],
                                              start=jb == 0, stop=jb == 3)
                    m_.then_inc(ret_t, RET_T.did(f"s{t}"))
                pe.wait_ge(ret_p, RET_P("sum3", h))
                pe.wait_ge(ret_a, RET_A("sq2", h))
                nc.tensor.matmul(ps[:, 6, :], ones[:], osum[:], start=True, stop=True).then_inc(ret_t, RET_T.did("n"))
                for g in range(4):
                    for b in (2 * g, 2 * g + 1):
                        if b < 2:
                            pe.wait_ge(ret_a, RET_A(f"s{b}", h))
                        else:
                            pe.wait_ge(ret_v, RET_V(f"u{b - 2}", h))
                        nc.tensor.matmul(ps[:, 4 + b % 2, :], sel[:, b, :], vtok_s[:], start=True, stop=True)\
                            .then_inc(ret_t, RET_T.did(f"b{b}"))
                    if g % 2 == 0:
                        slot(4 + g // 2)
                    pe.wait_ge(acc_free, ph.unit0 + RET_UNITS * h + 8 + g - 1)
                    in_products(g % 2, (4 + g // 2) % 2, False, g % 2).then_inc(parts_done, 1)
                    for b in (2 * g, 2 * g + 1):
                        if b == 0:
                            pe.wait_ge(ret_a, RET_A("sq3", h))
                        pe.wait_ge(ret_v, RET_V(f"u{b}", h))
                        for e in range(4):
                            for t in range(2):
                                m_ = nc.tensor.matmul(ps[:, 7, e * DEC + b:e * DEC + b + 1],
                                                      s_ring[:, b % RING, t, e * P:(e + 1) * P],
                                                      rq[:, t, SEQ + b:SEQ + b + 1], start=t == 0, stop=t == 1)
                        m_.then_inc(ret_t, RET_T.did(f"q{b}"))
                pe.wait_ge(ret_v, RET_V("ossq", h))
                pe.wait_ge(ret_a, RET_A("root", h))
                for e in range(4):
                    m_ = nc.tensor.matmul(ps[:, 6, 0:DEC], ones[:], osq_s[:, e, :], start=e == 0, stop=e == 3)
                m_.then_inc(ret_t, RET_T.did("ns"))
                pe.wait_ge(ret_v, RET_V("yl", h))
                for n in range(KT):
                    if n % 4 == 0:
                        slot(6 + n // 4)
                    pe.wait_ge(acc_free, ph.unit0 + RET_UNITS * h + 12 + n - 1)
                    m_ = products(n % 2, n // 4, 4, (n % 4) * P, 4 * P, yh, yl, 0, True, True)
                    m_.then_inc(parts_done, 1)

            def in_products(q, s, paired, g):
                for t in range(KT):
                    c = 2 * P * t
                    cols = slice(c + g, c + 2 * P, 2) if paired else slice(c + g * P, c + (g + 1) * P)
                    hi_w, lo_w = wh[:, s, cols], wl[:, s, cols]
                    for n, (w_, v) in enumerate(((hi_w, xh), (hi_w, xl), (lo_w, xh))):
                        for h in range(2):
                            m_ = nc.tensor.matmul(ps[:, 2 * q + h, 0:HALF], w_, v[:, t, h * HALF:(h + 1) * HALF],
                                                  start=t == 0 and n == 0, stop=t == KT - 1 and n == 2)
                return m_

            def gdn_pre(ph):
                pe.wait_ge(pre_landed, 96)
                nc.tensor.transpose(ps[:, 4, 0:96], conv_rows[:, :], ident[0:96, 0:96]).then_inc(pre_t, PRE_T.did("cw"))
                pe.wait_ge(pre_v, PRE_V("wl", 0))
                pe.wait_ge(pre_v, PRE_V("cw", 0))
                starts = [0, P, 2 * P, 3 * P, NTOK - P]
                for n, c in enumerate(starts):
                    for t in range(KT):
                        for q, (v, w_) in enumerate(((xh, wbah), (xl, wbah), (xh, wbal))):
                            m_ = nc.tensor.matmul(ps[:, 5, n * 16:(n + 1) * 16], v[:, t, c:c + P], w_[:, t, :],
                                                  start=t == 0 and q == 0, stop=t == KT - 1 and q == 2)
                m_.then_inc(pre_t, PRE_T.did("ba"))
                norm_sum(ph.norm - 1)
                pe.wait_ge(ssq_inv, ph.norm)
                for n, c in enumerate(starts):
                    m_ = nc.tensor.matmul(ps[:, 4, 128 + n:129 + n], rinv[:, c:c + P], ident[:, 0:1], start=True, stop=True)
                m_.then_inc(pre_t, PRE_T.did("rc"))
                pe.wait_ge(pre_v, PRE_V("a", 0))
                a_tok = small[:, 5, 0:4, :].rearrange("p c h -> p (c h)")
                nc.tensor.matmul(ps[:, 5, 128:160], ut, a_tok, start=True, stop=True).then_inc(pre_t, PRE_T.did("bcol"))
                nc.tensor.matmul(ps[:, 5, 160:192], ones[:], a_tok, start=True, stop=True).then_inc(pre_t, PRE_T.did("blast"))
                pe.wait_ge(pre_v, PRE_V("smb", 0))
                nc.tensor.matmul(ps[:, 4, 256:384], ones[:], sm[:].rearrange("p a h b -> p (a h b)"), start=True, stop=True)\
                    .then_inc(pre_t, PRE_T.did("smp"))
                pe.wait_ge(pre_v, PRE_V("eab", 0))

            def gdn_body(ph, g):
                T, V, A, Q = GDN_T, GDN_V, GDN_A, GDN_P
                h0 = g * GG

                def v(name):
                    pe.wait_ge(gdn_v, V(name, g))

                def act_(name):
                    pe.wait_ge(gdn_a, A(name, g))

                def did(m_, name):
                    m_.then_inc(gdn_t, T.did(name))

                def turn(n):
                    v(f"ux{n}")
                    if n in (4, 8):
                        act_(f"cse{n // 4 - 1}")
                    did(nc.tensor.transpose(ps[0:TAIL, 7, (n % 4) * P:(n % 4 + 1) * P], uu[:, n % 2, SEQ:U_LEN], ident[:]), f"cs{n}")

                def lengths(n):
                    act_(f"sq{n}")
                    if n >= 2:
                        act_(f"rt{n - 2}")
                    if n == 0:
                        act_("cse2")
                    for h in range(2):
                        m_ = nc.tensor.matmul(ps[:, 4 + 2 * (n % 2) + h, 0:HALF], ones[:], sq[:, n % 2, h * HALF:(h + 1) * HALF],
                                              start=True, stop=True)
                    did(m_, f"ln{n}")

                pe.wait_ge(c_landed, 16 * (g + 1))
                if g:
                    pe.wait_ge(gdn_a, A("nrt3", g - 1))
                for n in range(12):
                    m_ = nc.tensor.transpose(ps[:, 6, n * 24:(n + 1) * 24], c_in[:, n // 4, (n % 4) * P:(n % 4 + 1) * P], ident[0:24, 0:24])
                did(m_, "ct")
                for n in range(16):
                    if n % 2 == 0:
                        pe.wait_ge(w_low, ph.slot0 + GDN_SLOTS * g + n // 2 + 1)
                    pe.wait_ge(acc_free, ph.unit0 + GDN_UNITS * g + n - 1)
                    in_products(n % 2, (n // 2) % 2, False, n % 2).then_inc(parts_done, 1)
                    if 1 <= n <= 12:
                        turn(n - 1)
                    if n >= 12:
                        lengths(2 * (n - 12))
                        lengths(2 * (n - 12) + 1)
                v("dq7")
                act_("si11")
                pe.wait_ge(acc_free, ph.unit0 + GDN_UNITS * g + 16)
                for p in range(2):
                    both = [(2 * p + x_, 4 * x_, chain[x_]) for x_ in range(2)]
                    if p:
                        v("S.1")
                        act_("oc.1")
                    for c, bb, ch in both:
                        at_ = slice(c * P, (c + 1) * P)
                        v(f"aut.{c}")
                        did(nc.tensor.matmul(ps[:, bb, :], ones[:], ch["t1"][:].rearrange("p h n -> p (h n)"), start=True, stop=True), f"br.{c}")
                        for n, src, name in ((1, gk, "kt"), (2, gv, "vt")):
                            for h in range(GG):
                                m_ = nc.tensor.transpose(ps[:, bb + n, h * P:(h + 1) * P], src[:, h, at_], ident[:])
                            did(m_, f"{name}.{c}")
                        for h in range(GG):
                            m_ = nc.tensor.matmul(ps[:, bb + 3, h * P:(h + 1) * P], gk[:, h, at_], gk[:, h, at_], start=True, stop=True)
                        did(m_, f"kk.{c}")
                    for c, bb, ch in both:
                        at_ = slice(c * P, (c + 1) * P)
                        v(f"kd.{c}")
                        for h in range(GG):
                            m_ = nc.tensor.matmul(ps[:, bb + 1, h * P:(h + 1) * P], gk[:, h, at_], gq[:, h, at_], start=True, stop=True)
                        did(m_, f"qk.{c}")
                        v(f"vb.{c}")
                        v(f"m0.{c}")
                        for h in range(GG):
                            m_ = nc.tensor.transpose(ps[:, bb + 2, h * P:(h + 1) * P], ch["m"][:, h, :], ident[:])
                        did(m_, f"mt.{c}")

                    def four(bank, left, right, name):
                        for h in range(GG):
                            m_ = nc.tensor.matmul(ps[:, bank, h * P:(h + 1) * P], left[:, h, :], right[:, h, :], start=True, stop=True)
                        did(m_, name)

                    for l in range(1, LV + 1):
                        for c, bb, ch in both:
                            pe.wait_ge(gdn_p, Q(f"l{l}.{c}", g))
                            if l == 1:
                                act_(f"mt.{c}")
                            else:
                                v(f"a{l - 1}.{c}")
                                act_(f"t{l - 1}.{c}")
                            four(bb + 3, ch["lb" if l % 2 else "la"], ch["mt"], f"t{l}.{c}")
                        for c, bb, ch in both:
                            act_(f"t{l}.{c}")
                            if l == 1:
                                v(f"dd.{c}")
                                act_(f"eb.{c}")
                            else:
                                v(f"b{l - 1}.{c}")
                            four(bb, ch["m"], ch["t1"], f"a{l}.{c}")
                            if l < LV:
                                four(bb + 2, ch["t1"], ch["m"], f"b{l}.{c}")
                    for c, bb, ch in both:
                        v(f"a{LV}.{c}")
                        v(f"pt.{c}")
                        four(bb + 1, ch["mt"], ch["vb"], f"u.{c}")
                        act_(f"t{LV}.{c}")
                        four(bb + 3, ch["kb"], ch["mt"], f"wk.{c}")
                    for c, bb, ch in both:
                        act_(f"wk.{c}")
                        v("s0" if c == 0 else f"S.{c - 1}")
                        four(bb, ch["wk"], gs, f"w.{c}")
                        act_(f"u.{c}")
                        v(f"W.{c}")
                        v(f"qd.{c}")
                        for h in range(GG):
                            o = ps[:, bb + 1, h * P:(h + 1) * P]
                            nc.tensor.matmul(o, gs[:, h, :], ch["eb"][:, h, :], start=True, stop=False)
                            m_ = nc.tensor.matmul(o, ch["u"][:, h, :], ch["d2"][:, h, :], start=False, stop=True)
                        did(m_, f"o.{c}")
                        four(bb + 2, ch["kd"], ch["u"], f"s.{c}")
                for hf in range(2):
                    mine = range(4 * hf, 4 * hf + 4)
                    if hf == 0:
                        v("S.3")
                        act_("oc.3")
                    for b in mine:
                        pe.wait_ge(g_landed[b % RING], 32 * g + 16 * hf + 16)
                        for h in range(GG):
                            m_ = nc.tensor.matmul(ps[:, 0, h * 4 + b % 4:h * 4 + b % 4 + 1], g_ring[:, b % RING, h, :],
                                                  gk[:, h, SEQ + b:SEQ + b + 1], start=True, stop=True)
                    did(m_, f"r{hf}")
                    for b in mine:
                        v(f"dg{b}")
                        if hf:
                            v(f"kw{b - 4}")
                        did(nc.tensor.matmul(ps[:, 4 + b % 4, :], ones[:], dg[:, b % 4].rearrange("p h n -> p (h n)"), start=True, stop=True), f"wr{b}")
                    for b in mine:
                        v(f"sn{b}")
                        for h in range(GG):
                            m_ = nc.tensor.matmul(ps[:, 1, h * DEC + b:h * DEC + b + 1], g_ring[:, b % RING, h, :],
                                                  gq[:, h, SEQ + b:SEQ + b + 1], start=True, stop=True)
                        did(m_, f"os{b}")
                v("oz")
                for h in range(GG):
                    act_(f"nsq{h}")
                    for q in range(2):
                        m_ = nc.tensor.matmul(ps[:, 2 * h + q, 0:HALF], ones[:], gsq[:, h % 2, q * HALF:(q + 1) * HALF], start=True, stop=True)
                    did(m_, f"nn{h}")
                v("lo3")
                act_("nrt3")
                for n in range(KT):
                    if n % 4 == 0:
                        pe.wait_ge(w_low, ph.slot0 + GDN_SLOTS * g + 8 + n // 4 + 1)
                    pe.wait_ge(acc_free, ph.unit0 + GDN_UNITS * g + 16 + n - 1)
                    products(n % 2, n // 4, 4, (n % 4) * P, 4 * P, gyh, gyl, 0, True, True).then_inc(parts_done, 1)

            for ph in phases:
                if ph.kind == "gdn":
                    pe.wait_ge(x_low, KT * ph.norm)
                    gdn_pre(ph)
                    for g in range(2):
                        gdn_body(ph, g)
                if ph.kind == "ret":
                    pe.wait_ge(x_low, KT * ph.norm)
                    ret_body(ph, 0)
                    with pe.Fori(1, RH) as h:
                        ret_body(ph, h)
                if ph.kind == "gate_up":
                    pe.wait_ge(x_low, KT * (ph.norm + 1))

                    def body(i, last):
                        for s in range(2):
                            k = ph.slot0 + 2 * i + s
                            pe.wait_ge(w_low, k + 1)
                            for g in range(2):
                                u = ph.unit0 + 2 * (2 * i + s) + g
                                pe.wait_ge(acc_free, u - 1)
                                m_ = products(g, s, KT, g * KT * P, P, xh, xl, 0, True, True)
                                m_.then_inc(parts_done, 1)
                                if isinstance(i, int) and i == 0 and s == 0 and g == 0:
                                    norm_sum(ph.norm)
                    rolled(pe, ph.slots // 2, body, True)
                if ph.kind == "down":
                    pe.wait_ge(h_low, FT * (ph.index + 1))

                    def body(i, last):
                        for q in range(2):
                            u = ph.unit0 + 2 * i + q
                            pe.wait_ge(acc_free, u - 1)
                            for s in range(2):
                                k = ph.slot0 + 4 * i + 2 * q + s
                                pe.wait_ge(w_low, k + 1)
                                m_ = products(q, s, 11, 0, P, hh, hl, 11 * s, s == 0, s == 1)
                                m_.then_inc(parts_done, 1)
                    rolled(pe, ph.units // 2, body)

            norm_sum(6)
            for c in range(5):
                n_ = P if c < 4 else DEC
                if c == 0:
                    pe.wait_ge(y_ready, KT)
                if c >= 2:
                    pe.wait_ge(y_out, c - 1)
                for t in range(KT):
                    m_ = nc.tensor.transpose(ps[0:n_, 2 * (c % 2) + t // 4, (t % 4) * P:(t % 4 + 1) * P], yy[:, t, c * P:c * P + n_], ident[:])
                m_.then_inc(y_turned, 1)

        @block.scalar
        def _(act):
            def split(ph, k, s, cols, done=None):
                act.wait_ge(w_landed[s], 16 * (k - s) + 32)
                if not isinstance(k, int) or k >= 2:
                    act.wait_ge(parts_done, ph.slot_done(k - 2) if done is None else done)
                nc.scalar.activation(wh[:, s, 0:cols], raw[:, s, 0:cols], ACT.Copy).then_inc(w_high, 1)

            def scaled(m, t, q, initial=True):
                if initial:
                    act.wait_ge(acc_free, t + 1)
                nc.scalar.activation(xh[:, t, :], x[:, t, :], ACT.Copy, scale=gains[:, KT * m + t:KT * m + t + 1]).then_inc(x_high, 1)
                if m or t >= 2:
                    act.wait_ge(x_ssq, KT * m + t - 1)
                nc.scalar.activation(sq[:, q, :], x[:, t, :], ACT.Square).then_inc(x_sq, 1)

            def root_of(m):
                act.wait_ge(ssq_sum, m + 1)
                nc.scalar.activation(halves(rinv[:]), ps[:, 6:8, 0:HALF], ACT.Sqrt, scale=1.0 / D,
                                     bias=eps[:, 0:1]).then_inc(ssq_root, 1)

            split(phases[0], 0, 0, SLOT)
            act.wait_ge(gains_ready, 1)
            act.wait_ge(ones_set, 2)
            for t in range(KT):
                scaled(0, t, t % 2)

            def ret_body(ph, h, last):
                def split_next(j):
                    if not (last and j == RET_SLOTS - 1 and not ph.next_cols):
                        cols = ph.next_cols if last and j == RET_SLOTS - 1 else ph.cols
                        split(ph, ph.slot0 + RET_SLOTS * h + j + 1, (j + 1) % 2, cols,
                              ph.part0 + RET_UNITS * h + RET_SLOT_DONE[j])

                first = isinstance(h, int) and h == 0
                for j in range(4):
                    split_next(j)
                    if first and j == 0:
                        root_of(ph.norm - 1)
                for c in range(4):
                    act.wait_ge(ret_t, RET_T(f"v{c}", h))
                    nc.scalar.activation(vtok[:, c, :], ps[:, 4 + c, :], ACT.Copy).then_inc(ret_a, RET_A.did(f"v{c}"))
                act.wait_ge(ret_t, RET_T("vs", h))
                nc.scalar.activation(vtok_s[:], ps[0:DEC, 7, :], ACT.Copy).then_inc(ret_a, RET_A.did("vs"))
                for e in range(4):
                    act.wait_ge(ret_t, RET_T(f"o{e}", h))
                    nc.scalar.activation(ro[:, e, :], ps[:, 4 + e, :], ACT.Copy).then_inc(ret_a, RET_A.did(f"o{e}"))
                    if e >= 2:
                        act.wait_ge(ret_p, RET_P(f"sum{e - 2}", h))
                    nc.scalar.activation(osq[:, e % 2, :], ps[:, 4 + e, :], ACT.Square).then_inc(ret_a, RET_A.did(f"sq{e}"))
                split_next(4)
                if not first:
                    act.wait_ge(s_out_stored, 16 * h)
                for t in range(2):
                    act.wait_ge(ret_t, RET_T(f"s{t}", h))
                    nc.scalar.activation(s_out[:, t, :], ps[:, 4 + t, :], ACT.Copy).then_inc(ret_a, RET_A.did(f"s{t}"))
                act.wait_ge(ret_t, RET_T("n", h))
                nc.scalar.activation(rinv_o[:], ps[:, 6, :], ACT.Sqrt, scale=1.0 / RV, bias=eps[:, 0:1])\
                    .then_inc(ret_a, RET_A.did("root"))
                act.wait_ge(head_landed, 16 * h + 16)
                for g in range(4):
                    for b in (2 * g, 2 * g + 1):
                        act.wait_ge(s_landed[b % RING], 32 * h + 16 * (b // RING) + 16)
                        nc.scalar.activation(s_ring[:, b % RING], s_ring[:, b % RING], ACT.Copy, scale=head_c[:, SEQ + 4:SEQ + 5])\
                            .then_inc(ret_a, RET_A.did(f"g{b}"))
                    act.wait_ge(acc_free, ph.unit0 + RET_UNITS * h + 8 + g + 1)
                    nc.scalar.activation(rg[:, g, :], rg[:, g, :], ACT.Silu).then_inc(ret_a, RET_A.did(f"silu{g}"))
                    act.wait_ge(ret_v, RET_V(f"y{g}", h))
                    nc.scalar.activation(yh[:, g, 0:SEQ], ro[:, g, :], ACT.Copy).then_inc(ret_a, RET_A.did(f"hi{g}"))
                    if g % 2 == 1:
                        split_next(5 + g // 2)
                act.wait_ge(ret_t, RET_T("ns", h))
                nc.scalar.activation(rinv_s[:], ps[:, 6, 0:DEC], ACT.Sqrt, scale=1.0 / RV, bias=eps[:, 0:1])\
                    .then_inc(ret_a, RET_A.did("rs"))
                for n in range(KT):
                    if n == 3:
                        split_next(7)
                    if last:
                        act.wait_ge(acc_free, ph.unit0 + RET_UNITS * h + 12 + n + 1)
                        scaled(ph.norm, n, n % 2, False)

            def gdn_pre(ph):
                act.wait_ge(pre_landed, 96)
                nc.scalar.activation(wbah[:], wba[:], ACT.Copy).then_inc(pre_a, PRE_A.did("wh"))
                root_of(ph.norm - 1)
                act.wait_ge(pre_v, PRE_V("m", 0))
                nc.scalar.activation(small[:, 1], small[:, 1], ACT.Exp).then_inc(pre_a, PRE_A.did("e"))
                nc.scalar.activation(a_log[:], a_log[:], ACT.Exp).then_inc(pre_a, PRE_A.did("na"))
                nc.scalar.activation(small[:, 6], ba[:, :, 0:GH], ACT.Sigmoid).then_inc(pre_a, PRE_A.did("beta"))
                act.wait_ge(pre_v, PRE_V("kd", 0))
                nc.scalar.activation(ebcol[:], bcol[:], ACT.Exp).then_inc(pre_a, PRE_A.did("ebc"))
                nc.scalar.activation(cdrep[:], cdrep[:], ACT.Exp).then_inc(pre_a, PRE_A.did("cd"))
                nc.scalar.activation(kdcol[:], kdcol[:], ACT.Exp).then_inc(pre_a, PRE_A.did("kd"))
                nc.scalar.activation(small[:, 4, 4, :], small[:, 5, 4, :], ACT.Exp).then_inc(pre_a, PRE_A.did("ea"))

            def gdn_body(ph, g, last):
                T, V, A, Q = GDN_T, GDN_V, GDN_A, GDN_P

                def split_next(j):
                    cols = ph.next_cols if last and j == GDN_SLOTS - 1 else ph.cols
                    split(ph, ph.slot0 + GDN_SLOTS * g + j + 1, (j + 1) % 2, cols, ph.part0 + GDN_UNITS * g + GDN_SLOT_DONE[j])

                def t_(name):
                    act.wait_ge(gdn_t, T(name, g))

                def v(name):
                    act.wait_ge(gdn_v, V(name, g))

                for n in range(12):
                    if n % 2 == 0:
                        split_next(n // 2)
                    dst = (gq, gk, gv)[n // 4]
                    v(f"cd{n}")
                    nc.scalar.activation(dst[:, n % 4, 0:SEQ], cv[:, n % 2, 0:SEQ], ACT.Silu)
                    nc.scalar.activation(dst[:, n % 4, SEQ:NTOK], cv[:, n % 2, SEQ + 3:C_LEN:TAPS], ACT.Silu).then_inc(gdn_a, A.did(f"si{n}"))
                    if n in (4, 8, 11):
                        y_ = min(n // 4 - 1, 2) if n < 11 else 2
                        t_(f"cs{4 * y_ + 3}")
                        if g and y_ == 0:
                            act.wait_ge(c_stored, 144 * g)
                        nc.scalar.activation(c_out[:, y_, :], ps[0:TAIL, 7, :], ACT.Copy).then_inc(gdn_a, A.did(f"cse{y_}"))
                act.wait_ge(eps_set, 1)
                for n in range(8):
                    if n in (0, 4):
                        split_next(6 + n // 4)
                    src = (gq, gk)[n // 4]
                    if n == 0:
                        act.wait_ge(x_ssq, KT * ph.norm)
                        act.wait_ge(gdn_a, A("si11", g))
                    else:
                        act.wait_ge(gdn_a, A(f"rt{n - 1}", g))
                    if n >= 2:
                        t_(f"ln{n - 2}")
                    nc.scalar.activation(sq[:, n % 2, :], src[:, n % 4, :], ACT.Square).then_inc(gdn_a, A.did(f"sq{n}"))
                    t_(f"ln{n}")
                    if n >= 2:
                        v(f"dq{n - 2}")
                    f_, e_ = (float(P), eps_q) if n < 4 else (1.0, eps)
                    b_ = 4 + 2 * (n % 2)
                    nc.scalar.activation(halves(cv[:, n % 2, 0:NTOK]), ps[:, b_:b_ + 2, 0:HALF], ACT.Sqrt, scale=f_, bias=e_[:, 0:1])\
                        .then_inc(gdn_a, A.did(f"rt{n}"))
                split_next(8)
                for p in range(2):
                    both = [(2 * p + x_, 4 * x_, chain[x_]) for x_ in range(2)]

                    def copy(dst, bank, name, f_=ACT.Copy):
                        nc.scalar.activation(dst, by_head(bank), f_).then_inc(gdn_a, A.did(name))

                    for c, bb, ch in both:
                        v(f"dd.{c}")
                        copy(ch["eb"][:], bb, f"eb.{c}", ACT.Exp)
                    for c, bb, ch in both:
                        act.wait_ge(gdn_p, Q(f"n2.{c}", g))
                        nc.scalar.activation(ch["d2"][:], ch["d2"][:], ACT.Exp).then_inc(gdn_a, A.did(f"d2.{c}"))
                        act.wait_ge(gdn_p, Q(f"n1.{c}", g))
                        nc.scalar.activation(ch["d1"][:], ch["d1"][:], ACT.Exp, scale=-1.0).then_inc(gdn_a, A.did(f"d1.{c}"))
                    for c, bb, ch in both:
                        t_(f"mt.{c}")
                        copy(ch["mt"][:], bb + 2, f"mt.{c}")
                    for l in range(1, LV + 1):
                        for c, bb, ch in both:
                            t_(f"t{l}.{c}")
                            copy(ch["t1"][:], bb + 3, f"t{l}.{c}")
                    for c, bb, ch in both:
                        t_(f"u.{c}")
                        copy(ch["u"][:], bb + 1, f"u.{c}")
                        t_(f"wk.{c}")
                        copy(ch["wk"][:], bb + 3, f"wk.{c}")
                    for c, bb, ch in both:
                        t_(f"o.{c}")
                        nc.scalar.activation(gq[:, :, c * P:(c + 1) * P], by_head(bb + 1), ACT.Copy).then_inc(gdn_a, A.did(f"oc.{c}"))
                act.wait_ge(acc_free, ph.unit0 + GDN_UNITS * g + 16)
                nc.scalar.activation(gz[:], gz[:], ACT.Silu).then_inc(gdn_a, A.did("sz"))
                v("oz")
                for h in range(GG):
                    if h >= 2:
                        t_(f"nn{h - 2}")
                    act.wait_ge(gdn_a, A("oc.3", g) if h == 0 else A(f"nrt{h - 1}", g))
                    nc.scalar.activation(gsq[:, h % 2, :], gq[:, h, :], ACT.Square).then_inc(gdn_a, A.did(f"nsq{h}"))
                    t_(f"nn{h}")
                    if h >= 2:
                        v(f"y{h - 2}")
                    nc.scalar.activation(halves(grt[:, h % 2, :]), ps[:, 2 * h:2 * h + 2, 0:HALF], ACT.Sqrt, scale=1.0 / P, bias=eps[:, 0:1])\
                        .then_inc(gdn_a, A.did(f"nrt{h}"))
                for h in range(GG):
                    v(f"yz{h}")
                    nc.scalar.activation(gyh[:, h, :], gq[:, h, :], ACT.Copy).then_inc(gdn_a, A.did(f"hi{h}"))
                for n in range(KT):
                    if n == 3:
                        split_next(9)
                    if last:
                        act.wait_ge(acc_free, ph.unit0 + GDN_UNITS * g + 16 + n + 1)
                        scaled(ph.norm, n, n % 2, False)

            for ph in phases:
                if ph.kind == "gdn":
                    gdn_pre(ph)
                    for g in range(2):
                        gdn_body(ph, g, g == 1)
                if ph.kind == "ret":
                    ret_body(ph, 0, False)
                    with act.Fori(1, RH - 1) as h:
                        ret_body(ph, h, False)
                    ret_body(ph, RH - 1, True)
                if ph.kind == "gate_up":
                    def body(i, last):
                        for s in range(2):
                            k = ph.slot0 + 2 * i + s
                            cols = ph.next_cols if last and s == 1 else ph.cols
                            split(ph, k + 1, (s + 1) % 2, cols)
                            if isinstance(i, int) and i == 0 and s == 0:
                                root_of(ph.norm)
                            j = 2 * i + s
                            n = FT * ph.index + j
                            act.wait_ge(acc_free, ph.unit0 + 2 * j + 1)
                            nc.scalar.activation(gate[:], gate[:], ACT.Silu).then_inc(gate_ready, 1)
                            act.wait_ge(h_ready, n + 1)
                            act.sem_inc(act_held, 1)
                            nc.scalar.activation(hh[:, j, :], up[:], ACT.Copy).then_inc(h_high, 1)
                    rolled(act, ph.slots // 2, body, True)
                if ph.kind == "down":
                    def body(i, last):
                        for q in range(2):
                            for s in range(2):
                                k = ph.slot0 + 4 * i + 2 * q + s
                                cols = ph.next_cols if last and q == 1 and s == 1 else ph.cols
                                if cols:
                                    split(ph, k + 1, (s + 1) % 2, cols)
                            t = 2 * i + q
                            act.wait_ge(acc_free, ph.unit0 + t + 1)
                            act.sem_inc(act_held, 1)
                            nc.scalar.activation(xh[:, t, :], x[:, t, :], ACT.Copy,
                                                 scale=gains[:, bass.ds(KT * ph.norm + t, 1)]).then_inc(x_high, 1)
                            act.wait_ge(x_ssq, KT * ph.norm + t - 1)
                            act.sem_inc(act_held, 1)
                            nc.scalar.activation(sq[:, q, :], x[:, t, :], ACT.Square).then_inc(x_sq, 1)
                    rolled(act, ph.units // 2, body)

            root_of(6)

        @block.vector
        def _(dve):
            def split(ph, k, s, cols):
                dve.wait_ge(w_high, k + 1)
                nc.vector.tensor_tensor(wl[:, s, 0:cols], raw[:, s, 0:cols], wh[:, s, 0:cols].bitcast(F32),
                                        ALU.subtract).then_inc(w_low, 1)

            def scaled_low(m, t):
                dve.wait_ge(x_high, KT * m + t + 1)
                nc.vector.scalar_tensor_tensor(xl[:, t, :], x[:, t, :], gains[:, bass.ds(KT * m + t, 1)],
                                               xh[:, t, :].bitcast(F32), ALU.mult, ALU.subtract).then_inc(x_low, 1)

            dve.wait_ge(gains_turned, 1)
            nc.vector.tensor_copy(gains[:], ps[:, 7, 0:56]).then_inc(gains_ready, 1)
            dve.wait_ge(gains_ready, 1)
            for t in range(KT):
                b = 2 * (t % 2)
                dve.wait_ge(parts_done, t + 1)
                nc.vector.tensor_copy(x[:, t, 0:SEQ], ps[:, b, :])
                m_ = nc.vector.tensor_copy(x[:, t, SEQ:NTOK], ps[:, b + 1, 0:DEC])
                m_.then_inc(acc_free, 1)
                scaled_low(0, t)
            split(phases[0], 0, 0, SLOT)

            def ret_body(ph, h, last):
                def split_next(j):
                    if not (last and j == RET_SLOTS - 1 and not ph.next_cols):
                        cols = ph.next_cols if last and j == RET_SLOTS - 1 else ph.cols
                        split(ph, ph.slot0 + RET_SLOTS * h + j + 1, (j + 1) % 2, cols)

                def arrived(j):
                    dve.wait_ge(parts_done, ph.part0 + RET_UNITS * h + j + 1)

                def freed(j):
                    dve.wait_ge(acc_free, ph.unit0 + RET_UNITS * h + j + 1)

                first = isinstance(h, int) and h == 0
                V, A, T = RET_V, RET_A, RET_T
                for j, (dst, scale, name) in enumerate(((rq, 1.0, "q"), (rk, RET_SCALE, "k"))):
                    split_next(j)
                    if first and j == 0:
                        dve.wait_ge(ssq_root, ph.norm)
                        nc.vector.reciprocal(rinv[:], rinv[:]).then_inc(ssq_inv, 1)
                        dve.wait_ge(ssq_inv, ph.norm)
                        dve.wait_ge(ret_consts, 48)
                        nc.vector.tensor_tensor(cosr[:], cosr[:], rinv[:], ALU.mult).then_inc(ret_tables, 1)
                        nc.vector.tensor_tensor(sinr[:], sinr[:], rinv[:], ALU.mult).then_inc(ret_tables, 1)
                        dve.wait_ge(ret_tables, 2)
                    if j or not first:
                        dve.wait_ge(ret_v, V("q", h) if j else V("yl", h - 1))
                    mul = lambda o, u, t: nc.vector.scalar_tensor_tensor(halves(o), pair(u), scale, halves(t[:]), ALU.mult, ALU.mult)
                    arrived(2 * j)
                    mul(dst[:, 0, :], 0, cosr)
                    mul(rot[:, 0, :], 0, sinr).then_inc(acc_free, 1)
                    arrived(2 * j + 1)
                    mul(rot[:, 1, :], 1, sinr)
                    mul(dst[:, 1, :], 1, cosr).then_inc(acc_free, 1)
                    freed(2 * j + 1)
                    nc.vector.tensor_tensor(dst[:, 0, :], dst[:, 0, :], rot[:, 1, :], ALU.subtract)
                    nc.vector.tensor_tensor(dst[:, 1, :], dst[:, 1, :], rot[:, 0, :], ALU.add).then_inc(ret_v, V.did(name))
                for e in range(4):
                    if e % 2 == 0:
                        split_next(2 + e // 2)
                    arrived(4 + e)
                    nc.vector.tensor_tensor(halves(rv[:, e, :]), pair(e), halves(rinv[:]), ALU.mult).then_inc(acc_free, 1)
                dve.wait_ge(head_landed, 16 * h + 16)
                dve.wait_ge(ret_t, T("p0", h))
                nc.vector.tensor_tensor(pt[:, 0:512], ps[:, 4, :], head_c[:, 0:512], ALU.mult).then_inc(ret_v, V.did("pt0"))
                dve.wait_ge(ret_t, T("p1", h))
                nc.vector.tensor_tensor(pt[:, 512:896], ps[:, 5, 0:384], head_c[:, 0:384], ALU.mult).then_inc(ret_v, V.did("pt1"))
                dve.wait_ge(ret_t, T("p23", h))
                nc.vector.tensor_tensor(pt[:, 896:1152], ps[:, 6, 0:256], head_c[:, 0:256], ALU.mult)
                nc.vector.tensor_tensor(pt[:, 1152:1280], ps[:, 6, 256:384], head_c[:, 0:128], ALU.mult).then_inc(ret_v, V.did("pt23"))
                for name, c in (("k01", 0), ("k23", 2)):
                    dve.wait_ge(ret_t, T(name, h))
                    for n in range(2):
                        m_ = nc.vector.tensor_scalar(ktok[:, c + n, :], ps[:, 7, n * RK:(n + 1) * RK],
                                                     head_c[:, SEQ + c + n:SEQ + c + n + 1], None, ALU.mult)
                    m_.then_inc(ret_v, V.did(name))
                split_next(4)
                dve.wait_ge(ret_a, A("root", h))
                nc.vector.reciprocal(rinv_o[:], rinv_o[:]).then_inc(ret_v, V.did("ro"))
                for g in range(4):
                    for b in (2 * g, 2 * g + 1):
                        dve.wait_ge(ret_t, T(f"b{b}", h))
                        dve.wait_ge(ret_a, A(f"g{b}", h))
                        for t in range(2):
                            st_ = s_ring[:, b % RING, t, :]
                            m_ = nc.vector.scalar_tensor_tensor(st_, ps[:, 4 + b % 2, :], rk[:, t, SEQ + b:SEQ + b + 1], st_,
                                                                ALU.mult, ALU.add)
                        m_.then_inc(ret_v, V.did(f"u{b}"))
                    arrived(8 + g)
                    nc.vector.tensor_tensor(halves(rg[:, g, :]), pair(g), halves(rinv[:]), ALU.mult).then_inc(acc_free, 1)
                    dve.wait_ge(ret_v, V("ro", h))
                    nc.vector.tensor_tensor(ro[:, g, :], ro[:, g, :], rinv_o[:], ALU.mult).then_inc(ret_v, V.did(f"on{g}"))
                    dve.wait_ge(ret_a, A(f"silu{g}", h))
                    dve.wait_ge(ret_v, V(f"on{g}", h))
                    nc.vector.tensor_tensor(ro[:, g, :], ro[:, g, :], rg[:, g, 0:SEQ], ALU.mult).then_inc(ret_v, V.did(f"y{g}"))
                    dve.wait_ge(ret_a, A(f"hi{g}", h))
                    nc.vector.tensor_tensor(yl[:, g, 0:SEQ], ro[:, g, :], yh[:, g, 0:SEQ].bitcast(F32), ALU.subtract)\
                        .then_inc(ret_v, V.did(f"lo{g}"))
                    if g % 2 == 1:
                        split_next(5 + g // 2)
                dve.wait_ge(ret_t, T("q7", h))
                nc.vector.tensor_copy(o_s[:].rearrange("p e b -> p (e b)"), ps[:, 7, 0:4 * DEC]).then_inc(ret_v, V.did("os"))
                dve.wait_ge(ret_v, V("os", h))
                nc.vector.tensor_tensor(osq_s[:], o_s[:], o_s[:], ALU.mult).then_inc(ret_v, V.did("ossq"))
                dve.wait_ge(ret_a, A("rs", h))
                nc.vector.reciprocal(rinv_s[:], rinv_s[:]).then_inc(ret_v, V.did("rs"))
                dve.wait_ge(ret_v, V("rs", h))
                nc.vector.tensor_tensor(o_s[:], o_s[:], rinv_s[:].rearrange("p (e b) -> p e b", e=1).broadcast_to([P, 4, DEC]),
                                        ALU.mult).then_inc(ret_v, V.did("osn"))
                dve.wait_ge(ret_v, V("osn", h))
                nc.vector.tensor_tensor(o_s[:], o_s[:], rg[:, :, SEQ:NTOK], ALU.mult).then_inc(ret_v, V.did("ys"))
                dve.wait_ge(ret_v, V("ys", h))
                nc.vector.tensor_copy(yh[:, :, SEQ:NTOK], o_s[:]).then_inc(ret_v, V.did("yh"))
                dve.wait_ge(ret_v, V("yh", h))
                nc.vector.tensor_tensor(yl[:, :, SEQ:NTOK], o_s[:], yh[:, :, SEQ:NTOK].bitcast(F32), ALU.subtract)\
                    .then_inc(ret_v, V.did("yl"))
                for n in range(KT):
                    arrived(12 + n)
                    xt = halves(x[:, n, :])
                    nc.vector.tensor_tensor(xt, pair(n), xt, ALU.add).then_inc(acc_free, 1)
                    if n == 3:
                        split_next(7)
                    if last:
                        scaled_low(ph.norm, n)

            def gdn_pre(ph):
                V, A, T = PRE_V, PRE_A, PRE_T

                def did(m_, name):
                    m_.then_inc(pre_v, V.did(name))

                def v(name):
                    dve.wait_ge(pre_v, V(name, 0))

                dve.wait_ge(pre_a, A("wh", 0))
                did(nc.vector.tensor_tensor(wbal[:], wba[:], wbah[:].bitcast(F32), ALU.subtract), "wl")
                dve.wait_ge(pre_t, T("cw", 0))
                did(nc.vector.tensor_copy(conv_w[:].rearrange("p j t -> p (j t)"), ps[:, 4, 0:96]), "cw")
                dve.wait_ge(ssq_root, ph.norm)
                nc.vector.reciprocal(rinv[:], rinv[:]).then_inc(ssq_inv, 1)
                dve.wait_ge(pre_t, T("rc", 0))
                did(nc.vector.tensor_copy(r_col[:], ps[:, 4, 128:133]), "rc")
                v("rc")
                did(nc.vector.tensor_tensor(ba[:], ps[:, 5, 0:80].rearrange("p (c n) -> p c n", c=5),
                                            r_col[:].rearrange("p (c o) -> p c o", o=1).broadcast_to([P, 5, 16]), ALU.mult), "ba")
                v("ba")
                each_block = lambda t: t[:].rearrange("p (o h) -> p o h", o=1).broadcast_to([P, 5, GH])
                y_, e_, z_, w_, p_, a_ = (small[:, n] for n in range(6))
                did(nc.vector.tensor_tensor(y_, ba[:, :, GH:2 * GH], each_block(dt_b), ALU.add), "y")
                v("y")
                did(nc.vector.scalar_tensor_tensor(e_, y_, -1.0, y_, ALU.mult, ALU.min), "m")
                dve.wait_ge(pre_a, A("e", 0))
                did(nc.vector.tensor_scalar(w_, e_, 2.0, None, ALU.add), "d")
                v("d")
                did(nc.vector.reciprocal(w_, w_), "di")
                v("di")
                did(nc.vector.tensor_tensor(z_, e_, w_, ALU.mult), "z")
                v("z")
                did(nc.vector.tensor_tensor(w_, z_, z_, ALU.mult), "w")
                v("w")
                did(nc.vector.tensor_scalar(p_, w_, 1.0 / 17, None, ALU.mult), "p0")
                for n in range(1, 7):
                    v(f"p{n - 1}")
                    did(nc.vector.scalar_tensor_tensor(p_, p_, 1.0 / (17 - 2 * n), w_, ALU.add, ALU.mult), f"p{n}")
                v("p6")
                did(nc.vector.scalar_tensor_tensor(p_, p_, 1.0 / 3, w_, ALU.add, ALU.mult), "l")
                v("l")
                did(nc.vector.scalar_tensor_tensor(p_, p_, 1.0, z_, ALU.add, ALU.mult), "r")
                v("r")
                did(nc.vector.tensor_scalar(y_, y_, 0.0, None, ALU.max), "sp")
                v("sp")
                nc.vector.scalar_tensor_tensor(e_, p_, 2.0, y_, ALU.mult, ALU.add).then_inc(softplus_ready, 1)
                dve.wait_ge(softplus_ready, 1)
                dve.wait_ge(pre_a, A("na", 0))
                did(nc.vector.scalar_tensor_tensor(a_, e_, -1.0, each_block(a_log), ALU.mult, ALU.mult), "a")
                dve.wait_ge(pre_t, T("blast", 0))
                flat = lambda t: t[:].rearrange("p c h -> p (c h)")
                did(nc.vector.tensor_copy(flat(bcol), ps[:, 5, 128:160]), "bcol")
                v("bcol")
                did(nc.vector.tensor_copy(flat(cdrep), ps[:, 5, 160:192]), "cdl")
                v("cdl")
                did(nc.vector.tensor_tensor(kdcol[:], cdrep[:], bcol[:], ALU.subtract), "kd")
                dve.wait_ge(pre_a, A("ea", 0))
                did(nc.vector.tensor_tensor(bebcol[:], ebcol[:], small[:, 6, 0:4, :], ALU.mult), "beb")
                for n, src, name in ((0, small[:, 4, 4, :], "sma"), (1, small[:, 6, 4, :], "smb")):
                    did(nc.vector.tensor_tensor(sm[:, n], src.rearrange("p (h o) -> p h o", o=1).broadcast_to([P, GH, DEC]),
                                                smask.rearrange("p (o b) -> p o b", o=1).broadcast_to([P, GH, DEC]), ALU.mult), name)
                dve.wait_ge(pre_t, T("smp", 0))
                did(nc.vector.tensor_copy(eab[:].rearrange("p a h b -> p (a h b)"), ps[:, 4, 256:384]), "eab")
                v("eab")

            def gdn_body(ph, g, last):
                T, V, A, Q = GDN_T, GDN_V, GDN_A, GDN_P
                h0 = g * GG

                def split_next(j):
                    cols = ph.next_cols if last and j == GDN_SLOTS - 1 else ph.cols
                    split(ph, ph.slot0 + GDN_SLOTS * g + j + 1, (j + 1) % 2, cols)

                def t_(name):
                    dve.wait_ge(gdn_t, T(name, g))

                def v(name):
                    dve.wait_ge(gdn_v, V(name, g))

                def act_(name):
                    dve.wait_ge(gdn_a, A(name, g))

                def did(m_, name):
                    m_.then_inc(gdn_v, V.did(name))

                if g:
                    dve.wait_ge(parts_done, ph.part0 + GDN_UNITS * g)
                did(nc.vector.memset(uu[:, :, 0:TAPS - 1], 0.0), "uz")
                if g:
                    dve.wait_ge(gs_stored, 16 * g)
                did(nc.vector.memset(gs[:], 0.0), "s0")
                v("s0")
                for n in range(12):
                    if n % 2 == 0:
                        split_next(n // 2)
                    dve.wait_ge(parts_done, ph.part0 + GDN_UNITS * g + n + 1)
                    if n >= 2:
                        t_(f"cs{n - 2}")
                        v(f"cd{n - 2}")
                    q, r_ = n % 2, uu[:, n % 2]
                    nc.vector.tensor_tensor(r_[:, 3:3 + HALF], ps[:, 2 * q, 0:HALF], rinv[:, 0:HALF], ALU.mult)
                    nc.vector.tensor_tensor(r_[:, 3 + HALF:3 + SEQ], ps[:, 2 * q + 1, 0:SEQ - HALF], rinv[:, HALF:SEQ], ALU.mult)
                    nc.vector.tensor_tensor(r_[:, 3 + SEQ + 3:U_LEN:TAPS], ps[:, 2 * q + 1, SEQ - HALF:HALF], rinv[:, SEQ:NTOK], ALU.mult)\
                        .then_inc(acc_free, 1)
                    if n == 0:
                        t_("ct")
                    did(nc.vector.tensor_copy(r_[:, 3 + SEQ:U_LEN].rearrange("p (b j) -> p b j", j=TAPS)[:, :, 0:3],
                                              ps[:, 6, n * 24:(n + 1) * 24].rearrange("p (b j) -> p b j", j=3)), f"ux{n}")
                    v(f"ux{n}")
                    w_ = lambda j: conv_w[:, j, (n // 4) * GH + h0 + n % 4:(n // 4) * GH + h0 + n % 4 + 1]
                    c_ = cv[:, n % 2, :]
                    if n >= 2:
                        act_(f"si{n - 2}")
                    did(nc.vector.tensor_scalar(c_, r_[:, 0:C_LEN], w_(0), None, ALU.mult), f"ca{n}")
                    for j, name in ((1, "cb"), (2, "cc"), (3, "cd")):
                        v(f"{('ca', 'cb', 'cc')[j - 1]}{n}")
                        did(nc.vector.scalar_tensor_tensor(c_, r_[:, j:j + C_LEN], w_(j), c_, ALU.mult, ALU.add), f"{name}{n}")
                for n in range(4):
                    if n % 2 == 0:
                        split_next(6 + n // 2)
                    dve.wait_ge(parts_done, ph.part0 + GDN_UNITS * g + 12 + n + 1)
                    nc.vector.tensor_tensor(halves(gz[:, n, :]), pair(n), halves(rinv[:]), ALU.mult).then_inc(acc_free, 1)
                    for m in (2 * n, 2 * n + 1):
                        act_(f"rt{m}")
                        dst = (gq, gk)[m // 4][:, m % 4, :]
                        did(nc.vector.reciprocal(cv[:, m % 2, 0:NTOK], cv[:, m % 2, 0:NTOK]), f"ri{m}")
                        v(f"ri{m}")
                        did(nc.vector.tensor_tensor(dst, dst, cv[:, m % 2, 0:NTOK], ALU.mult), f"dq{m}")
                split_next(8)
                v("dq7")
                for p in range(2):
                    both = [(2 * p + x_, 4 * x_, chain[x_]) for x_ in range(2)]
                    tt = nc.vector.tensor_tensor
                    hs = lambda t, c: heads(t[:, c, h0:h0 + GG])
                    for c, bb, ch in both:
                        if p:
                            t_(f"s.{c - 2}")
                            v(f"S.{c - 2}")
                        else:
                            dve.wait_ge(c_stored, 144 * (g + 1))
                            act_("rt7")
                        did(tt(ch["t1"][:], every(ut), heads(small[:, 5, c, h0:h0 + GG]), ALU.mult), f"aut.{c}")
                    for c, bb, ch in both:
                        t_(f"br.{c}")
                        did(tt(ch["dd"][:], by_head(bb), hs(bcol, c), ALU.subtract), f"dd.{c}")
                    for c, bb, ch in both:
                        t_(f"kt.{c}")
                        did(tt(ch["kb"][:], by_head(bb + 1), hs(bebcol, c), ALU.mult), f"kb.{c}")
                        did(tt(ch["kd"][:], by_head(bb + 1), hs(kdcol, c), ALU.mult), f"kd.{c}")
                        t_(f"vt.{c}")
                        did(tt(ch["vb"][:], by_head(bb + 2), heads(small[:, 6, c, h0:h0 + GG]), ALU.mult), f"vb.{c}")
                    for c, bb, ch in both:
                        t_(f"kk.{c}")
                        dve.wait_ge(gdn_p, Q(f"d1b.{c}", g))
                        did(tt(ch["d1"][:], by_head(bb + 3), ch["d1"][:], ALU.mult), f"L.{c}")
                    for c, bb, ch in both:
                        dve.wait_ge(gdn_p, Q(f"l0.{c}", g))
                        did(tt(ch["m"][:], every(ident[:]), ch["la"][:], ALU.subtract), f"m0.{c}")
                        t_(f"qk.{c}")
                        act_(f"d2.{c}")
                        did(tt(ch["d2"][:], by_head(bb + 1), ch["d2"][:], ALU.mult), f"pt.{c}")
                        act_(f"eb.{c}")
                        did(tt(ch["eb"][:], gq[:, :, c * P:(c + 1) * P], ch["eb"][:], ALU.mult), f"qd.{c}")
                    for l in range(1, LV + 1):
                        for c, bb, ch in both:
                            t_(f"a{l}.{c}")
                            act_(f"mt.{c}" if l == 1 else f"t{l}.{c}")
                            v(f"m0.{c}" if l == 1 else f"b{l - 1}.{c}")
                            did(tt(ch["mt"][:], ch["mt"][:], by_head(bb), ALU.subtract), f"a{l}.{c}")
                            if l < LV:
                                t_(f"b{l}.{c}")
                                did(tt(ch["m"][:], ch["m"][:], by_head(bb + 2), ALU.subtract), f"b{l}.{c}")
                    for c, bb, ch in both:
                        t_(f"w.{c}")
                        act_(f"u.{c}")
                        did(tt(ch["u"][:], ch["u"][:], by_head(bb), ALU.subtract), f"W.{c}")
                        t_(f"s.{c}")
                        dve.wait_ge(gdn_p, Q(f"s2.{c}", g))
                        did(tt(gs[:], gs2[:], by_head(bb + 2), ALU.add), f"S.{c}")
                for hf in range(2):
                    mine = slice(4 * hf, 4 * hf + 4)
                    t_(f"r{hf}")
                    w_ = wt[:, :, mine]
                    if hf == 0:
                        v("S.3")
                        act_("oc.3")
                    r_ = ps[:, 0, 0:16].rearrange("p (h b) -> p h b", h=GG)
                    did(nc.vector.tensor_tensor(w_, r_, eab[:, 0, h0:h0 + GG, mine], ALU.mult), f"wa{hf}")
                    v(f"wa{hf}")
                    did(nc.vector.tensor_tensor(w_, gv[:, :, SEQ + 4 * hf:SEQ + 4 * hf + 4], w_, ALU.subtract), f"wb{hf}")
                    v(f"wb{hf}")
                    did(nc.vector.tensor_tensor(w_, w_, eab[:, 1, h0:h0 + GG, mine], ALU.mult), f"wc{hf}")
                    v(f"wc{hf}")
                    for b in range(4 * hf, 4 * hf + 4):
                        did(nc.vector.tensor_tensor(dg[:, b % 4], every(ident[:]), heads(wt[:, :, b]), ALU.mult), f"dg{b}")
                    for b in range(4 * hf, 4 * hf + 4):
                        t_(f"wr{b}")
                        did(nc.vector.tensor_tensor(dg[:, b % 4], by_head(4 + b % 4), heads(gk[:, :, SEQ + b]), ALU.mult), f"kw{b}")
                        dve.wait_ge(gdn_p, Q(f"se{b}", g))
                        v(f"kw{b}")
                        did(nc.vector.tensor_tensor(g_ring[:, b % RING], g_ring[:, b % RING], dg[:, b % 4], ALU.add), f"sn{b}")
                t_("os7")
                did(nc.vector.tensor_copy(gq[:, :, SEQ:NTOK], ps[:, 1, 0:GG * DEC].rearrange("p (h b) -> p h b", h=GG)), "oz")
                for h in range(GG):
                    act_(f"nrt{h}")
                    if h == 0:
                        act_("sz")
                    did(nc.vector.reciprocal(grt[:, h % 2, :], grt[:, h % 2, :]), f"rn{h}")
                    v(f"rn{h}")
                    did(nc.vector.scalar_tensor_tensor(gq[:, h, :], gq[:, h, :], norm_w[:, 0:1], grt[:, h % 2, :], ALU.mult, ALU.mult), f"y{h}")
                    v(f"y{h}")
                    did(nc.vector.tensor_tensor(gq[:, h, :], gq[:, h, :], gz[:, h, :], ALU.mult), f"yz{h}")
                for h in range(GG):
                    act_(f"hi{h}")
                    did(nc.vector.tensor_tensor(gyl[:, h, :], gq[:, h, :], gyh[:, h, :].bitcast(F32), ALU.subtract), f"lo{h}")
                for n in range(KT):
                    dve.wait_ge(parts_done, ph.part0 + GDN_UNITS * g + 16 + n + 1)
                    xt = halves(x[:, n, :])
                    nc.vector.tensor_tensor(xt, pair(n), xt, ALU.add).then_inc(acc_free, 1)
                    if n == 3:
                        split_next(9)
                    if last:
                        scaled_low(ph.norm, n)

            def mixer_stored(index):
                if index == 1:
                    for n in range(RING):
                        dve.wait_ge(s_stored[n], 32 * RH)
                    dve.wait_ge(s_out_stored, 16 * RH)
                if index == 3:
                    for n in range(RING):
                        dve.wait_ge(g_stored[n], 64)
                    dve.wait_ge(gs_stored, 32)

            for ph in phases:
                if ph.kind == "gdn":
                    gdn_pre(ph)
                    for g in range(2):
                        gdn_body(ph, g, g == 1)
                if ph.kind == "ret":
                    ret_body(ph, 0, False)
                    with dve.Fori(1, RH - 1) as h:
                        ret_body(ph, h, False)
                    ret_body(ph, RH - 1, True)
                if ph.kind == "gate_up":
                    def body(i, last):
                        for s in range(2):
                            k = ph.slot0 + 2 * i + s
                            cols = ph.next_cols if last and s == 1 else ph.cols
                            split(ph, k + 1, (s + 1) % 2, cols)
                            if isinstance(i, int) and i == 0 and s == 0:
                                dve.wait_ge(ssq_root, ph.norm + 1)
                                nc.vector.reciprocal(rinv[:], rinv[:]).then_inc(ssq_inv, 1)
                                dve.wait_ge(ssq_inv, ph.norm + 1)
                                mixer_stored(ph.index)
                            j = 2 * i + s
                            n = FT * ph.index + j
                            if not isinstance(n, int) or n > 0:
                                dve.wait_ge(h_low, n)
                            for g, t_ in ((0, gate), (1, up)):
                                dve.wait_ge(parts_done, ph.unit_done(ph.unit0 + 2 * j + g))
                                nc.vector.tensor_tensor(halves(t_[:]), pair(g), halves(rinv[:]), ALU.mult).then_inc(acc_free, 1)
                            dve.wait_ge(gate_ready, n + 1)
                            dve.wait_ge(acc_free, ph.unit0 + 2 * j + 2)
                            nc.vector.tensor_tensor(up[:], up[:], gate[:], ALU.mult).then_inc(h_ready, 1)
                            dve.wait_ge(h_high, n + 1)
                            nc.vector.tensor_tensor(hl[:, j, :], up[:], hh[:, j, :].bitcast(F32), ALU.subtract).then_inc(h_low, 1)
                    rolled(dve, ph.slots // 2, body, True)
                if ph.kind == "down":
                    def body(i, last):
                        for q in range(2):
                            for s in range(2):
                                k = ph.slot0 + 4 * i + 2 * q + s
                                cols = ph.next_cols if last and q == 1 and s == 1 else ph.cols
                                if cols:
                                    split(ph, k + 1, (s + 1) % 2, cols)
                            t = 2 * i + q
                            dve.wait_ge(parts_done, ph.unit_done(ph.unit0 + t))
                            xt = halves(x[:, t, :])
                            m_ = nc.vector.scalar_tensor_tensor(xt, pair(q), 0.5, xt, ALU.mult, ALU.add)
                            m_.then_inc(acc_free, 1)
                            scaled_low(ph.norm, t)
                    rolled(dve, ph.units // 2, body)

            dve.wait_ge(ssq_root, 7)
            nc.vector.reciprocal(rinv[:], rinv[:]).then_inc(ssq_inv, 1)
            dve.wait_ge(ssq_inv, 7)
            for t in range(KT):
                nc.vector.scalar_tensor_tensor(yy[:, t, :], x[:, t, :], gains[:, 6 * KT + t:6 * KT + t + 1], rinv[:], ALU.mult, ALU.mult)\
                    .then_inc(y_ready, 1)
            for c in range(5):
                n_ = P if c < 4 else DEC
                dve.wait_ge(y_turned, c + 1)
                if c >= 2:
                    dve.wait_ge(y_stored[c % 2], 16 * (c // 2))
                nc.vector.tensor_copy(y_tok[0:n_, c % 2, :].rearrange("p (q n) -> p q n", q=2), ps[0:n_, 2 * (c % 2):2 * (c % 2) + 2, :])\
                    .then_inc(y_out, 1)


_INS = ['x_prompt', 'x_sample', 'state_ret', 'state_gdn', 'state_gdn_conv', 'gdn_w_in', 'gdn_conv_w', 'gdn_a_log',
        'gdn_dt_bias', 'gdn_norm_w', 'gdn_w_out', 'norm_g', 'ffn_gu', 'ffn_down', 'ret_w_in', 'ret_w_out', 'final_g']
_OUTS = [((1, 512, 1024), 'float32'), ((8, 1, 1024), 'float32'), ((1, 1, 4, 256, 512), 'float32'),
         ((1, 1, 8, 128, 128), 'float32'), ((1, 1, 3, 3072), 'float32'), ((1, 8, 4, 256, 512), 'float32'),
         ((1, 8, 8, 128, 128), 'float32'), ((1, 8, 3, 3072), 'float32')]


def tables():
    import numpy as np

    f = np.float32
    t = {"c_ident": np.eye(P, dtype=f)}
    sel = np.zeros((DEC, DEC, P), f)
    for b in range(DEC):
        sel[b, b] = 1
    t["c_sel"] = sel
    theta = (f(1) / (f(10000.0) ** np.linspace(0, 1, RK // 2, dtype=f))).astype(f)
    pos = np.concatenate([np.arange(SEQ), np.full(DEC, 4096)]).astype(f)
    ang = (theta[:, None] * pos[None, :]).astype(f).astype(np.float64)
    t["c_cos"], t["c_sin"] = np.cos(ang).astype(f), np.sin(ang).astype(f)
    head = np.zeros((RH, P, SEQ + 5))
    j = np.arange(P)[:, None]
    i = np.arange(SEQ)[None, :]
    for h in range(RH):
        g = 1.0 - 2.0 ** (-5 - h)
        head[h, :, 0:SEQ] = np.where(i >= j, g ** np.maximum(i - j, 0), 0)
        for c in range(4):
            head[h, :, SEQ + c] = g ** (SEQ - 1 - (c * P + np.arange(P)))
        head[h, :, SEQ + 4] = g
    t["c_head"] = head.astype(f)
    con = np.zeros((P, 10 * P + DEC), f)
    row, col = np.arange(P)[:, None], np.arange(P)[None, :]
    con[:, 0:P] = row <= col
    con[:, P:2 * P] = np.where(col >= row, 0, -1e30)
    con[:, 2 * P:3 * P] = np.where(col < row, 0, 1e30)
    for n in range(7):
        half = 2 ** n
        con[:, (3 + n) * P:(4 + n) * P] = (row // (2 * half) == col // (2 * half)) & (row // half % 2 == 1) & (col // half % 2 == 0)
    for b in range(DEC):
        con[P - DEC + b, 10 * P + b] = 1
    t["c_gdn"] = con
    return t


def kernel(**inputs):
    import numpy as _np
    import concourse.bacc as _bacc
    from concourse import mybir as _mybir
    from concourse.bass_utils import run_bass_kernel_spmd as _run

    nc = _bacc.Bacc("TRN2", target_bir_lowering=False, num_devices=1)
    arrays, args = {}, {}
    given = {n: _np.ascontiguousarray(inputs[n]) for n in _INS}
    given.update(tables())
    for name, v in given.items():
        arrays[f"in_{name}_dram"] = v
        args[name] = nc.dram_tensor(f"in_{name}_dram", v.shape, _mybir.dt.from_np(v.dtype), kind="ExternalInput").ap()
    outs = []
    for i, (shape, dtype) in enumerate(_OUTS):
        outs.append(nc.dram_tensor(f"out_{i}_dram", shape, _mybir.dt.from_np(_np.dtype(dtype)), kind="ExternalOutput").ap())
    build(nc, args, outs)
    r = _run(nc, [arrays], core_ids=[0])
    return tuple(r.results[0][f"out_{i}_dram"] for i in range(len(_OUTS)))
```

```python
from contextlib import ExitStack

import concourse.bass as bass
from concourse import mybir

F32 = mybir.dt.float32
F32R = mybir.dt.float32r
ALU = mybir.AluOpType
ACT = mybir.ActivationFunctionType

P = 128
D, SEQ, DEC = 1024, 512, 8
KT = D // P
NTOK = SEQ + DEC
HALF = NTOK // 2
FF = 2816
FT = FF // P
EPS = 1e-6
SLOT = 16 * P

RH, RK, RV = 4, 256, 512
RET_SCALE = RK ** -0.5
RING = 4
Y_PARTS = ((0, 4), (4, 6), (6, 8))


class Steps:

    def __init__(self, names):
        self.names, self.seen = names.split(), 0

    def __call__(self, name, turn):
        return turn * len(self.names) + self.names.index(name) + 1

    def did(self, name):
        assert self.names[self.seen % len(self.names)] == name, (name, self.names[self.seen % len(self.names)])
        self.seen += 1
        return 1


RET_T = Steps("p0 p1 p23 k01 v0 v1 v2 k23 v3 vs o0 o1 o2 o3 s0 s1 n "
              "b0 b1 b2 b3 q0 q1 b4 b5 q2 q3 b6 b7 q4 q5 q6 q7 ns")
RET_V = Steps("q k pt0 pt1 pt23 k01 k23 ro u0 u1 on0 u2 u3 y0 lo0 on1 u4 u5 y1 lo1 on2 u6 u7 y2 lo2 on3 "
              "os ossq rs osn ys2 yh2 yl2 y3 ys yh lo3 yl")
RET_A = Steps("v0 v1 v2 v3 vs o0 sq0 o1 sq1 o2 sq2 o3 sq3 s0 s1 root "
              "g0 g1 g2 g3 silu0 hi0 g4 g5 silu1 hi1 g6 g7 silu2 hi2 rs silu3 hi3")
RET_P = Steps("sum0 sum1 sum2 sum3")
RET_UNITS, RET_SLOTS = 20, 8
RET_SLOT_DONE = [0, 2, 4, 6, 8, 10, 12, 16, 20]


GH, GG, GC, LV = 8, 4, 4, 6
GDN_SLOTS, GDN_UNITS = 10, 24
GDN_SLOT_DONE = [0, 2, 4, 6, 8, 10, 12, 14, 16, 20, 24]
TAPS = 4
U_LEN = TAPS - 1 + SEQ + TAPS * DEC
C_LEN = U_LEN - (TAPS - 1)
TAIL = U_LEN - SEQ
FFN_WORDS = (2 + 2 * FT) * NTOK
GDN_WORDS = 24560


def pairs(before, level, late, samples=None, early={}):
    out = []
    for p in range(2):
        both = (2 * p, 2 * p + 1)
        for group in before:
            out += [f"{n}.{c}" for c in both for n in group.split()]
        for l in range(1, LV + 1):
            for group in level:
                for c in both:
                    out += [f"{n}{l}.{c}" for n in group.split() if not (l == LV and n in ("b", "z"))]
                    if group == "a b" and l in early and c % 2 == 0:
                        out += [f"os{GC * p + b}" for b in early[l]]
            if samples and l in samples:
                out += [f"{n}{p}" for n in samples[l][0].split()]
                out += [f"{n}{GC * p + b}" for b in samples[l][1] for n in samples[l][2].split()]
        for group in late:
            out += [f"{n}.{c}" for c in both for n in group.split()]
    return " ".join(out)


def each(n, *names):
    return " ".join(f"{m}{i}" for i in range(n) for m in names)


PRE_T = Steps("cw ba tb bcol blast smp")
PRE_V = Steps("wg cw bf ba y m d di z w p0 p1 p2 p3 p4 p5 p6 l r sp a bcol cdl kd beb sma smb eab")
PRE_A = Steps("e na beta ebc cd kd ea")
TURN_AFTER = {n: n - 1 for n in range(1, 13)}
LENGTH_AFTER = {n: n - 2 for n in range(2, 10)}
SPREAD_AFTER = {12: [0], 13: [1, 2, 3], 14: [4, 5, 6, 7]}
GDN_T = Steps(" ".join([
    "ct", " ".join((f"cs{TURN_AFTER[n]} " if n in TURN_AFTER else "") + (f"ln{LENGTH_AFTER[n]} " if n in LENGTH_AFTER else "")
                   + " ".join(f"bc{m}" for m in SPREAD_AFTER.get(n, [])) for n in range(16)),
    pairs(["br kt vt kk", "qk mt"], ["t", "a b"], ["u wk", "w o s"],
          early={3: (0,), 5: (2,)}, samples={1: ("r", (), ""), 2: ("", (0, 1), "wr"), 3: ("", (1,), "os"), 4: ("", (2, 3), "wr"), 5: ("", (3,), "os")}),
    each(4, "nn"), each(4, "nb")]))
GDN_V = Steps(" ".join([
    "uz s0", each(11, "ux", "ca", "cb", "cc", "cd"), "ri ux11 ca11 cb11 cc11 cd11", each(8, "dq"),
    pairs(["aut", "dd kb kd vb n2", "L l0 m0", "pt qd"], ["a b"], ["W S"],
          {1: ("wa wb wc", (0, 1), "dg"), 2: ("", (0, 1), "kw sn"), 3: ("", (0, 1, 2, 3), "oz"), 4: ("", (2, 3), "kw sn"),
           5: ("", (2, 3), "oz")}).replace("oz2 oz3", "dg2 dg3", 1).replace("oz6 oz7", "dg6 dg7", 1),
    "rn y0 yz0 y1 yz1 lo0 y2 yz2 lo1 y3 yz3 lo2 lo3"]))
GDN_A = Steps(" ".join([
    "ctc", each(4, "si", "sq"), "si4 cse0 sq4 si5 sq5 si6 sq6 si7 sq7 si8 cse1 si9 rt si10 si11 cse2",
    pairs(["eb d1", "d2", "mt"], ["z", "t"], ["u wk", "oc"]),
    "sz", each(4, "nsq"), "nrt", each(4, "hi")]))
GDN_P = Steps(" ".join([
    pairs(["n1"], ["l"], ["s2"], {2: ("", (0, 1), "se"), 4: ("", (2, 3), "se")})]))


class Phase:

    def __init__(self, kind, slots, units, cols, norm, index):
        self.per_slot, self.per_unit = max(slots, units) // slots, max(slots, units) // units
        self.kind, self.slots, self.units, self.cols, self.norm, self.index = kind, slots, units, cols, norm, index

    def slot_done(self, k):
        return self.part0 + self.per_slot * (k - self.slot0 + 1)

    def unit_done(self, u):
        return self.part0 + self.per_unit * (u - self.unit0 + 1)


def plan():
    phases = [
        Phase("gate_up", FT, 2 * FT, 16 * P, 0, 0),
        Phase("down", 2 * KT, KT, 11 * P, 1, 0),
        Phase("ret", RET_SLOTS * RH, RET_UNITS * RH, 16 * P, 2, 0),
        Phase("gate_up", FT, 2 * FT, 16 * P, 2, 1),
        Phase("down", 2 * KT, KT, 11 * P, 3, 1),
        Phase("gate_up", FT, 2 * FT, 16 * P, 3, 2),
        Phase("down", 2 * KT, KT, 11 * P, 4, 2),
        Phase("gdn", GDN_SLOTS * 2, GDN_UNITS * 2, 16 * P, 5, 0),
        Phase("gate_up", FT, 2 * FT, 16 * P, 5, 3),
        Phase("down", 2 * KT, KT, 11 * P, 6, 3),
    ]
    slot, unit, part = 0, KT, KT
    for n, ph in enumerate(phases):
        ph.slot0, ph.unit0, ph.part0 = slot, unit, part
        slot, unit = slot + ph.slots, unit + ph.units
        part += max(ph.slots, ph.units)
        ph.next_cols = phases[n + 1].cols if n + 1 < len(phases) else 0
    return phases


def rolled(eng, n, body, peel_first=False):
    start = 0
    if peel_first:
        body(0, n == 1)
        start = 1
    if n - 1 > start:
        with eng.Fori(start, n - 1) as i:
            body(i, False)
    if n - 1 >= start:
        body(n - 1, True)


def build(nc, a, outs):
    with ExitStack() as ctx:
        def sb(name, shape, dt=F32, stack=ctx):
            return stack.enter_context(nc.sbuf_tensor(name, shape, dt))

        def sem(name):
            return ctx.enter_context(nc.semaphore(name))

        x = sb("x", [P, KT, NTOK])
        xh = sb("xh", [P, KT, NTOK], F32R)
        xl = sb("xl", [P, KT, NTOK], F32R)
        raw = sb("raw", [P, 2, SLOT])
        wh = sb("wh", [P, 2, SLOT], F32R)
        wl = sb("wl", [P, 2, SLOT], F32R)
        ident = sb("ident", [P, P])
        ones = sb("ones", [P, P])
        gains = sb("gains", [P, 56])
        gain_rows = sb("gain_rows", [56, P])
        eps = sb("eps", [P, 1])
        ssq = sb("ssq", [P, NTOK])
        sq = sb("sq", [P, 2, NTOK])
        rinv = sb("rinv", [P, NTOK])
        ps = ctx.enter_context(nc.psum_tensor("ps", [P, 8, 512], F32))

        def pair(u):
            return ps[:, 2 * (u % 2):2 * (u % 2) + 2, 0:HALF]

        def halves(ap):
            return ap.rearrange("p (h t) -> p h t", h=2)

        w_landed = [sem("w_landed0"), sem("w_landed1")]
        w_high = sem("w_high")
        w_low = sem("w_low")
        parts_done = sem("parts_done")
        acc_free = sem("acc_free")
        x_high = sem("x_high")
        x_sq = sem("x_sq")
        x_low = sem("x_low")
        x_ssq = sem("x_ssq")
        ssq_sum = sem("ssq_sum")
        ssq_root = sem("ssq_root")
        ssq_inv = sem("ssq_inv")
        consts = sem("consts")
        ones_set = sem("ones_set")
        x_landed = sem("x_landed")
        gains_turned = sem("gains_turned")
        gains_ready = sem("gains_ready")
        gate_ready = sem("gate_ready")
        h_ready = sem("h_ready")
        h_high = sem("h_high")
        h_low = sem("h_low")
        act_held, pool_held = sem("act_held"), sem("pool_held")
        ret_consts = sem("ret_consts")
        ret_tables = sem("ret_tables")
        ret_t, ret_v, ret_a, ret_p = sem("ret_t"), sem("ret_v"), sem("ret_a"), sem("ret_p")
        head_landed = sem("head_landed")
        s_landed = [sem(f"s_landed{n}") for n in range(RING)]
        s_stored = [sem(f"s_stored{n}") for n in range(RING)]
        s_out_stored = sem("s_out_stored")
        pre_landed = sem("pre_landed")
        pre_t, pre_v, pre_a = sem("pre_t"), sem("pre_v"), sem("pre_a")
        gdn_t, gdn_v, gdn_a, gdn_p = sem("gdn_t"), sem("gdn_v"), sem("gdn_a"), sem("gdn_p")
        c_landed = sem("c_landed")
        c_stored = sem("c_stored")
        g_landed = [sem(f"g_landed{n}") for n in range(RING)]
        g_stored = [sem(f"g_stored{n}") for n in range(RING)]
        gs_stored = sem("gs_stored")
        eps_set = sem("eps_set")
        softplus_ready = sem("softplus_ready")
        y_ready, y_turned, y_out = sem("y_ready"), sem("y_turned"), sem("y_out")
        y_stored = sem("y_stored")

        phases = plan()

        def heads(ap):
            return ap.rearrange("p (h o) -> p h o", o=1).broadcast_to([P, ap.shape[1], P])

        def every(ap):
            return ap.rearrange("p (o n) -> p o n", o=1).broadcast_to([P, GG, P])

        def blocks(ap, l, odd):
            return ap.rearrange("p (m two j) -> p m two j", two=2, j=2 ** l)[:, :, odd, :]

        def flat(t):
            return t[:].rearrange("p h n -> p (h n)")

        def gather(n):
            return one_col[:, GH - 1 - n:2 * GH - 1 - n]

        def spread(n):
            return ident[0:GH, n:n + 1].broadcast_to([GH, P])

        def by_head(bank, n=P):
            return ps[:, bank, 0:GG * n].rearrange("p (h n) -> p h n", h=GG)

        with ExitStack() as st:
            xin = sb("xin", [P, 4, D], stack=st)
            xin_s = sb("xin_s", [DEC, D], stack=st)
        with ExitStack() as st:
            rq = sb("rq", [P, 2, NTOK], stack=st)
            rk = sb("rk", [P, 2, NTOK], stack=st)
            rv = sb("rv", [P, 4, NTOK], stack=st)
            rg = sb("rg", [P, 4, NTOK], stack=st)
            ro = sb("ro", [P, 4, SEQ], stack=st)
            vtok = sb("vtok", [P, 4, RV], stack=st)
            vtok_s = sb("vtok_s", [DEC, RV], stack=st)
            head_c = sb("head_c", [P, SEQ + 5], stack=st)
            cosr = sb("cosr", [P, NTOK], stack=st)
            sinr = sb("sinr", [P, NTOK], stack=st)
            rot = sb("rot", [P, 2, NTOK], stack=st)
            osq = rot[:, :, 0:SEQ]
            osum = sb("osum", [P, SEQ], stack=st)
            rinv_o = sb("rinv_o", [P, SEQ], stack=st)
            s_out = sb("s_out", [P, 2, RV], stack=st)
            s_ring = sb("s_ring", [P, RING, 2, RV], stack=st)
            sel = sb("sel", [DEC, DEC, P], stack=st)
            o_s = sb("o_s", [P, 4, DEC], stack=st)
            osq_s = sb("osq_s", [P, 4, DEC], stack=st)
            rinv_s = sb("rinv_s", [P, DEC], stack=st)
            yh = sb("yh", [P, 4, NTOK], F32R, stack=st)
            with ExitStack() as scores:
                ktok = sb("ktok", [P, 4, RK], stack=scores)
                pt = sb("pt", [P, 1280], stack=scores)
            yl = sb("yl", [P, 4, NTOK], F32R, stack=st)
        with ExitStack() as st:
            with ExitStack() as sc:
                sb("gdn_below", [P, GDN_WORDS], stack=sc)
                gcon = sb("gcon", [P, 3 * P + 7 * P + DEC], stack=sc)
                a_log = sb("a_log", [P, GH], stack=sc)
                dt_b = sb("dt_b", [P, GH], stack=sc)
                norm_w = sb("norm_w", [P, 1], stack=sc)
                eps_q = sb("eps_q", [GH, 1], stack=sc)
                scale_q = sb("scale_q", [GH, 1], stack=sc)
                one_col = sb("one_col", [P, 2 * GH - 1], stack=sc)
            with ExitStack() as sc:
                sb("ffn_below", [P, FFN_WORDS], stack=sc)
                wba = sb("wba", [P, KT, 2 * GH], stack=sc)
                conv_rows = sb("conv_rows", [TAPS * 3 * GH, P], stack=sc)
            gq = sb("gq", [P, GG, NTOK], stack=st)
            gk = sb("gk", [P, GG, NTOK], stack=st)
            gv = sb("gv", [P, GG, NTOK], stack=st)
            gz = sb("gz", [P, GG, NTOK], stack=st)
            gs = sb("gs", [P, GG, P], stack=st)
            gs2 = sb("gs2", [P, GG, P], stack=st)
            g_ring = sb("g_ring", [P, RING, GG, P], stack=st)
            conv_w = sb("conv_w", [P, TAPS, 3 * GH], stack=st)
            small = sb("small", [P, 7, 5, GH], stack=st)
            ba = sb("ba", [P, 5, 2 * GH], stack=st)
            bcol = sb("bcol", [P, 4, GH], stack=st)
            ebcol = sb("ebcol", [P, 4, GH], stack=st)
            kdcol = sb("kdcol", [P, 4, GH], stack=st)
            cdrep = sb("cdrep", [P, 4, GH], stack=st)
            bebcol = sb("bebcol", [P, 4, GH], stack=st)
            sm = sb("sm", [P, 2, GH, DEC], stack=st)
            eab = sb("eab", [P, 2, GH, DEC], stack=st)
            with ExitStack() as sc:
                ba_rows = sb("ba_rows", [2 * GH, NTOK], stack=sc)
                roots = sb("roots", [GH, NTOK], stack=sc)
                c_old = sb("c_old", [P, 12 * 3 * DEC], stack=sc)
                uu = sb("uu", [P, 2, U_LEN], stack=sc)
                cv = sb("cv", [P, 2, C_LEN], stack=sc)
                c_in = sb("c_in", [DEC * 3, 3, GG * P], stack=sc)
                c_out = sb("c_out", [TAIL, 3, GG * P], stack=sc)
            with ExitStack() as sc:
                names = "d1 d2 eb kb kd vb m mt t1 la lb u".split()
                chain = [{n: sb(f"{n}_{x_}", [P, GG, P], stack=sc) for n in names} for x_ in range(2)]
                for ch in chain:
                    ch["dd"], ch["wk"] = ch["u"], ch["lb"]
            with ExitStack() as sc:
                gyh = sb("gyh", [P, GG, NTOK], F32R, stack=sc)
                gyl = sb("gyl", [P, GG, NTOK], F32R, stack=sc)
                gsq = sb("gsq", [P, 4, NTOK], stack=sc)
                roots_o = sb("roots_o", [GH, NTOK], stack=sc)
        wt = ssq[:, 0:GG * DEC].rearrange("p (h b) -> p h b", h=GG)
        dg = [sq[:, n, 0:GG * P].rearrange("p (h n) -> p h n", h=GG) for n in range(2)]
        ut, negup, biglo = (gcon[:, n * P:(n + 1) * P] for n in range(3))
        levels = [gcon[:, (3 + n) * P:(4 + n) * P] for n in range(7)]
        smask = gcon[:, 10 * P:10 * P + DEC]
        with ExitStack() as st:
            yy = sb("yy", [P, KT, NTOK], stack=st)
            y_tok = sb("y_tok", [P, 4, D], stack=st)
            y_new = sb("y_new", [DEC, D], stack=st)
        with ExitStack() as st:
            gate = sb("gate", [P, NTOK], stack=st)
            up = sb("up", [P, NTOK], stack=st)
            hh = sb("hh", [P, FT, NTOK], F32R, stack=st)
            hl = sb("hl", [P, FT, NTOK], F32R, stack=st)

        block = ctx.enter_context(nc.Block())

        @block.sync
        def _(sp):
            sp.dma_start(ident[:], a["c_ident"]).then_inc(consts, 16)
            sp.dma_start(gain_rows[0:48, :], a["norm_g"].rearrange("l n (t p) -> (l n t) p", p=P)).then_inc(consts, 16)
            sp.dma_start(gain_rows[48:56, :], a["final_g"].rearrange("(t p) -> t p", p=P)).then_inc(consts, 16)
            sp.dma_start(xin[:], a["x_prompt"].rearrange("b (c p) d -> p (b c) d", p=P)).then_inc(x_landed, 16)
            sp.dma_start(xin_s[:], a["x_sample"].rearrange("b s d -> (b s) d")).then_inc(x_landed, 16)

            def tiles(s, t0, n, cols=P):
                return raw[:, s, t0 * P:t0 * P + n * cols].rearrange("p (t c) -> p t c", c=cols)

            def ret_body(ph, h):
                wi = a["ret_w_in"][0].rearrange("(t p) n -> p t n", p=P)
                wo = a["ret_w_out"][0].rearrange("(h t p) n -> h p t n", p=P, t=4)
                starts = [h * RK, RH * RK + h * RK, 2 * RH * RK + h * RV, 2 * RH * RK + h * RV + 2 * P,
                          2 * RH * RK + RH * RV + h * RV, 2 * RH * RK + RH * RV + h * RV + 2 * P]
                for j in range(RET_SLOTS):
                    s, k = j % 2, ph.slot0 + RET_SLOTS * h + j
                    sp.wait_ge(w_low, k - 1)
                    if j < 6:
                        for t in (0, 4):
                            sp.dma_start(tiles(s, 2 * t, 4, 2 * P), wi[:, t:t + 4, bass.ds(starts[j], 2 * P)]).then_inc(w_landed[s], 16)
                    else:
                        for t in (0, 2):
                            src = wo[bass.ds(h, 1), :, t:t + 2, (j - 6) * 4 * P:(j - 5) * 4 * P]
                            sp.dma_start(tiles(s, 4 * t, 2, 4 * P), src.rearrange("h p t n -> p (h t) n")).then_inc(w_landed[s], 16)

            def gdn_body(ph, g):
                wi = a["gdn_w_in"][0].rearrange("(t p) n -> p t n", p=P)
                wo = a["gdn_w_out"][0].rearrange("(g t p) n -> g p t n", p=P, t=GG)
                for j in range(GDN_SLOTS):
                    s, k = j % 2, ph.slot0 + GDN_SLOTS * g + j
                    sp.wait_ge(w_low, k - 1)
                    if j < 8:
                        c = (j // 2) * D + g * GG * P + (j % 2) * 2 * P
                        for t in (0, 4):
                            sp.dma_start(tiles(s, 2 * t, 4, 2 * P), wi[:, t:t + 4, c:c + 2 * P]).then_inc(w_landed[s], 16)
                    else:
                        for t in (0, 2):
                            sp.dma_start(tiles(s, 4 * t, 2, 4 * P), wo[g, :, t:t + 2, (j - 8) * 4 * P:(j - 7) * 4 * P])\
                                .then_inc(w_landed[s], 16)

            for ph in phases:
                if ph.kind == "gdn":
                    for g in range(2):
                        gdn_body(ph, g)
                    continue
                if ph.kind == "ret":
                    with sp.Fori(0, RH) as h:
                        ret_body(ph, h)
                    continue

                def body(i, last):
                    for s in range(2):
                        k = ph.slot0 + 2 * i + s
                        if not isinstance(k, int) or k >= 2:
                            sp.wait_ge(w_low, k - 1)
                        if ph.kind == "gate_up":
                            w = a["ffn_gu"][ph.index // 2, ph.index % 2].rearrange("(t p) n -> p t n", p=P)
                            c = (2 * i + s) * P
                            sp.dma_start(tiles(s, 0, KT), w[:, :, bass.ds(c, P)]).then_inc(w_landed[s], 16)
                            sp.dma_start(tiles(s, KT, KT), w[:, :, bass.ds(c + FF, P)]).then_inc(w_landed[s], 16)
                        if ph.kind == "down":
                            w = a["ffn_down"][ph.index // 2, ph.index % 2].rearrange("(s t p) n -> p s t n", s=2, p=P)
                            sp.dma_start(tiles(s, 0, 6), w[:, s, 0:6, bass.ds(i * P, P)]).then_inc(w_landed[s], 16)
                            sp.dma_start(tiles(s, 6, 5), w[:, s, 6:11, bass.ds(i * P, P)]).then_inc(w_landed[s], 16)
                rolled(sp, ph.slots // 2, body, ph.slot0 == 0)

            for t0, t1 in Y_PARTS:
                sp.wait_ge(y_out, 2 * t1)
                for c in range(4):
                    sp.dma_start(outs[0][0, c * P:(c + 1) * P, t0 * P:t1 * P], y_tok[:, c, t0 * P:t1 * P]).then_inc(y_stored, 16)
            sp.dma_start(outs[1].rearrange("b s d -> (b s) d"), y_new[:]).then_inc(y_stored, 16)
            sp.wait_ge(y_stored, 16 * (4 * len(Y_PARTS) + 1))

        @block.gpsimd
        def _(pool):
            nc.gpsimd.memset(ones[:], 1.0).then_inc(ones_set, 1)
            nc.gpsimd.memset(eps[:], EPS).then_inc(ones_set, 1)

            def sum_squares(m):
                if m:
                    pool.wait_ge(ssq_sum, m)
                for t in range(KT):
                    pool.wait_ge(x_sq, KT * m + t + 1)
                    if t == 0:
                        nc.gpsimd.tensor_copy(ssq[:], sq[:, t % 2, :]).then_inc(x_ssq, 1)
                    else:
                        pool.wait_ge(x_ssq, KT * m + t)
                        nc.gpsimd.tensor_tensor(ssq[:], ssq[:], sq[:, t % 2, :], ALU.add).then_inc(x_ssq, 1)

            ret_in = a["state_ret"][0].rearrange("b h (p t) e -> b h p t e", t=2)
            ret_new = outs[5][0].rearrange("b h (p t) e -> b h p t e", t=2)
            ret_last = outs[2][0, 0].rearrange("h (p t) e -> h p t e", t=2)

            def ret_body(ph, h):
                def state(dram, b):
                    return dram[b, bass.ds(h, 1)].rearrange("h p t e -> p (h t) e")

                first = isinstance(h, int) and h == 0
                if not first:
                    pool.wait_ge(ret_v, RET_V("k23", h - 1))
                    pool.wait_ge(ret_a, RET_A("g7", h - 1))
                pool.sem_inc(pool_held, 1)
                pool.dma_start(head_c[:], a["c_head"][bass.ds(h, 1)].rearrange("h p n -> (h p) n")).then_inc(head_landed, 16)
                for b in range(RING):
                    if not first:
                        pool.wait_ge(s_stored[b], 32 * h)
                        pool.wait_ge(ret_t, RET_T(f"q{b + RING}", h - 1))
                    pool.sem_inc(pool_held, 1)
                    pool.dma_start(s_ring[:, b], state(ret_in, b)).then_inc(s_landed[b], 16)
                for e in range(4):
                    pool.wait_ge(ret_a, RET_A(f"sq{e}", h))
                    if e == 0:
                        if not first:
                            pool.wait_ge(ret_t, RET_T("n", h - 1))
                        pool.sem_inc(pool_held, 1)
                        nc.gpsimd.tensor_copy(osum[:], osq[:, 0, :]).then_inc(ret_p, RET_P.did("sum0"))
                    else:
                        pool.wait_ge(ret_p, RET_P(f"sum{e - 1}", h))
                        nc.gpsimd.tensor_tensor(osum[:], osum[:], osq[:, e % 2, :], ALU.add).then_inc(ret_p, RET_P.did(f"sum{e}"))
                pool.wait_ge(ret_a, RET_A("s1", h))
                pool.sem_inc(pool_held, 1)
                pool.dma_start(ret_last[bass.ds(h, 1)].rearrange("h p t e -> p (h t) e"), s_out[:]).then_inc(s_out_stored, 16)
                for b in range(DEC):
                    pool.wait_ge(ret_v, RET_V(f"u{b}", h))
                    pool.sem_inc(pool_held, 1)
                    pool.dma_start(state(ret_new, b), s_ring[:, b % RING]).then_inc(s_stored[b % RING], 16)
                    c = b - 1
                    if c >= 0 and c + RING < DEC:
                        pool.wait_ge(s_stored[c], 32 * h + 16)
                        pool.wait_ge(ret_t, RET_T(f"q{c}", h))
                        pool.sem_inc(pool_held, 1)
                        pool.dma_start(s_ring[:, c], state(ret_in, c + RING)).then_inc(s_landed[c], 16)

            def gdn_consts():
                def row(src, n):
                    return src.rearrange("(o n) -> o n", o=1).broadcast_to([P, n])
                for dst, src in ((gcon[:], a["c_gdn"]), (wba[:], a["gdn_w_in"][0].rearrange("(t p) n -> p t n", p=P)[:, :, 4 * D:4 * D + 16]),
                                 (conv_rows[:], a["gdn_conv_w"][0].rearrange("j (t p) -> (j t) p", p=P)),
                                 (a_log[:], row(a["gdn_a_log"][0], GH)), (dt_b[:], row(a["gdn_dt_bias"][0], GH)),
                                 (norm_w[:], a["gdn_norm_w"].rearrange("o (p n) -> (o p) n", n=1))):
                    pool.dma_start(dst, src).then_inc(pre_landed, 16)
                nc.gpsimd.memset(one_col[:], 0.0).then_inc(eps_set, 1)
                nc.gpsimd.memset(scale_q[:], 1.0).then_inc(eps_set, 1)
                nc.gpsimd.memset(eps_q[:], EPS).then_inc(eps_set, 1)
                pool.wait_ge(eps_set, 3)
                nc.gpsimd.memset(one_col[:, GH - 1:GH], 1.0).then_inc(eps_set, 1)
                nc.gpsimd.memset(scale_q[0:GG, :], float(P)).then_inc(eps_set, 1)
                nc.gpsimd.memset(eps_q[0:GG, :], EPS * P).then_inc(eps_set, 1)

            def gdn_body(ph, g):
                T, V, A, Q = GDN_T, GDN_V, GDN_A, GDN_P
                h0 = g * GG

                def state(dram, b):
                    return dram[0, b, h0:h0 + GG].rearrange("h p e -> p h e")

                pool.wait_ge(parts_done, ph.part0 + GDN_UNITS * g)
                c_src = a["state_gdn_conv"][0].rearrange("b j (y n) -> (b j) y n", y=3)[:, :, h0 * P:(h0 + GG) * P]
                pool.dma_start(c_in[:], c_src).then_inc(c_landed, 16)
                for b in range(RING):
                    if g:
                        pool.wait_ge(g_stored[b], 32 * g)
                    pool.dma_start(g_ring[:, b], state(a["state_gdn"], b)).then_inc(g_landed[b], 16)
                pool.wait_ge(gdn_a, A("cse2", g))
                cols = lambda o: o.rearrange("j (y n) -> j y n", y=3)[:, :, h0 * P:(h0 + GG) * P]
                pool.dma_start(cols(outs[4][0, 0]), c_out[0:3]).then_inc(c_stored, 16)
                for b in range(DEC):
                    pool.dma_start(cols(outs[7][0, b]), c_out[4 + 4 * b:7 + 4 * b]).then_inc(c_stored, 16)
                add = lambda o, i0, i1, op: nc.gpsimd.tensor_tensor(o, i0, i1, op)
                for p in range(2):
                    both = [(2 * p + x_, chain[x_]) for x_ in range(2)]
                    for c, ch in both:
                        pool.wait_ge(gdn_v, V(f"dd.{c}", g))
                        if p == 0:
                            pool.wait_ge(c_stored, 144 * (g + 1))
                        add(ch["d1"][:], ch["dd"][:], every(biglo), ALU.add).then_inc(gdn_p, Q.did(f"n1.{c}"))
                    for l in range(1, LV + 1):
                        for c, ch in both:
                            if l < 3:
                                pool.wait_ge(gdn_v, V(f"m0.{c}" if l == 2 else f"L.{c}", g))
                            if l > 2:
                                pool.wait_ge(gdn_t, T(f"t{l - 2}.{c}", g))
                            add(ch["lb" if l % 2 else "la"][:], ch["d1"][:], every(levels[l]), ALU.mult).then_inc(gdn_p, Q.did(f"l{l}.{c}"))
                        if l in (2, 4):
                            for b in range(GC * p + l - 2, GC * p + l):
                                pool.wait_ge(g_landed[b % RING], 32 * g + 16 * p + 16)
                                pool.wait_ge(gdn_t, T(f"r{p}", g))
                                mine = g_ring[:, b % RING]
                                add(mine, mine, heads(eab[:, 0, h0:h0 + GG, b]), ALU.mult).then_inc(gdn_p, Q.did(f"se{b}"))
                    for c, ch in both:
                        pool.wait_ge(gdn_v, V("s0" if c == 0 else f"S.{c - 1}", g))
                        add(gs2[:], gs[:], heads(cdrep[:, c, h0:h0 + GG]), ALU.mult).then_inc(gdn_p, Q.did(f"s2.{c}"))
                    for b in range(GC * p, GC * p + GC):
                        pool.wait_ge(gdn_v, V(f"sn{b}", g))
                        pool.dma_start(state(outs[6], b), g_ring[:, b % RING]).then_inc(g_stored[b % RING], 16)
                    if p == 0:
                        for b in range(RING):
                            pool.wait_ge(g_stored[b], 32 * g + 16)
                            pool.wait_ge(gdn_t, T(f"os{b}", g))
                            pool.dma_start(g_ring[:, b], state(a["state_gdn"], b + RING)).then_inc(g_landed[b], 16)
                pool.wait_ge(gdn_v, V("S.3", g))
                pool.dma_start(outs[3][0, 0, h0:h0 + GG].rearrange("h p e -> p h e"), gs[:]).then_inc(gs_stored, 16)

            sum_squares(0)
            for ph in phases:
                if ph.kind == "gdn":
                    for g in range(2):
                        gdn_body(ph, g)
                    sum_squares(ph.norm)
                    for b in range(RING):
                        pool.wait_ge(g_stored[b], 64)
                    pool.wait_ge(gs_stored, 32)
                if ph.kind == "down":
                    sum_squares(ph.norm)
                    if ph.index == 1:
                        gdn_consts()
                if ph.kind == "ret":
                    pool.dma_start(sel[:], a["c_sel"]).then_inc(ret_consts, 16)
                    pool.dma_start(cosr[:], a["c_cos"]).then_inc(ret_consts, 16)
                    pool.dma_start(sinr[:], a["c_sin"]).then_inc(ret_consts, 16)
                    ret_body(ph, 0)
                    with pool.Fori(1, RH) as h:
                        ret_body(ph, h)
                    sum_squares(ph.norm)
                    for b in range(RING):
                        pool.wait_ge(s_stored[b], 32 * RH)
                    pool.wait_ge(s_out_stored, 16 * RH)

        @block.tensor
        def _(pe):
            pe.wait_ge(consts, 48)
            nc.tensor.transpose(ps[:, 7, 0:56], gain_rows[:, :], ident[0:56, 0:56]).then_inc(gains_turned, 1)
            pe.wait_ge(x_landed, 32)
            for t in range(KT):
                if t >= 2:
                    pe.wait_ge(acc_free, t - 1)
                b = 4 + 2 * (t % 2)
                if t == 1:
                    pe.wait_ge(gains_ready, 1)
                for c in range(4):
                    nc.tensor.transpose(ps[:, b, c * P:(c + 1) * P], xin[:, c, t * P:(t + 1) * P], ident[:])
                nc.tensor.transpose(ps[:, b + 1, 0:DEC], xin_s[:, t * P:(t + 1) * P],
                                    ident[0:DEC, 0:DEC]).then_inc(parts_done, 1)

            def products(q, s, n_tiles, col0, step, high, low, kt0, first, last_):
                for t in range(n_tiles):
                    c = col0 + t * step
                    hi_w, lo_w = wh[:, s, c:c + P], wl[:, s, c:c + P]
                    begin, end = first and t == 0, last_ and t == n_tiles - 1
                    for w_, v, b_, e_ in ((hi_w, high, begin, False), (hi_w, low, False, False), (lo_w, high, False, end)):
                        for h in range(2):
                            m_ = nc.tensor.matmul(ps[:, 2 * q + h, 0:HALF], w_, v[:, kt0 + t, h * HALF:(h + 1) * HALF],
                                                  start=b_, stop=e_)
                return m_

            def norm_sum(m):
                pe.wait_ge(x_ssq, KT * (m + 1))
                if m == 0:
                    pe.wait_ge(ones_set, 2)
                    pe.wait_ge(gains_ready, 1)
                for h in range(2):
                    m_ = nc.tensor.matmul(ps[:, 6 + h, 0:HALF], ones[:], ssq[:, h * HALF:(h + 1) * HALF],
                                          start=True, stop=True)
                m_.then_inc(ssq_sum, 1)

            def ret_body(ph, h):
                def slot(j):
                    pe.wait_ge(w_low, ph.slot0 + RET_SLOTS * h + j + 1)

                first = isinstance(h, int) and h == 0
                for j in range(4):
                    if first and j == 0:
                        first_units(ph, True)
                        continue
                    slot(j)
                    for g in range(2):
                        pe.wait_ge(acc_free, ph.unit0 + RET_UNITS * h + 2 * j + g - 1)
                        in_products(g, j % 2, j < 2, g).then_inc(parts_done, 1)
                pe.wait_ge(ret_v, RET_V("k", h))
                if first:
                    pe.wait_ge(ssq_root, ph.norm)
                    pe.wait_ge(ret_consts, 48)
                off = [0, 512, 896, 1152]
                for jb in range(4):
                    w = SEQ - P * jb
                    o = ps[:, 4 + min(jb, 2), 0:w] if jb < 3 else ps[:, 6, 256:384]
                    for t in range(2):
                        m_ = nc.tensor.matmul(o, rk[:, t, jb * P:(jb + 1) * P], rq[:, t, jb * P:SEQ], start=t == 0, stop=t == 1)
                    if jb != 2:
                        m_.then_inc(ret_t, RET_T.did(["p0", "p1", "", "p23"][jb]))

                def turn_k(c, name):
                    for n in range(2):
                        for t in range(2):
                            m_ = nc.tensor.transpose(ps[:, 7, (2 * n + t) * P:(2 * n + t + 1) * P],
                                                     rk[:, t, (c + n) * P:(c + n + 1) * P], ident[:])
                    m_.then_inc(ret_t, RET_T.did(name))

                def turn_v(c):
                    for e in range(4):
                        m_ = nc.tensor.transpose(ps[:, 4 + c, e * P:(e + 1) * P], rv[:, e, c * P:(c + 1) * P], ident[:])
                    m_.then_inc(ret_t, RET_T.did(f"v{c}"))

                turn_k(0, "k01")
                for c in range(3):
                    pe.wait_ge(ret_v, RET_V(["pt0", "pt1", "pt23"][c], h))
                    if c == 0:
                        pe.wait_ge(acc_free, ph.unit0 + RET_UNITS * h + 8)
                    turn_v(c)
                pe.wait_ge(ret_v, RET_V("k01", h))
                turn_k(2, "k23")
                pe.wait_ge(ret_v, RET_V("k23", h))
                turn_v(3)
                pe.wait_ge(ret_a, RET_A("v3", h))
                for e in range(4):
                    m_ = nc.tensor.transpose(ps[0:DEC, 7, e * P:(e + 1) * P], rv[:, e, SEQ:NTOK], ident[:])
                m_.then_inc(ret_t, RET_T.did("vs"))
                pe.wait_ge(ret_a, RET_A("vs", h))
                for e in range(4):
                    for jb in range(4):
                        m_ = nc.tensor.matmul(ps[:, 4 + e, jb * P:SEQ], vtok[:, jb, e * P:(e + 1) * P],
                                              pt[:, off[jb]:off[jb] + SEQ - P * jb], start=jb == 0, stop=jb == 3)
                    m_.then_inc(ret_t, RET_T.did(f"o{e}"))
                for t in range(2):
                    pe.wait_ge(ret_a, RET_A(f"sq{t}", h))
                    for jb in range(4):
                        m_ = nc.tensor.matmul(ps[:, 4 + t, :], ktok[:, jb, t * P:(t + 1) * P], vtok[:, jb, :],
                                              start=jb == 0, stop=jb == 3)
                    m_.then_inc(ret_t, RET_T.did(f"s{t}"))
                pe.wait_ge(ret_p, RET_P("sum3", h))
                pe.wait_ge(ret_a, RET_A("sq2", h))
                nc.tensor.matmul(ps[:, 6, :], ones[:], osum[:], start=True, stop=True).then_inc(ret_t, RET_T.did("n"))
                def value(b):
                    if b < 2:
                        pe.wait_ge(ret_a, RET_A(f"s{b}", h))
                    else:
                        pe.wait_ge(ret_v, RET_V(f"u{b - 2}", h))
                    nc.tensor.matmul(ps[:, 4 + b % 2, :], sel[:, b, :], vtok_s[:], start=True, stop=True)\
                        .then_inc(ret_t, RET_T.did(f"b{b}"))

                def query(b):
                    if b == 0:
                        pe.wait_ge(ret_a, RET_A("sq3", h))
                    pe.wait_ge(ret_v, RET_V(f"u{b}", h))
                    for e in range(4):
                        for t in range(2):
                            m_ = nc.tensor.matmul(ps[:, 7, e * DEC + b:e * DEC + b + 1],
                                                  s_ring[:, b % RING, t, e * P:(e + 1) * P],
                                                  rq[:, t, SEQ + b:SEQ + b + 1], start=t == 0, stop=t == 1)
                    m_.then_inc(ret_t, RET_T.did(f"q{b}"))

                value(0)
                value(1)
                for g in range(4):
                    if g % 2 == 0:
                        slot(4 + g // 2)
                    pe.wait_ge(acc_free, ph.unit0 + RET_UNITS * h + 8 + g - 1)
                    unit = (g % 2, (4 + g // 2) % 2, False, g % 2)
                    if g == 0:
                        in_products(*unit).then_inc(parts_done, 1)
                    elif g < 3:
                        in_products(*unit, range(0, 2))
                        query(2 * g - 2)
                        in_products(*unit, range(2, 5))
                        query(2 * g - 1)
                        in_products(*unit, range(5, KT)).then_inc(parts_done, 1)
                    else:
                        in_products(*unit, range(0, 2))
                        query(4)
                        in_products(*unit, range(2, 4))
                        query(5)
                        in_products(*unit, range(4, 5))
                        query(6)
                        in_products(*unit, range(5, 6))
                        query(7)
                        in_products(*unit, range(6, 7))
                        pe.wait_ge(ret_v, RET_V("ossq", h))
                        pe.wait_ge(ret_a, RET_A("root", h))
                        for e in range(4):
                            m_ = nc.tensor.matmul(ps[:, 6, 0:DEC], ones[:], osq_s[:, e, :], start=e == 0, stop=e == 3)
                        m_.then_inc(ret_t, RET_T.did("ns"))
                        in_products(*unit, range(7, KT)).then_inc(parts_done, 1)
                    if g < 3:
                        value(2 * g + 2)
                        value(2 * g + 3)
                slot(6)
                pe.wait_ge(ret_v, RET_V("yl2", h))
                for n in range(2):
                    pe.wait_ge(acc_free, ph.unit0 + RET_UNITS * h + 12 + n - 1)
                    products(n, 0, 3, n * P, 4 * P, yh, yl, 0, True, False)
                pe.wait_ge(ret_v, RET_V("yl", h))
                for n in range(KT):
                    if n < 2:
                        m_ = products(n, 0, 1, n * P + 3 * 4 * P, 4 * P, yh, yl, 3, False, True)
                    else:
                        if n == 4:
                            slot(7)
                        pe.wait_ge(acc_free, ph.unit0 + RET_UNITS * h + 12 + n - 1)
                        m_ = products(n % 2, n // 4, 4, (n % 4) * P, 4 * P, yh, yl, 0, True, True)
                    m_.then_inc(parts_done, 1)

            def first_units(ph, paired):
                pe.wait_ge(w_low, ph.slot0 + 1)
                for t in range(KT):
                    if t == 3:
                        norm_sum(ph.norm - 1)
                    pe.wait_ge(x_low, KT * (ph.norm - 1) + t + 1)
                    for g in range(2):
                        if t == 0:
                            pe.wait_ge(acc_free, ph.unit0 + g - 1)
                        m_ = in_products(g, 0, paired, g, range(t, t + 1))
                        if t == KT - 1:
                            m_.then_inc(parts_done, 1)

            def in_products(q, s, paired, g, steps=range(KT)):
                for t in steps:
                    c = 2 * P * t
                    cols = slice(c + g, c + 2 * P, 2) if paired else slice(c + g * P, c + (g + 1) * P)
                    hi_w, lo_w = wh[:, s, cols], wl[:, s, cols]
                    for n, (w_, v) in enumerate(((hi_w, xh), (hi_w, xl), (lo_w, xh))):
                        for h in range(2):
                            m_ = nc.tensor.matmul(ps[:, 2 * q + h, 0:HALF], w_, v[:, t, h * HALF:(h + 1) * HALF],
                                                  start=t == 0 and n == 0, stop=t == KT - 1 and n == 2)
                return m_

            def gdn_pre(ph):
                pe.wait_ge(pre_landed, 96)
                nc.tensor.transpose(ps[:, 4, 0:96], conv_rows[:, :], ident[0:96, 0:96]).then_inc(pre_t, PRE_T.did("cw"))
                pe.wait_ge(pre_v, PRE_V("cw", 0))
                for h in range(2):
                    for t in range(KT):
                        m_ = nc.tensor.matmul(ps[0:2 * GH, 4 + h, 0:HALF], wba[:, t, :], x[:, t, h * HALF:(h + 1) * HALF],
                                              start=t == 0, stop=t == KT - 1)
                m_.then_inc(pre_t, PRE_T.did("ba"))

            def gdn_pre_after(n):
                if n == 2:
                    pe.wait_ge(pre_v, PRE_V("bf", 0))
                    pe.wait_ge(gdn_a, GDN_A("ctc", 0))
                    for c, at_ in enumerate((0, P, 2 * P, 3 * P, NTOK - P)):
                        m_ = nc.tensor.transpose(ps[:, 6, c * 16:(c + 1) * 16], ba_rows[:, at_:at_ + P], ident[0:2 * GH, 0:2 * GH])
                    m_.then_inc(pre_t, PRE_T.did("tb"))
                if n == 5:
                    pe.wait_ge(pre_v, PRE_V("a", 0))
                    a_tok = small[:, 5, 0:4, :].rearrange("p c h -> p (c h)")
                    nc.tensor.matmul(ps[:, 6, 128:160], ut, a_tok, start=True, stop=True).then_inc(pre_t, PRE_T.did("bcol"))
                    nc.tensor.matmul(ps[:, 6, 160:192], ones[:], a_tok, start=True, stop=True).then_inc(pre_t, PRE_T.did("blast"))
                if n == 8:
                    pe.wait_ge(pre_v, PRE_V("smb", 0))
                    nc.tensor.matmul(ps[:, 6, 256:384], ones[:], sm[:].rearrange("p a h b -> p (a h b)"), start=True, stop=True)\
                        .then_inc(pre_t, PRE_T.did("smp"))

            def gdn_body(ph, g):
                T, V, A, Q = GDN_T, GDN_V, GDN_A, GDN_P
                h0 = g * GG

                def v(name):
                    pe.wait_ge(gdn_v, V(name, g))

                def act_(name):
                    pe.wait_ge(gdn_a, A(name, g))

                def did(m_, name):
                    m_.then_inc(gdn_t, T.did(name))

                def turn(n):
                    v(f"ux{n}")
                    if n in (4, 8):
                        act_(f"cse{n // 4 - 1}")
                    did(nc.tensor.transpose(ps[0:TAIL, 7, (n % 4) * P:(n % 4 + 1) * P], uu[:, n % 2, SEQ:U_LEN], ident[:]), f"cs{n}")

                def lengths(n):
                    act_(f"sq{n}")
                    if n == 0:
                        pe.wait_ge(eps_set, 6)
                        pe.wait_ge(pre_v, PRE_V("bf", 0))
                    for h in range(2):
                        m_ = nc.tensor.matmul(ps[0:GH, 4 + h, 0:HALF], gather(n), sq[:, n % 2, h * HALF:(h + 1) * HALF],
                                              start=n == 0, stop=n == 7)
                    did(m_, f"ln{n}")

                def spread_out(n):
                    if n == 0:
                        v("ri")
                    if n == 1:
                        act_("cse2")
                    if n >= 2:
                        v(f"dq{n - 2}")
                    for h in range(2):
                        m_ = nc.tensor.matmul(ps[:, 4 + 2 * (n % 2) + h, 0:HALF], spread(n), roots[:, h * HALF:(h + 1) * HALF],
                                              start=True, stop=True)
                    did(m_, f"bc{n}")

                if g == 0:
                    pe.wait_ge(ssq_root, ph.norm)
                pe.wait_ge(c_landed, 16 * (g + 1))
                if g:
                    pe.wait_ge(gdn_v, GDN_V("yz3", g - 1))
                for n in range(12):
                    m_ = nc.tensor.transpose(ps[:, 6, n * 24:(n + 1) * 24], c_in[:, n // 4, (n % 4) * P:(n % 4 + 1) * P], ident[0:24, 0:24])
                did(m_, "ct")
                def unit(n):
                    if n % 2 == 0:
                        pe.wait_ge(w_low, ph.slot0 + GDN_SLOTS * g + n // 2 + 1)
                    pe.wait_ge(acc_free, ph.unit0 + GDN_UNITS * g + n - 1)
                    in_products(n % 2, (n // 2) % 2, False, n % 2).then_inc(parts_done, 1)

                for n in range(15):
                    if g or n >= 2:
                        unit(n)
                    if g == 0:
                        gdn_pre_after(n)
                    if n in TURN_AFTER:
                        turn(TURN_AFTER[n])
                    if n in LENGTH_AFTER:
                        lengths(LENGTH_AFTER[n])
                    for m in SPREAD_AFTER.get(n, []):
                        spread_out(m)
                v("dq7")
                act_("si11")
                def sample_step(p, l, part):
                    if l == 1:
                        if part == 0:
                            v("pt.1" if p == 0 else "pt.3")
                        for b in (GC * p + part,) if part < 2 else (GC * p + 2, GC * p + 3):
                            pe.wait_ge(g_landed[b % RING], 32 * g + 16 * p + 16)
                            for h in range(GG):
                                m_ = nc.tensor.matmul(ps[:, 1, h * GC + b % GC:h * GC + b % GC + 1], g_ring[:, b % RING, h, :],
                                                      gk[:, h, SEQ + b:SEQ + b + 1], start=True, stop=True)
                        if part == 2:
                            did(m_, f"r{p}")
                    if l in (2, 4) and part == 2:
                        for b in range(GC * p + l - 2, GC * p + l):
                            v(f"dg{b}")
                            did(nc.tensor.matmul(ps[:, 5 - 4 * (b % 2), :], ones[:], sq[:, b % 2, 0:GG * P], start=True, stop=True), f"wr{b}")
                    if l in (3, 5) and part:
                        for b in (GC * p + l - 4 + part,):
                            v(f"sn{b}")
                            for h in range(GG):
                                m_ = nc.tensor.matmul(ps[:, 5 - 4 * (b % 2), h:h + 1], g_ring[:, b % RING, h, :],
                                                      gq[:, h, SEQ + b:SEQ + b + 1], start=True, stop=True)
                            did(m_, f"os{b}")

                for p in range(2):
                    both = [(2 * p + x_, 4 - 4 * x_, chain[x_]) for x_ in range(2)]
                    if p:
                        v("S.1")
                        act_("oc.1")
                    for c, bb, ch in both:
                        at_ = slice(c * P, (c + 1) * P)
                        if p == 0 and c == 1:
                            unit(15)
                            pe.wait_ge(acc_free, ph.unit0 + GDN_UNITS * g + 16)
                        v(f"aut.{c}")
                        did(nc.tensor.matmul(ps[:, bb, :], ones[:], ch["t1"][:].rearrange("p h n -> p (h n)"), start=True, stop=True), f"br.{c}")
                        for n, src, name in ((1, gk, "kt"), (2, gv, "vt")):
                            for h in range(GG):
                                m_ = nc.tensor.transpose(ps[:, bb + n, h * P:(h + 1) * P], src[:, h, at_], ident[:])
                            did(m_, f"{name}.{c}")
                        for h in range(GG):
                            m_ = nc.tensor.matmul(ps[:, bb + 3, h * P:(h + 1) * P], gk[:, h, at_], gk[:, h, at_], start=True, stop=True)
                        did(m_, f"kk.{c}")
                    for c, bb, ch in both:
                        at_ = slice(c * P, (c + 1) * P)
                        v(f"kd.{c}")
                        for h in range(GG):
                            m_ = nc.tensor.matmul(ps[:, bb + 1, h * P:(h + 1) * P], gk[:, h, at_], gq[:, h, at_], start=True, stop=True)
                        did(m_, f"qk.{c}")
                        v(f"vb.{c}")
                        v(f"m0.{c}")
                        for h in range(GG):
                            m_ = nc.tensor.transpose(ps[:, bb + 2, h * P:(h + 1) * P], ch["m"][:, h, :], ident[:])
                        did(m_, f"mt.{c}")

                    def four(bank, left, right, name):
                        for h in range(GG):
                            m_ = nc.tensor.matmul(ps[:, bank, h * P:(h + 1) * P], left[:, h, :], right[:, h, :], start=True, stop=True)
                        did(m_, name)

                    for l in range(1, LV + 1):
                        for c, bb, ch in both:
                            pe.wait_ge(gdn_p, Q(f"l{l}.{c}", g))
                            if l == 1:
                                act_(f"mt.{c}")
                            else:
                                v(f"a{l - 1}.{c}")
                                act_(f"t{l - 1}.{c}")
                            four(bb + 3, ch["lb" if l % 2 else "la"], ch["mt"], f"t{l}.{c}")
                        sample_step(p, l, 0)
                        for c, bb, ch in both:
                            act_(f"t{l}.{c}")
                            if l == 1:
                                v(f"dd.{c}")
                                act_(f"eb.{c}")
                            else:
                                v(f"b{l - 1}.{c}")
                            four(bb, ch["m"], ch["t1"], f"a{l}.{c}")
                            if l < LV:
                                four(bb + 2, ch["t1"], ch["m"], f"b{l}.{c}")
                            sample_step(p, l, 1 + c % 2)
                    for c, bb, ch in both:
                        v(f"a{LV}.{c}")
                        v(f"oz{GC * p + GC - 1}")
                        four(bb + 1, ch["mt"], ch["vb"], f"u.{c}")
                        act_(f"t{LV}.{c}")
                        four(bb + 3, ch["kb"], ch["mt"], f"wk.{c}")
                    for c, bb, ch in both:
                        act_(f"wk.{c}")
                        v("s0" if c == 0 else f"S.{c - 1}")
                        four(bb, ch["wk"], gs, f"w.{c}")
                        act_(f"u.{c}")
                        v(f"W.{c}")
                        v(f"qd.{c}")
                        for h in range(GG):
                            o = ps[:, bb + 1, h * P:(h + 1) * P]
                            nc.tensor.matmul(o, gs[:, h, :], ch["eb"][:, h, :], start=True, stop=False)
                            m_ = nc.tensor.matmul(o, ch["u"][:, h, :], ch["d2"][:, h, :], start=False, stop=True)
                        did(m_, f"o.{c}")
                        four(bb + 2, ch["kd"], ch["u"], f"s.{c}")
                for h in range(GG):
                    act_(f"nsq{h}")
                    for q in range(2):
                        m_ = nc.tensor.matmul(ps[0:GH, 2 + q, 0:HALF], gather(h), gsq[:, h, q * HALF:(q + 1) * HALF],
                                              start=h == 0, stop=h == GG - 1)
                    did(m_, f"nn{h}")
                v("rn")
                for h in range(GG):
                    if h >= 2:
                        v(f"y{h - 2}")
                    for q in range(2):
                        m_ = nc.tensor.matmul(ps[:, 4 + 2 * (h % 2) + q, 0:HALF], spread(h), roots_o[:, q * HALF:(q + 1) * HALF],
                                              start=True, stop=True)
                    did(m_, f"nb{h}")
                slot0, unit0 = ph.slot0 + GDN_SLOTS * g + 8, ph.unit0 + GDN_UNITS * g + 16
                pe.wait_ge(w_low, slot0 + 1)
                for t in range(GG):
                    v(f"lo{t}")
                    for n in range(2):
                        if t == 0:
                            pe.wait_ge(acc_free, unit0 + n - 1)
                        m_ = products(n, 0, 1, n * P + t * 4 * P, 4 * P, gyh, gyl, t, t == 0, t == GG - 1)
                        if t == GG - 1:
                            m_.then_inc(parts_done, 1)
                for n in range(2, KT):
                    if n == 4:
                        pe.wait_ge(w_low, slot0 + 2)
                    pe.wait_ge(acc_free, unit0 + n - 1)
                    products(n % 2, n // 4, 4, (n % 4) * P, 4 * P, gyh, gyl, 0, True, True).then_inc(parts_done, 1)

            for ph in phases:
                if ph.kind == "gdn":
                    first_units(ph, False)
                    gdn_pre(ph)
                    for g in range(2):
                        gdn_body(ph, g)
                if ph.kind == "ret":
                    ret_body(ph, 0)
                    with pe.Fori(1, RH) as h:
                        ret_body(ph, h)
                if ph.kind == "gate_up":
                    def body(i, last):
                        for s in range(2):
                            k = ph.slot0 + 2 * i + s
                            pe.wait_ge(w_low, k + 1)
                            if isinstance(i, int) and i == 0 and s == 0:
                                for t in range(KT):
                                    if t == (3 if ph.index else KT - 1):
                                        norm_sum(ph.norm)
                                    pe.wait_ge(x_low, KT * ph.norm + t + 1)
                                    for g in range(2):
                                        if t == 0 and ph.index:
                                            pe.wait_ge(acc_free, ph.unit0 + g - 1)
                                        m_ = products(g, s, 1, g * KT * P + t * P, P, xh, xl, t, t == 0, t == KT - 1)
                                        if t == KT - 1:
                                            m_.then_inc(parts_done, 1)
                                continue
                            for g in range(2):
                                u = ph.unit0 + 2 * (2 * i + s) + g
                                pe.wait_ge(acc_free, u - 1)
                                m_ = products(g, s, KT, g * KT * P, P, xh, xl, 0, True, True)
                                m_.then_inc(parts_done, 1)
                    rolled(pe, ph.slots // 2, body, True)
                if ph.kind == "down":
                    pe.wait_ge(h_low, FT * (ph.index + 1))

                    def body(i, last):
                        for q in range(2):
                            u = ph.unit0 + 2 * i + q
                            pe.wait_ge(acc_free, u - 1)
                            for s in range(2):
                                k = ph.slot0 + 4 * i + 2 * q + s
                                pe.wait_ge(w_low, k + 1)
                                m_ = products(q, s, 11, 0, P, hh, hl, 11 * s, s == 0, s == 1)
                                m_.then_inc(parts_done, 1)
                    rolled(pe, ph.units // 2, body)

            norm_sum(6)
            for t in range(KT):
                pe.wait_ge(y_ready, t + 1)
                if t >= 2:
                    pe.wait_ge(y_out, 2 * t - 2)
                b = 2 * (t % 2)
                for c in range(4):
                    nc.tensor.transpose(ps[:, b, c * P:(c + 1) * P], yy[:, t, c * P:(c + 1) * P], ident[:])
                nc.tensor.transpose(ps[0:DEC, b + 1, 0:P], yy[:, t, SEQ:NTOK], ident[:]).then_inc(y_turned, 1)

        @block.scalar
        def _(act):
            def split(ph, k, s, cols, done=None):
                act.wait_ge(w_landed[s], 16 * (k - s) + 32)
                if not isinstance(k, int) or k >= 2:
                    act.wait_ge(parts_done, ph.slot_done(k - 2) if done is None else done)
                nc.scalar.activation(wh[:, s, 0:cols], raw[:, s, 0:cols], ACT.Copy).then_inc(w_high, 1)

            def scaled(m, t, q, initial=True):
                if initial:
                    act.wait_ge(acc_free, t + 1)
                nc.scalar.activation(xh[:, t, :], x[:, t, :], ACT.Copy, scale=gains[:, KT * m + t:KT * m + t + 1]).then_inc(x_high, 1)
                if m or t >= 2:
                    act.wait_ge(x_ssq, KT * m + t - 1)
                nc.scalar.activation(sq[:, q, :], x[:, t, :], ACT.Square).then_inc(x_sq, 1)

            def root_of(m):
                act.wait_ge(ssq_sum, m + 1)
                nc.scalar.activation(halves(rinv[:]), ps[:, 6:8, 0:HALF], ACT.Sqrt, scale=1.0 / D,
                                     bias=eps[:, 0:1]).then_inc(ssq_root, 1)

            split(phases[0], 0, 0, SLOT)
            act.wait_ge(gains_ready, 1)
            act.wait_ge(ones_set, 2)
            for t in range(KT):
                scaled(0, t, t % 2)

            def ret_body(ph, h, last):
                def split_next(j):
                    if not (last and j == RET_SLOTS - 1 and not ph.next_cols):
                        cols = ph.next_cols if last and j == RET_SLOTS - 1 else ph.cols
                        split(ph, ph.slot0 + RET_SLOTS * h + j + 1, (j + 1) % 2, cols,
                              ph.part0 + RET_UNITS * h + RET_SLOT_DONE[j])

                first = isinstance(h, int) and h == 0
                for j in range(4):
                    split_next(j)
                    if first and j == 0:
                        root_of(ph.norm - 1)
                for c in range(4):
                    act.wait_ge(ret_t, RET_T(f"v{c}", h))
                    nc.scalar.activation(vtok[:, c, :], ps[:, 4 + c, :], ACT.Copy).then_inc(ret_a, RET_A.did(f"v{c}"))
                act.wait_ge(ret_t, RET_T("vs", h))
                nc.scalar.activation(vtok_s[:], ps[0:DEC, 7, :], ACT.Copy).then_inc(ret_a, RET_A.did("vs"))
                for e in range(4):
                    act.wait_ge(ret_t, RET_T(f"o{e}", h))
                    nc.scalar.activation(ro[:, e, :], ps[:, 4 + e, :], ACT.Copy).then_inc(ret_a, RET_A.did(f"o{e}"))
                    if e >= 2:
                        act.wait_ge(ret_p, RET_P(f"sum{e - 2}", h))
                    nc.scalar.activation(osq[:, e % 2, :], ps[:, 4 + e, :], ACT.Square).then_inc(ret_a, RET_A.did(f"sq{e}"))
                split_next(4)
                if not first:
                    act.wait_ge(s_out_stored, 16 * h)
                for t in range(2):
                    act.wait_ge(ret_t, RET_T(f"s{t}", h))
                    nc.scalar.activation(s_out[:, t, :], ps[:, 4 + t, :], ACT.Copy).then_inc(ret_a, RET_A.did(f"s{t}"))
                act.wait_ge(ret_t, RET_T("n", h))
                nc.scalar.activation(rinv_o[:], ps[:, 6, :], ACT.Sqrt, scale=1.0 / RV, bias=eps[:, 0:1])\
                    .then_inc(ret_a, RET_A.did("root"))
                act.wait_ge(head_landed, 16 * h + 16)
                for g in range(4):
                    for b in ((0, 1, 2, 3), (4, 5), (6, 7), ())[g]:
                        act.wait_ge(s_landed[b % RING], 32 * h + 16 * (b // RING) + 16)
                        nc.scalar.activation(s_ring[:, b % RING], s_ring[:, b % RING], ACT.Copy, scale=head_c[:, SEQ + 4:SEQ + 5])\
                            .then_inc(ret_a, RET_A.did(f"g{b}"))
                    if g == 3:
                        act.wait_ge(ret_t, RET_T("ns", h))
                        nc.scalar.activation(rinv_s[:], ps[:, 6, 0:DEC], ACT.Sqrt, scale=1.0 / RV, bias=eps[:, 0:1])\
                            .then_inc(ret_a, RET_A.did("rs"))
                    act.wait_ge(acc_free, ph.unit0 + RET_UNITS * h + 8 + g + 1)
                    nc.scalar.activation(rg[:, g, :], rg[:, g, :], ACT.Silu).then_inc(ret_a, RET_A.did(f"silu{g}"))
                    act.wait_ge(ret_v, RET_V(f"y{g}", h))
                    nc.scalar.activation(yh[:, g, 0:SEQ], ro[:, g, :], ACT.Copy).then_inc(ret_a, RET_A.did(f"hi{g}"))
                    if g % 2 == 1:
                        split_next(5 + g // 2)
                for n in range(KT):
                    if n == 3:
                        split_next(7)
                    if last:
                        act.wait_ge(acc_free, ph.unit0 + RET_UNITS * h + 12 + n + 1)
                        scaled(ph.norm, n, n % 2, False)

            def gdn_pre_after(n):
                if n == 2:
                    act.wait_ge(pre_v, PRE_V("m", 0))
                    nc.scalar.activation(small[:, 1], small[:, 1], ACT.Exp).then_inc(pre_a, PRE_A.did("e"))
                    nc.scalar.activation(a_log[:], a_log[:], ACT.Exp).then_inc(pre_a, PRE_A.did("na"))
                    nc.scalar.activation(small[:, 6], ba[:, :, 0:GH], ACT.Sigmoid).then_inc(pre_a, PRE_A.did("beta"))
                if n == 6:
                    act.wait_ge(pre_v, PRE_V("kd", 0))
                    nc.scalar.activation(ebcol[:], bcol[:], ACT.Exp).then_inc(pre_a, PRE_A.did("ebc"))
                    nc.scalar.activation(cdrep[:], cdrep[:], ACT.Exp).then_inc(pre_a, PRE_A.did("cd"))
                    nc.scalar.activation(kdcol[:], kdcol[:], ACT.Exp).then_inc(pre_a, PRE_A.did("kd"))
                    nc.scalar.activation(small[:, 4, 4, :], small[:, 5, 4, :], ACT.Exp).then_inc(pre_a, PRE_A.did("ea"))

            def gdn_body(ph, g, last):
                T, V, A, Q = GDN_T, GDN_V, GDN_A, GDN_P

                def split_next(j):
                    cols = ph.next_cols if last and j == GDN_SLOTS - 1 else ph.cols
                    split(ph, ph.slot0 + GDN_SLOTS * g + j + 1, (j + 1) % 2, cols, ph.part0 + GDN_UNITS * g + GDN_SLOT_DONE[j])

                def t_(name):
                    act.wait_ge(gdn_t, T(name, g))

                def v(name):
                    act.wait_ge(gdn_v, V(name, g))

                t_("ct")
                nc.scalar.activation(c_old[:], ps[:, 6, 0:12 * 3 * DEC], ACT.Copy).then_inc(gdn_a, A.did("ctc"))
                for n in range(12):
                    if n % 2 == 0:
                        split_next(n // 2)
                    dst = (gq, gk, gv)[n // 4]
                    v(f"cd{n}")
                    nc.scalar.activation(dst[:, n % 4, 0:SEQ], cv[:, n % 2, 0:SEQ], ACT.Silu)
                    nc.scalar.activation(dst[:, n % 4, SEQ:NTOK], cv[:, n % 2, SEQ + 3:C_LEN:TAPS], ACT.Silu).then_inc(gdn_a, A.did(f"si{n}"))
                    if g == 0:
                        gdn_pre_after(n)
                    if n in (4, 8, 11):
                        y_ = min(n // 4 - 1, 2) if n < 11 else 2
                        t_(f"cs{4 * y_ + 3}")
                        if g and y_ == 0:
                            act.wait_ge(c_stored, 144 * g)
                        nc.scalar.activation(c_out[:, y_, :], ps[0:TAIL, 7, :], ACT.Copy).then_inc(gdn_a, A.did(f"cse{y_}"))
                    if n < 8:
                        if n == 0:
                            act.wait_ge(x_ssq, KT * ph.norm)
                        if n >= 2:
                            t_(f"ln{n - 2}")
                        act.wait_ge(gdn_a, A(f"si{n}", g))
                        nc.scalar.activation(sq[:, n % 2, :], dst[:, n % 4, :], ACT.Square).then_inc(gdn_a, A.did(f"sq{n}"))
                    if n == 9:
                        t_("ln7")
                        act.wait_ge(eps_set, 6)
                        nc.scalar.activation(halves(roots[:]), ps[0:GH, 4:6, 0:HALF], ACT.Sqrt, scale=scale_q[:, 0:1], bias=eps_q[:, 0:1])\
                            .then_inc(gdn_a, A.did("rt"))
                split_next(6)
                split_next(7)
                for p in range(2):
                    both = [(2 * p + x_, 4 - 4 * x_, chain[x_]) for x_ in range(2)]

                    def copy(dst, bank, name, f_=ACT.Copy):
                        nc.scalar.activation(dst, by_head(bank), f_).then_inc(gdn_a, A.did(name))

                    for c, bb, ch in both:
                        v(f"dd.{c}")
                        copy(ch["eb"][:], bb, f"eb.{c}", ACT.Exp)
                        act.wait_ge(gdn_p, Q(f"n1.{c}", g))
                        nc.scalar.activation(ch["d1"][:], ch["d1"][:], ACT.Exp, scale=-1.0).then_inc(gdn_a, A.did(f"d1.{c}"))
                    for c, bb, ch in both:
                        v(f"n2.{c}")
                        nc.scalar.activation(ch["d2"][:], ch["d2"][:], ACT.Exp).then_inc(gdn_a, A.did(f"d2.{c}"))
                    if p == 0:
                        split_next(8)
                    for c, bb, ch in both:
                        t_(f"mt.{c}")
                        copy(ch["mt"][:], bb + 2, f"mt.{c}")
                    for l in range(1, LV + 1):
                        for c, bb, ch in both:
                            if l < LV:
                                t_(f"mt.{c}" if l == 1 else f"b{l - 1}.{c}")
                                none = levels[LV][:, P // 2:P // 2 + 2 ** l].rearrange("p (o j) -> p o j", o=1)
                                dst = blocks(flat(ch["t1"]), l, 0)
                                nc.scalar.activation(dst, none.broadcast_to([P, dst.shape[1], 2 ** l]), ACT.Copy)\
                                    .then_inc(gdn_a, A.did(f"z{l}.{c}"))
                        for c, bb, ch in both:
                            t_(f"t{l}.{c}")
                            nc.scalar.activation(blocks(flat(ch["t1"]), l, 1), blocks(ps[:, bb + 3, :], l, 1), ACT.Copy).then_inc(gdn_a, A.did(f"t{l}.{c}"))
                    for c, bb, ch in both:
                        t_(f"u.{c}")
                        copy(ch["u"][:], bb + 1, f"u.{c}")
                        t_(f"wk.{c}")
                        copy(ch["wk"][:], bb + 3, f"wk.{c}")
                    for c, bb, ch in both:
                        t_(f"o.{c}")
                        nc.scalar.activation(gq[:, :, c * P:(c + 1) * P], by_head(bb + 1), ACT.Copy).then_inc(gdn_a, A.did(f"oc.{c}"))
                act.wait_ge(acc_free, ph.unit0 + GDN_UNITS * g + 16)
                nc.scalar.activation(gz[:], gz[:], ACT.Silu).then_inc(gdn_a, A.did("sz"))
                v("S.3")
                v("oz7")
                t_("s.3")
                for h in range(GG):
                    if h == 0:
                        act.wait_ge(gdn_a, A("oc.3", g))
                    nc.scalar.activation(gsq[:, h, :], gq[:, h, :], ACT.Square).then_inc(gdn_a, A.did(f"nsq{h}"))
                t_("nn3")
                nc.scalar.activation(halves(roots_o[:]), ps[0:GH, 2:4, 0:HALF], ACT.Sqrt, scale=1.0 / P, bias=eps[0:GH, 0:1])\
                    .then_inc(gdn_a, A.did("nrt"))
                for h in range(GG):
                    v(f"yz{h}")
                    nc.scalar.activation(gyh[:, h, :], gq[:, h, :], ACT.Copy).then_inc(gdn_a, A.did(f"hi{h}"))
                for n in range(KT):
                    if n == 3:
                        split_next(9)
                    if last:
                        act.wait_ge(acc_free, ph.unit0 + GDN_UNITS * g + 16 + n + 1)
                        scaled(ph.norm, n, n % 2, False)

            for ph in phases:
                if ph.kind == "gdn":
                    root_of(ph.norm - 1)
                    for g in range(2):
                        gdn_body(ph, g, g == 1)
                if ph.kind == "ret":
                    ret_body(ph, 0, False)
                    with act.Fori(1, RH - 1) as h:
                        ret_body(ph, h, False)
                    ret_body(ph, RH - 1, True)
                if ph.kind == "gate_up":
                    def body(i, last):
                        for s in range(2):
                            k = ph.slot0 + 2 * i + s
                            cols = ph.next_cols if last and s == 1 else ph.cols
                            split(ph, k + 1, (s + 1) % 2, cols)
                            if isinstance(i, int) and i == 0 and s == 0:
                                root_of(ph.norm)
                            j = 2 * i + s
                            n = FT * ph.index + j
                            act.wait_ge(acc_free, ph.unit0 + 2 * j + 1)
                            nc.scalar.activation(gate[:], gate[:], ACT.Silu).then_inc(gate_ready, 1)
                            act.wait_ge(h_ready, n + 1)
                            act.sem_inc(act_held, 1)
                            nc.scalar.activation(hh[:, j, :], up[:], ACT.Copy).then_inc(h_high, 1)
                    rolled(act, ph.slots // 2, body, True)
                if ph.kind == "down":
                    def body(i, last):
                        for q in range(2):
                            for s in range(2):
                                k = ph.slot0 + 4 * i + 2 * q + s
                                cols = ph.next_cols if last and q == 1 and s == 1 else ph.cols
                                if cols:
                                    split(ph, k + 1, (s + 1) % 2, cols)
                            t = 2 * i + q
                            act.wait_ge(acc_free, ph.unit0 + t + 1)
                            act.sem_inc(act_held, 1)
                            nc.scalar.activation(xh[:, t, :], x[:, t, :], ACT.Copy,
                                                 scale=gains[:, bass.ds(KT * ph.norm + t, 1)]).then_inc(x_high, 1)
                            act.wait_ge(x_ssq, KT * ph.norm + t - 1)
                            act.sem_inc(act_held, 1)
                            nc.scalar.activation(sq[:, q, :], x[:, t, :], ACT.Square).then_inc(x_sq, 1)
                    rolled(act, ph.units // 2, body)

            root_of(6)
            for t in range(KT):
                act.wait_ge(y_turned, t + 1)
                nc.scalar.activation(y_tok[:, :, t * P:(t + 1) * P], by_head(2 * (t % 2)), ACT.Copy).then_inc(y_out, 1)
                nc.scalar.activation(y_new[:, t * P:(t + 1) * P], ps[0:DEC, 2 * (t % 2) + 1, 0:P], ACT.Copy).then_inc(y_out, 1)

        @block.vector
        def _(dve):
            def split(ph, k, s, cols):
                dve.wait_ge(w_high, k + 1)
                nc.vector.tensor_tensor(wl[:, s, 0:cols], raw[:, s, 0:cols], wh[:, s, 0:cols].bitcast(F32),
                                        ALU.subtract).then_inc(w_low, 1)

            def scaled_low(m, t):
                dve.wait_ge(x_high, KT * m + t + 1)
                nc.vector.scalar_tensor_tensor(xl[:, t, :], x[:, t, :], gains[:, bass.ds(KT * m + t, 1)],
                                               xh[:, t, :].bitcast(F32), ALU.mult, ALU.subtract).then_inc(x_low, 1)

            dve.wait_ge(gains_turned, 1)
            nc.vector.tensor_copy(gains[:], ps[:, 7, 0:56]).then_inc(gains_ready, 1)
            dve.wait_ge(gains_ready, 1)
            for t in range(KT):
                b = 4 + 2 * (t % 2)
                dve.wait_ge(parts_done, t + 1)
                nc.vector.tensor_copy(x[:, t, 0:SEQ], ps[:, b, :])
                m_ = nc.vector.tensor_copy(x[:, t, SEQ:NTOK], ps[:, b + 1, 0:DEC])
                m_.then_inc(acc_free, 1)
                if t == 1:
                    split(phases[0], 0, 0, SLOT)
                if t:
                    scaled_low(0, t - 1)
            scaled_low(0, KT - 1)

            def ret_body(ph, h, last):
                def split_next(j):
                    if not (last and j == RET_SLOTS - 1 and not ph.next_cols):
                        cols = ph.next_cols if last and j == RET_SLOTS - 1 else ph.cols
                        split(ph, ph.slot0 + RET_SLOTS * h + j + 1, (j + 1) % 2, cols)

                def arrived(j):
                    dve.wait_ge(parts_done, ph.part0 + RET_UNITS * h + j + 1)

                def freed(j):
                    dve.wait_ge(acc_free, ph.unit0 + RET_UNITS * h + j + 1)

                first = isinstance(h, int) and h == 0
                V, A, T = RET_V, RET_A, RET_T
                for j, (dst, scale, name) in enumerate(((rq, 1.0, "q"), (rk, RET_SCALE, "k"))):
                    split_next(j)
                    if first and j == 0:
                        dve.wait_ge(ssq_root, ph.norm)
                        nc.vector.reciprocal(rinv[:], rinv[:]).then_inc(ssq_inv, 1)
                        dve.wait_ge(ssq_inv, ph.norm)
                        dve.wait_ge(ret_consts, 48)
                        nc.vector.tensor_tensor(cosr[:], cosr[:], rinv[:], ALU.mult).then_inc(ret_tables, 1)
                        nc.vector.tensor_tensor(sinr[:], sinr[:], rinv[:], ALU.mult).then_inc(ret_tables, 1)
                        dve.wait_ge(ret_tables, 2)
                    if j or not first:
                        dve.wait_ge(ret_v, V("q", h) if j else V("yl", h - 1))
                    mul = lambda o, u, t: nc.vector.scalar_tensor_tensor(halves(o), pair(u), scale, halves(t[:]), ALU.mult, ALU.mult)
                    arrived(2 * j)
                    mul(dst[:, 0, :], 0, cosr)
                    mul(rot[:, 0, :], 0, sinr).then_inc(acc_free, 1)
                    arrived(2 * j + 1)
                    mul(rot[:, 1, :], 1, sinr)
                    mul(dst[:, 1, :], 1, cosr).then_inc(acc_free, 1)
                    freed(2 * j + 1)
                    nc.vector.tensor_tensor(dst[:, 0, :], dst[:, 0, :], rot[:, 1, :], ALU.subtract)
                    nc.vector.tensor_tensor(dst[:, 1, :], dst[:, 1, :], rot[:, 0, :], ALU.add).then_inc(ret_v, V.did(name))
                for e in range(4):
                    if e % 2 == 0:
                        split_next(2 + e // 2)
                    arrived(4 + e)
                    nc.vector.tensor_tensor(halves(rv[:, e, :]), pair(e), halves(rinv[:]), ALU.mult).then_inc(acc_free, 1)
                dve.wait_ge(head_landed, 16 * h + 16)
                dve.wait_ge(ret_t, T("p0", h))
                nc.vector.tensor_tensor(pt[:, 0:512], ps[:, 4, :], head_c[:, 0:512], ALU.mult).then_inc(ret_v, V.did("pt0"))
                dve.wait_ge(ret_t, T("p1", h))
                nc.vector.tensor_tensor(pt[:, 512:896], ps[:, 5, 0:384], head_c[:, 0:384], ALU.mult).then_inc(ret_v, V.did("pt1"))
                dve.wait_ge(ret_t, T("p23", h))
                nc.vector.tensor_tensor(pt[:, 896:1152], ps[:, 6, 0:256], head_c[:, 0:256], ALU.mult)
                nc.vector.tensor_tensor(pt[:, 1152:1280], ps[:, 6, 256:384], head_c[:, 0:128], ALU.mult).then_inc(ret_v, V.did("pt23"))
                for name, c in (("k01", 0), ("k23", 2)):
                    dve.wait_ge(ret_t, T(name, h))
                    for n in range(2):
                        m_ = nc.vector.tensor_scalar(ktok[:, c + n, :], ps[:, 7, n * RK:(n + 1) * RK],
                                                     head_c[:, SEQ + c + n:SEQ + c + n + 1], None, ALU.mult)
                    m_.then_inc(ret_v, V.did(name))
                split_next(4)
                dve.wait_ge(ret_a, A("root", h))
                nc.vector.reciprocal(rinv_o[:], rinv_o[:]).then_inc(ret_v, V.did("ro"))
                def update(b):
                    dve.wait_ge(ret_t, T(f"b{b}", h))
                    dve.wait_ge(ret_a, A(f"g{b}", h))
                    for t in range(2):
                        st_ = s_ring[:, b % RING, t, :]
                        m_ = nc.vector.scalar_tensor_tensor(st_, ps[:, 4 + b % 2, :], rk[:, t, SEQ + b:SEQ + b + 1], st_,
                                                            ALU.mult, ALU.add)
                    m_.then_inc(ret_v, V.did(f"u{b}"))

                def sample_outputs(e, gated, high):
                    nc.vector.tensor_tensor(o_s[:, e, :], o_s[:, e, :], rg[:, e, SEQ:NTOK], ALU.mult).then_inc(ret_v, V.did(gated))
                    dve.wait_ge(ret_v, V(gated, h))
                    nc.vector.tensor_copy(yh[:, e, SEQ:NTOK], o_s[:, e, :]).then_inc(ret_v, V.did(high))

                def sample_low(e, high, low):
                    dve.wait_ge(ret_v, V(high, h))
                    nc.vector.tensor_tensor(yl[:, e, SEQ:NTOK], o_s[:, e, :], yh[:, e, SEQ:NTOK].bitcast(F32), ALU.subtract)\
                        .then_inc(ret_v, V.did(low))

                update(0)
                update(1)
                for g in range(4):
                    dve.wait_ge(ret_v, V("ro", h))
                    nc.vector.tensor_tensor(ro[:, g, :], ro[:, g, :], rinv_o[:], ALU.mult).then_inc(ret_v, V.did(f"on{g}"))
                    if g == 3:
                        dve.wait_ge(ret_t, T("q7", h))
                        nc.vector.tensor_copy(o_s[:].rearrange("p e b -> p (e b)"), ps[:, 7, 0:4 * DEC]).then_inc(ret_v, V.did("os"))
                        dve.wait_ge(ret_v, V("os", h))
                        nc.vector.tensor_tensor(osq_s[:], o_s[:], o_s[:], ALU.mult).then_inc(ret_v, V.did("ossq"))
                        dve.wait_ge(ret_a, A("rs", h))
                        nc.vector.reciprocal(rinv_s[:], rinv_s[:]).then_inc(ret_v, V.did("rs"))
                        dve.wait_ge(ret_v, V("rs", h))
                        nc.vector.tensor_tensor(o_s[:], o_s[:], rinv_s[:].rearrange("p (e b) -> p e b", e=1).broadcast_to([P, 4, DEC]),
                                                ALU.mult).then_inc(ret_v, V.did("osn"))
                        dve.wait_ge(ret_v, V("osn", h))
                        sample_outputs(slice(0, 3), "ys2", "yh2")
                        sample_low(slice(0, 3), "yh2", "yl2")
                    arrived(8 + g)
                    nc.vector.tensor_tensor(halves(rg[:, g, :]), pair(g), halves(rinv[:]), ALU.mult).then_inc(acc_free, 1)
                    if g < 3:
                        update(2 * g + 2)
                        update(2 * g + 3)
                    dve.wait_ge(ret_a, A(f"silu{g}", h))
                    dve.wait_ge(ret_v, V(f"on{g}", h))
                    nc.vector.tensor_tensor(ro[:, g, :], ro[:, g, :], rg[:, g, 0:SEQ], ALU.mult).then_inc(ret_v, V.did(f"y{g}"))
                    if g == 3:
                        sample_outputs(slice(3, 4), "ys", "yh")
                    dve.wait_ge(ret_a, A(f"hi{g}", h))
                    nc.vector.tensor_tensor(yl[:, g, 0:SEQ], ro[:, g, :], yh[:, g, 0:SEQ].bitcast(F32), ALU.subtract)\
                        .then_inc(ret_v, V.did(f"lo{g}"))
                    if g == 3:
                        sample_low(slice(3, 4), "yh", "yl")
                    if g % 2 == 1:
                        split_next(5 + g // 2)
                for n in range(KT):
                    arrived(12 + n)
                    xt = halves(x[:, n, :])
                    nc.vector.tensor_tensor(xt, pair(n), xt, ALU.add).then_inc(acc_free, 1)
                    if n == 3:
                        split_next(7)
                    if last:
                        scaled_low(ph.norm, n)

            def pre_did(m_, name):
                m_.then_inc(pre_v, PRE_V.did(name))

            def pre_own(name):
                dve.wait_ge(pre_v, PRE_V(name, 0))

            def gdn_pre(ph):
                dve.wait_ge(pre_landed, 96)
                own = gains[:, KT * (ph.norm - 1):KT * ph.norm].rearrange("p (t o) -> p t o", o=1)
                pre_did(nc.vector.tensor_tensor(wba[:], wba[:], own.broadcast_to([P, KT, 2 * GH]), ALU.mult), "wg")
                dve.wait_ge(pre_t, PRE_T("cw", 0))
                pre_did(nc.vector.tensor_copy(conv_w[:].rearrange("p j t -> p (j t)"), ps[:, 4, 0:96]), "cw")
                dve.wait_ge(ssq_root, ph.norm)
                nc.vector.reciprocal(rinv[:], rinv[:]).then_inc(ssq_inv, 1)
                dve.wait_ge(ssq_inv, ph.norm)

            def gdn_pre_after(n):
                did, v = pre_did, pre_own
                each_block = lambda t: t[:].rearrange("p (o h) -> p o h", o=1).broadcast_to([P, 5, GH])
                y_, e_, z_, w_, p_, a_ = (small[:, i] for i in range(6))
                if n == 0:
                    dve.wait_ge(pre_t, PRE_T("ba", 0))
                    pre_did(nc.vector.tensor_tensor(halves(ba_rows[:]), ps[0:2 * GH, 4:6, 0:HALF], halves(rinv[0:2 * GH, :]), ALU.mult), "bf")
                if n == 2:
                    dve.wait_ge(pre_t, PRE_T("tb", 0))
                    did(nc.vector.tensor_copy(ba[:].rearrange("p c n -> p (c n)"), ps[:, 6, 0:80]), "ba")
                    v("ba")
                    did(nc.vector.tensor_tensor(y_, ba[:, :, GH:2 * GH], each_block(dt_b), ALU.add), "y")
                    v("y")
                    did(nc.vector.scalar_tensor_tensor(e_, y_, -1.0, y_, ALU.mult, ALU.min), "m")
                if n == 3:
                    dve.wait_ge(pre_a, PRE_A("e", 0))
                    did(nc.vector.tensor_scalar(w_, e_, 2.0, None, ALU.add), "d")
                    v("d")
                    did(nc.vector.reciprocal(w_, w_), "di")
                    v("di")
                    did(nc.vector.tensor_tensor(z_, e_, w_, ALU.mult), "z")
                    v("z")
                    did(nc.vector.tensor_tensor(w_, z_, z_, ALU.mult), "w")
                    v("w")
                    did(nc.vector.tensor_scalar(p_, w_, 1.0 / 17, None, ALU.mult), "p0")
                    for i in range(1, 7):
                        v(f"p{i - 1}")
                        did(nc.vector.scalar_tensor_tensor(p_, p_, 1.0 / (17 - 2 * i), w_, ALU.add, ALU.mult), f"p{i}")
                if n == 4:
                    v("p6")
                    did(nc.vector.scalar_tensor_tensor(p_, p_, 1.0 / 3, w_, ALU.add, ALU.mult), "l")
                    v("l")
                    did(nc.vector.scalar_tensor_tensor(p_, p_, 1.0, z_, ALU.add, ALU.mult), "r")
                    v("r")
                    did(nc.vector.tensor_scalar(y_, y_, 0.0, None, ALU.max), "sp")
                    v("sp")
                    nc.vector.scalar_tensor_tensor(e_, p_, 2.0, y_, ALU.mult, ALU.add).then_inc(softplus_ready, 1)
                    dve.wait_ge(softplus_ready, 1)
                    dve.wait_ge(pre_a, PRE_A("na", 0))
                    did(nc.vector.scalar_tensor_tensor(a_, e_, -1.0, each_block(a_log), ALU.mult, ALU.mult), "a")
                if n == 6:
                    dve.wait_ge(pre_t, PRE_T("blast", 0))
                    tok = lambda t: t[:].rearrange("p c h -> p (c h)")
                    did(nc.vector.tensor_copy(tok(bcol), ps[:, 6, 128:160]), "bcol")
                    v("bcol")
                    did(nc.vector.tensor_copy(tok(cdrep), ps[:, 6, 160:192]), "cdl")
                    v("cdl")
                    did(nc.vector.tensor_tensor(kdcol[:], cdrep[:], bcol[:], ALU.subtract), "kd")
                if n == 7:
                    dve.wait_ge(pre_a, PRE_A("ea", 0))
                    did(nc.vector.tensor_tensor(bebcol[:], ebcol[:], small[:, 6, 0:4, :], ALU.mult), "beb")
                    for i, src, name in ((0, small[:, 4, 4, :], "sma"), (1, small[:, 6, 4, :], "smb")):
                        did(nc.vector.tensor_tensor(sm[:, i], src.rearrange("p (h o) -> p h o", o=1).broadcast_to([P, GH, DEC]),
                                                    smask.rearrange("p (o b) -> p o b", o=1).broadcast_to([P, GH, DEC]), ALU.mult), name)
                if n == 9:
                    dve.wait_ge(pre_t, PRE_T("smp", 0))
                    did(nc.vector.tensor_copy(eab[:].rearrange("p a h b -> p (a h b)"), ps[:, 6, 256:384]), "eab")
                    v("eab")

            def gdn_body(ph, g, last):
                T, V, A, Q = GDN_T, GDN_V, GDN_A, GDN_P
                h0 = g * GG

                def split_next(j):
                    cols = ph.next_cols if last and j == GDN_SLOTS - 1 else ph.cols
                    split(ph, ph.slot0 + GDN_SLOTS * g + j + 1, (j + 1) % 2, cols)

                def t_(name):
                    dve.wait_ge(gdn_t, T(name, g))

                def v(name):
                    dve.wait_ge(gdn_v, V(name, g))

                def act_(name):
                    dve.wait_ge(gdn_a, A(name, g))

                def did(m_, name):
                    m_.then_inc(gdn_v, V.did(name))

                if g:
                    dve.wait_ge(parts_done, ph.part0 + GDN_UNITS * g)
                did(nc.vector.memset(uu[:, :, 0:TAPS - 1], 0.0), "uz")
                if g:
                    dve.wait_ge(gs_stored, 16 * g)
                did(nc.vector.memset(gs[:], 0.0), "s0")
                v("s0")
                for n in range(12):
                    if n % 2 == 0:
                        split_next(n // 2)
                    dve.wait_ge(parts_done, ph.part0 + GDN_UNITS * g + n + 1)
                    if n >= 2:
                        t_(f"cs{n - 2}")
                        v(f"cd{n - 2}")
                    q, r_ = n % 2, uu[:, n % 2]
                    nc.vector.tensor_tensor(r_[:, 3:3 + HALF], ps[:, 2 * q, 0:HALF], rinv[:, 0:HALF], ALU.mult)
                    nc.vector.tensor_tensor(r_[:, 3 + HALF:3 + SEQ], ps[:, 2 * q + 1, 0:SEQ - HALF], rinv[:, HALF:SEQ], ALU.mult)
                    nc.vector.tensor_tensor(r_[:, 3 + SEQ + 3:U_LEN:TAPS], ps[:, 2 * q + 1, SEQ - HALF:HALF], rinv[:, SEQ:NTOK], ALU.mult)\
                        .then_inc(acc_free, 1)
                    if n == 0:
                        act_("ctc")
                    did(nc.vector.tensor_copy(r_[:, 3 + SEQ:U_LEN].rearrange("p (b j) -> p b j", j=TAPS)[:, :, 0:3],
                                              c_old[:, n * 24:(n + 1) * 24].rearrange("p (b j) -> p b j", j=3)), f"ux{n}")
                    v(f"ux{n}")
                    w_ = lambda j: conv_w[:, j, (n // 4) * GH + h0 + n % 4:(n // 4) * GH + h0 + n % 4 + 1]
                    c_ = cv[:, n % 2, :]
                    if n >= 2:
                        act_(f"si{n - 2}")
                    did(nc.vector.tensor_scalar(c_, r_[:, 0:C_LEN], w_(0), None, ALU.mult), f"ca{n}")
                    for j, name in ((1, "cb"), (2, "cc"), (3, "cd")):
                        v(f"{('ca', 'cb', 'cc')[j - 1]}{n}")
                        did(nc.vector.scalar_tensor_tensor(c_, r_[:, j:j + C_LEN], w_(j), c_, ALU.mult, ALU.add), f"{name}{n}")
                    if g == 0:
                        gdn_pre_after(n)
                    if n == 10:
                        act_("rt")
                        did(nc.vector.reciprocal(roots[:], roots[:]), "ri")
                def gate_unit(n):
                    dve.wait_ge(parts_done, ph.part0 + GDN_UNITS * g + 12 + n + 1)
                    nc.vector.tensor_tensor(halves(gz[:, n, :]), pair(n), halves(rinv[:]), ALU.mult).then_inc(acc_free, 1)

                for n in range(3):
                    if n % 2 == 0:
                        split_next(6 + n // 2)
                    gate_unit(n)
                    for m in SPREAD_AFTER.get(12 + n, []):
                        t_(f"bc{m}")
                        dst = (gq, gk)[m // 4][:, m % 4, :]
                        b_ = 4 + 2 * (m % 2)
                        did(nc.vector.tensor_tensor(halves(dst), halves(dst), ps[:, b_:b_ + 2, 0:HALF], ALU.mult), f"dq{m}")
                def sample_step(p, l):
                    tt = nc.vector.tensor_tensor
                    first = GC * p
                    if l == 1:
                        t_(f"r{p}")
                        w_, at_ = wt[:, :, first:first + GC], slice(first, first + GC)
                        r_ = ps[:, 1, 0:GG * GC].rearrange("p (h b) -> p h b", h=GG)
                        did(tt(w_, r_, eab[:, 0, h0:h0 + GG, at_], ALU.mult), f"wa{p}")
                        v(f"wa{p}")
                        did(tt(w_, gv[:, :, SEQ + first:SEQ + first + GC], w_, ALU.subtract), f"wb{p}")
                        v(f"wb{p}")
                        did(tt(w_, w_, eab[:, 1, h0:h0 + GG, at_], ALU.mult), f"wc{p}")
                        v(f"wc{p}")
                    if l in (2, 4):
                        for b in range(first + l - 2, first + l):
                            t_(f"wr{b}")
                            did(tt(dg[b % 2], by_head(5 - 4 * (b % 2)), heads(gk[:, :, SEQ + b]), ALU.mult), f"kw{b}")
                            dve.wait_ge(gdn_p, Q(f"se{b}", g))
                            v(f"kw{b}")
                            did(tt(g_ring[:, b % RING], g_ring[:, b % RING], dg[b % 2], ALU.add), f"sn{b}")
                    if l in (3, 5):
                        for b in range(first + l - 3, first + l - 1):
                            t_(f"os{b}")
                            did(nc.vector.tensor_copy(gq[:, :, SEQ + b], ps[:, 5 - 4 * (b % 2), 0:GG]), f"oz{b}")
                    if l in (1, 3):
                        if l == 3:
                            v(f"sn{first + 1}")
                        for b in range(first + l - 1, first + l + 1):
                            did(tt(dg[b % 2], every(ident[:]), heads(wt[:, :, b]), ALU.mult), f"dg{b}")

                v("dq7")
                for p in range(2):
                    both = [(2 * p + x_, 4 - 4 * x_, chain[x_]) for x_ in range(2)]
                    tt = nc.vector.tensor_tensor
                    hs = lambda t, c: heads(t[:, c, h0:h0 + GG])
                    for c, bb, ch in both:
                        if p:
                            t_(f"s.{c - 2}")
                            v(f"S.{c - 2}")
                        else:
                            dve.wait_ge(c_stored, 144 * (g + 1))
                            act_("cse2")
                        did(tt(ch["t1"][:], every(ut), heads(small[:, 5, c, h0:h0 + GG]), ALU.mult), f"aut.{c}")
                    for c, bb, ch in both:
                        if p == 0 and c == 1:
                            gate_unit(3)
                        t_(f"br.{c}")
                        did(tt(ch["dd"][:], by_head(bb), hs(bcol, c), ALU.subtract), f"dd.{c}")
                        t_(f"kt.{c}")
                        did(tt(ch["kb"][:], by_head(bb + 1), hs(bebcol, c), ALU.mult), f"kb.{c}")
                        did(tt(ch["kd"][:], by_head(bb + 1), hs(kdcol, c), ALU.mult), f"kd.{c}")
                        t_(f"vt.{c}")
                        did(tt(ch["vb"][:], by_head(bb + 2), heads(small[:, 6, c, h0:h0 + GG]), ALU.mult), f"vb.{c}")
                        v(f"dd.{c}")
                        did(tt(ch["d2"][:], ch["dd"][:], every(negup), ALU.add), f"n2.{c}")
                    for c, bb, ch in both:
                        t_(f"kk.{c}")
                        act_(f"d1.{c}")
                        for h in range(GG):
                            m_ = nc.vector.scalar_tensor_tensor(ch["d1"][:, h, :], by_head(bb + 3)[:, h, :], small[:, 6, c, h0 + h:h0 + h + 1],
                                                                ch["d1"][:, h, :], ALU.mult, ALU.mult)
                        did(m_, f"L.{c}")
                        v(f"L.{c}")
                        did(tt(ch["la"][:], ch["d1"][:], every(levels[0]), ALU.mult), f"l0.{c}")
                        v(f"l0.{c}")
                        did(tt(ch["m"][:], every(ident[:]), ch["la"][:], ALU.subtract), f"m0.{c}")
                    for c, bb, ch in both:
                        t_(f"qk.{c}")
                        act_(f"d2.{c}")
                        did(tt(ch["d2"][:], by_head(bb + 1), ch["d2"][:], ALU.mult), f"pt.{c}")
                        act_(f"eb.{c}")
                        did(tt(ch["eb"][:], gq[:, :, c * P:(c + 1) * P], ch["eb"][:], ALU.mult), f"qd.{c}")
                    if p == 0:
                        split_next(8)
                    for l in range(1, LV + 1):
                        for c, bb, ch in both:
                            t_(f"a{l}.{c}")
                            act_(f"mt.{c}" if l == 1 else f"t{l}.{c}")
                            v(f"m0.{c}" if l == 1 else f"b{l - 1}.{c}")
                            mine = blocks(flat(ch["mt"]), l, 1)
                            did(tt(mine, mine, blocks(ps[:, bb, :], l, 1), ALU.subtract), f"a{l}.{c}")
                            if l < LV:
                                t_(f"b{l}.{c}")
                                mine = blocks(flat(ch["m"]), l, 0)
                                did(tt(mine, mine, blocks(ps[:, bb + 2, :], l, 0), ALU.subtract), f"b{l}.{c}")
                        sample_step(p, l)
                    for c, bb, ch in both:
                        t_(f"w.{c}")
                        act_(f"u.{c}")
                        did(tt(ch["u"][:], ch["u"][:], by_head(bb), ALU.subtract), f"W.{c}")
                        t_(f"s.{c}")
                        dve.wait_ge(gdn_p, Q(f"s2.{c}", g))
                        did(tt(gs[:], gs2[:], by_head(bb + 2), ALU.add), f"S.{c}")
                act_("nrt")
                did(nc.vector.reciprocal(roots_o[:], roots_o[:]), "rn")
                act_("sz")
                for h in range(GG):
                    t_(f"nb{h}")
                    b_ = 4 + 2 * (h % 2)
                    mine = halves(gq[:, h, :])
                    did(nc.vector.scalar_tensor_tensor(mine, mine, norm_w[:, 0:1], ps[:, b_:b_ + 2, 0:HALF], ALU.mult, ALU.mult), f"y{h}")
                    v(f"y{h}")
                    did(nc.vector.tensor_tensor(gq[:, h, :], gq[:, h, :], gz[:, h, :], ALU.mult), f"yz{h}")
                    for low in ((), (0,), (1,), (2, 3))[h]:
                        act_(f"hi{low}")
                        did(nc.vector.tensor_tensor(gyl[:, low, :], gq[:, low, :], gyh[:, low, :].bitcast(F32), ALU.subtract), f"lo{low}")
                for n in range(KT):
                    dve.wait_ge(parts_done, ph.part0 + GDN_UNITS * g + 16 + n + 1)
                    xt = halves(x[:, n, :])
                    nc.vector.tensor_tensor(xt, pair(n), xt, ALU.add).then_inc(acc_free, 1)
                    if n == 3:
                        split_next(9)
                    if last:
                        scaled_low(ph.norm, n)

            def mixer_stored(index):
                if index == 1:
                    for n in range(RING):
                        dve.wait_ge(s_stored[n], 32 * RH)
                    dve.wait_ge(s_out_stored, 16 * RH)
                if index == 3:
                    for n in range(RING):
                        dve.wait_ge(g_stored[n], 64)
                    dve.wait_ge(gs_stored, 32)

            for ph in phases:
                if ph.kind == "gdn":
                    gdn_pre(ph)
                    for g in range(2):
                        gdn_body(ph, g, g == 1)
                if ph.kind == "ret":
                    ret_body(ph, 0, False)
                    with dve.Fori(1, RH - 1) as h:
                        ret_body(ph, h, False)
                    ret_body(ph, RH - 1, True)
                if ph.kind == "gate_up":
                    def body(i, last):
                        for s in range(2):
                            k = ph.slot0 + 2 * i + s
                            cols = ph.next_cols if last and s == 1 else ph.cols
                            split(ph, k + 1, (s + 1) % 2, cols)
                            if isinstance(i, int) and i == 0 and s == 0:
                                dve.wait_ge(ssq_root, ph.norm + 1)
                                nc.vector.reciprocal(rinv[:], rinv[:]).then_inc(ssq_inv, 1)
                                dve.wait_ge(ssq_inv, ph.norm + 1)
                                mixer_stored(ph.index)
                            j = 2 * i + s
                            n = FT * ph.index + j
                            if not isinstance(n, int) or n > 0:
                                dve.wait_ge(h_low, n)
                            for g, t_ in ((0, gate), (1, up)):
                                dve.wait_ge(parts_done, ph.unit_done(ph.unit0 + 2 * j + g))
                                nc.vector.tensor_tensor(halves(t_[:]), pair(g), halves(rinv[:]), ALU.mult).then_inc(acc_free, 1)
                            dve.wait_ge(gate_ready, n + 1)
                            dve.wait_ge(acc_free, ph.unit0 + 2 * j + 2)
                            nc.vector.tensor_tensor(up[:], up[:], gate[:], ALU.mult).then_inc(h_ready, 1)
                            dve.wait_ge(h_high, n + 1)
                            nc.vector.tensor_tensor(hl[:, j, :], up[:], hh[:, j, :].bitcast(F32), ALU.subtract).then_inc(h_low, 1)
                    rolled(dve, ph.slots // 2, body, True)
                if ph.kind == "down":
                    def body(i, last):
                        for q in range(2):
                            for s in range(2):
                                k = ph.slot0 + 4 * i + 2 * q + s
                                cols = ph.next_cols if last and q == 1 and s == 1 else ph.cols
                                if cols:
                                    split(ph, k + 1, (s + 1) % 2, cols)
                            t = 2 * i + q
                            dve.wait_ge(parts_done, ph.unit_done(ph.unit0 + t))
                            xt = halves(x[:, t, :])
                            m_ = nc.vector.scalar_tensor_tensor(xt, pair(q), 0.5, xt, ALU.mult, ALU.add)
                            m_.then_inc(acc_free, 1)
                            scaled_low(ph.norm, t)
                    rolled(dve, ph.units // 2, body)

            dve.wait_ge(ssq_root, 7)
            nc.vector.reciprocal(rinv[:], rinv[:]).then_inc(ssq_inv, 1)
            dve.wait_ge(ssq_inv, 7)
            for t in range(KT):
                nc.vector.scalar_tensor_tensor(yy[:, t, :], x[:, t, :], gains[:, 6 * KT + t:6 * KT + t + 1], rinv[:], ALU.mult, ALU.mult)\
                    .then_inc(y_ready, 1)


_INS = ['x_prompt', 'x_sample', 'state_ret', 'state_gdn', 'state_gdn_conv', 'gdn_w_in', 'gdn_conv_w', 'gdn_a_log',
        'gdn_dt_bias', 'gdn_norm_w', 'gdn_w_out', 'norm_g', 'ffn_gu', 'ffn_down', 'ret_w_in', 'ret_w_out', 'final_g']
_OUTS = [((1, 512, 1024), 'float32'), ((8, 1, 1024), 'float32'), ((1, 1, 4, 256, 512), 'float32'),
         ((1, 1, 8, 128, 128), 'float32'), ((1, 1, 3, 3072), 'float32'), ((1, 8, 4, 256, 512), 'float32'),
         ((1, 8, 8, 128, 128), 'float32'), ((1, 8, 3, 3072), 'float32')]


def tables():
    import numpy as np

    f = np.float32
    t = {"c_ident": np.eye(P, dtype=f)}
    sel = np.zeros((DEC, DEC, P), f)
    for b in range(DEC):
        sel[b, b] = 1
    t["c_sel"] = sel
    steps = (np.arange(RK // 2, dtype=f) * f(1 / (RK // 2 - 1))).astype(np.float64)
    theta = f(1) / (10000.0 ** steps).astype(f)
    pos = np.concatenate([np.arange(SEQ), np.full(DEC, 4096)]).astype(f)
    ang = (theta[:, None] * pos[None, :]).astype(f).astype(np.float64)
    t["c_cos"], t["c_sin"] = np.cos(ang).astype(f), np.sin(ang).astype(f)
    head = np.zeros((RH, P, SEQ + 5))
    j = np.arange(P)[:, None]
    i = np.arange(SEQ)[None, :]
    for h in range(RH):
        g = 1.0 - 2.0 ** (-5 - h)
        head[h, :, 0:SEQ] = np.where(i >= j, g ** np.maximum(i - j, 0), 0)
        for c in range(4):
            head[h, :, SEQ + c] = g ** (SEQ - 1 - (c * P + np.arange(P)))
        head[h, :, SEQ + 4] = g
    t["c_head"] = head.astype(f)
    con = np.zeros((P, 10 * P + DEC), f)
    row, col = np.arange(P)[:, None], np.arange(P)[None, :]
    con[:, 0:P] = row <= col
    con[:, P:2 * P] = np.where(col >= row, 0, -1e30)
    con[:, 2 * P:3 * P] = np.where(col < row, 0, 1e30)
    for n in range(7):
        half = 2 ** n
        con[:, (3 + n) * P:(4 + n) * P] = (row // (2 * half) == col // (2 * half)) & (row // half % 2 == 1) & (col // half % 2 == 0)
    for b in range(DEC):
        con[P - DEC + b, 10 * P + b] = 1
    t["c_gdn"] = con
    return t


def kernel(**inputs):
    import numpy as _np
    import concourse.bacc as _bacc
    from concourse import mybir as _mybir
    from concourse.bass_utils import run_bass_kernel_spmd as _run

    nc = _bacc.Bacc("TRN2", target_bir_lowering=False, num_devices=1)
    arrays, args = {}, {}
    given = {n: _np.ascontiguousarray(inputs[n]) for n in _INS}
    given.update(tables())
    for name, v in given.items():
        arrays[f"in_{name}_dram"] = v
        args[name] = nc.dram_tensor(f"in_{name}_dram", v.shape, _mybir.dt.from_np(v.dtype), kind="ExternalInput").ap()
    outs = []
    for i, (shape, dtype) in enumerate(_OUTS):
        outs.append(nc.dram_tensor(f"out_{i}_dram", shape, _mybir.dt.from_np(_np.dtype(dtype)), kind="ExternalOutput").ap())
    build(nc, args, outs)
    r = _run(nc, [arrays], core_ids=[0])
    return tuple(r.results[0][f"out_{i}_dram"] for i in range(len(_OUTS)))
```
